# Optimizing a Trainium2 kernel written in Bass

```python
import jax, jax.numpy as jnp
from jax import lax
import numpy as np

D_MODEL = 1024
BATCH = 1
SEQ = 256
DEPTH = 2

GRID_W = 64
N_MEM = 256
HEAD_DIM = 64
NORM_EPS = 1e-6
MEM_HEADS = 4
MEM_DIM = MEM_HEADS * HEAD_DIM
MIX_DIM = D_MODEL - MEM_DIM
NA_HEADS = MIX_DIM // HEAD_DIM
NA_WIN_H = 8
NA_WIN_W = 16
NA_QBLK_W = 16
NA_KBLK_W = NA_QBLK_W + NA_WIN_W
NA_IN = 3 * MIX_DIM + MEM_DIM
GLA_HEADS = 4
GLA_DK = MIX_DIM // 2 // GLA_HEADS
GLA_DV = MIX_DIM // GLA_HEADS
GLA_GATE_RANK = 16
GLA_TAU = 16.0
GLA_CHUNK = 64
GLA_IN = 2 * GLA_HEADS * GLA_DK + 2 * MIX_DIM + 2 * GLA_GATE_RANK + MEM_DIM
N_GROUPS = 4
EXPERTS_PER_GROUP = 8
N_EXPERTS = N_GROUPS * EXPERTS_PER_GROUP
TOP_K = 2
EXPERT_FF = 512
MOE_BLOCK = 256
N_NA_LAYERS = (DEPTH + 1) // 2
N_GLA_LAYERS = DEPTH // 2

kernel_name = "hybrid_na_gla_hmoe_encoder"

def rms_norm(x, g):
    xf = x.astype(jnp.float32)
    y = xf * lax.rsqrt(jnp.mean(xf * xf, axis=-1, keepdims=True) + NORM_EPS)
    return (y * g.astype(jnp.float32)).astype(x.dtype)

def neighbourhood_attention(q, k, v, rpb):
    B, T, H, Dh = q.shape
    rows = T // GRID_W
    kh = min(NA_WIN_H, rows)
    ncb = GRID_W // NA_QBLK_W
    n_keys = kh * NA_KBLK_W
    scale = HEAD_DIM ** -0.5
    qcol = np.arange(GRID_W).reshape(ncb, NA_QBLK_W)
    kcol = (np.clip(np.arange(ncb) * NA_QBLK_W - NA_WIN_W // 2, 0, GRID_W - NA_KBLK_W)[:, None]
            + np.arange(NA_KBLK_W))
    cstart = np.clip(qcol - NA_WIN_W // 2, 0, GRID_W - NA_WIN_W)
    col_in = ((kcol[:, None, :] >= cstart[:, :, None])
              & (kcol[:, None, :] < cstart[:, :, None] + NA_WIN_W))
    dcol = np.clip(kcol[:, None, :] - qcol[:, :, None], 1 - NA_WIN_W, NA_WIN_W - 1) + NA_WIN_W - 1
    rstart = np.clip(np.arange(rows) - kh // 2, 0, rows - kh)
    drow = rstart[:, None] + np.arange(kh)[None, :] - np.arange(rows)[:, None] + NA_WIN_H - 1
    bias = rpb.astype(jnp.float32)[:, drow[:, :, None, None, None], dcol[None, None]]
    bias = jnp.where(col_in[None, None, None], bias, -jnp.inf)
    bias = bias.transpose(1, 0, 3, 4, 2, 5).reshape(rows, H, ncb, NA_QBLK_W, n_keys)
    kg = k.reshape(B, rows, GRID_W, H, Dh)
    vg = v.reshape(B, rows, GRID_W, H, Dh)
    qg = q.reshape(B, rows, GRID_W, H, Dh).transpose(1, 0, 2, 3, 4)

    def row_block(args):
        r0, q_row, b_row = args

        def gather(a):
            a = lax.dynamic_slice_in_dim(a, r0, kh, axis=1)[:, :, kcol]
            return a.transpose(0, 2, 1, 3, 4, 5).reshape(B, ncb, n_keys, H, Dh)

        k_blk, v_blk = gather(kg), gather(vg)
        q_blk = q_row.reshape(B, ncb, NA_QBLK_W, H, Dh)
        s = jnp.einsum('bjqhd,bjnhd->bhjqn', q_blk, k_blk,
                       preferred_element_type=jnp.float32) * scale + b_row
        p = jax.nn.softmax(s, axis=-1).astype(v.dtype)
        o = jnp.einsum('bhjqn,bjnhd->bjqhd', p, v_blk)
        return o.reshape(B, GRID_W, H, Dh)

    out = lax.map(row_block, (jnp.asarray(rstart, jnp.int32), qg, bias))
    return out.transpose(1, 0, 2, 3, 4).reshape(B, T, H * Dh)

def gla_chunked(q, k, v, log_a):
    B, T, H, dk = q.shape
    dv = v.shape[-1]
    c = GLA_CHUNK
    n = T // c
    chunk = lambda a: a.reshape(B, n, c, H, a.shape[-1]).transpose(0, 1, 3, 2, 4)
    q, k, v, log_a = chunk(q), chunk(k), chunk(v), chunk(log_a)
    b = jnp.cumsum(log_a, axis=3)
    b_mid = b[:, :, :, c // 2 - 1:c // 2]
    b_last = b[:, :, :, -1:]
    a = jnp.einsum('bnhid,bnhjd->bnhij', q * jnp.exp(b - b_mid), k * jnp.exp(b_mid - b))
    a = jnp.where(jnp.tril(jnp.ones((c, c), dtype=bool)), a, 0.0)
    o_intra = jnp.einsum('bnhij,bnhjv->bnhiv', a, v)
    q_st = jnp.moveaxis(q * jnp.exp(b), 1, 0)
    k_st = jnp.moveaxis(k * jnp.exp(b_last - b), 1, 0)
    v_st = jnp.moveaxis(v, 1, 0)
    dec = jnp.moveaxis(jnp.exp(b_last[:, :, :, 0]), 1, 0)

    def step(S, xs):
        qs, ks, vs, d = xs
        o = jnp.einsum('bhid,bhdv->bhiv', qs, S)
        S = S * d[..., None] + jnp.einsum('bhjd,bhjv->bhdv', ks, vs)
        return S, o

    S0 = jnp.zeros((B, H, dk, dv), jnp.float32)
    _, o_inter = lax.scan(step, S0, (q_st, k_st, v_st, dec))
    o = o_intra + jnp.moveaxis(o_inter, 0, 1)
    return o.transpose(0, 1, 3, 2, 4).reshape(B, T, H, dv)

def gla_mixer(u, gate_up, gate_bias, out_norm):
    B, T, _ = u.shape
    kd = GLA_HEADS * GLA_DK
    q, k, v, g, r_f, r_b, mq = jnp.split(
        u, np.cumsum([kd, kd, MIX_DIM, MIX_DIM, GLA_GATE_RANK, GLA_GATE_RANK]), axis=-1)
    heads = lambda a, d: a.astype(jnp.float32).reshape(B, T, GLA_HEADS, d)
    q = heads(q, GLA_DK) * (GLA_DK ** -0.5)
    k = heads(k, GLA_DK)
    v = heads(v, GLA_DV)

    def log_decay(r, d):
        z = (r @ gate_up[d]).astype(jnp.float32) + gate_bias[d].astype(jnp.float32)
        return heads(jax.nn.log_sigmoid(z) / GLA_TAU, GLA_DK)

    flip = lambda a: a[:, ::-1]
    o_fwd = gla_chunked(q, k, v, log_decay(r_f, 0))
    o_bwd = flip(gla_chunked(flip(q), flip(k), flip(v), flip(log_decay(r_b, 1))))
    o = rms_norm(o_fwd + o_bwd, out_norm).astype(u.dtype).reshape(B, T, MIX_DIM)
    return o * jax.nn.silu(g), mq

def memory_attention(mq, mkv):
    B, T, _ = mq.shape
    q = mq.reshape(B, T, MEM_HEADS, HEAD_DIM)
    k, v = jnp.split(mkv, 2, axis=-1)
    k = k.reshape(B, -1, MEM_HEADS, HEAD_DIM)
    v = v.reshape(B, -1, MEM_HEADS, HEAD_DIM)
    s = jnp.einsum('bthd,bmhd->bhtm', q, k, preferred_element_type=jnp.float32) * (HEAD_DIM ** -0.5)
    p = jax.nn.softmax(s, axis=-1).astype(v.dtype)
    return jnp.einsum('bhtm,bmhd->bthd', p, v).reshape(B, T, MEM_DIM)

def hierarchical_moe(x, w_group, b_group, w_router, b_router, w1, w3, w2):
    B, T, D = x.shape
    xt = x.reshape(-1, D)
    n_tok = xt.shape[0]
    g_prob = jax.nn.softmax((xt @ w_group).astype(jnp.float32) + b_group.astype(jnp.float32), axis=-1)
    g_gate, g_idx = lax.top_k(g_prob, 1)
    e_logits = ((xt @ w_router).astype(jnp.float32) + b_router.astype(jnp.float32)
                ).reshape(n_tok, N_GROUPS, EXPERTS_PER_GROUP)
    e_logits = jnp.take_along_axis(e_logits, g_idx[:, :, None], axis=1)[:, 0]
    top_l, top_i = lax.top_k(e_logits, TOP_K)
    gate = jax.nn.softmax(top_l, axis=-1) * g_gate
    expert = g_idx * EXPERTS_PER_GROUP + top_i
    n_asg = n_tok * TOP_K
    a_exp = expert.reshape(-1)
    a_tok = jnp.repeat(jnp.arange(n_tok, dtype=jnp.int32), TOP_K)
    a_w = gate.reshape(-1)
    order = jnp.argsort(a_exp)
    s_exp = a_exp[order]
    counts = jnp.zeros((N_EXPERTS,), jnp.int32).at[a_exp].add(1)
    padded = (counts + MOE_BLOCK - 1) // MOE_BLOCK * MOE_BLOCK
    start = jnp.cumsum(counts) - counts
    pend = jnp.cumsum(padded)
    pstart = pend - padded
    dest = pstart[s_exp] + jnp.arange(n_asg, dtype=jnp.int32) - start[s_exp]
    n_blocks = -(-n_asg // MOE_BLOCK) + N_EXPERTS
    n_rows = n_blocks * MOE_BLOCK
    row_tok = jnp.full((n_rows,), n_tok, jnp.int32).at[dest].set(a_tok[order])
    row_w = jnp.zeros((n_rows,), x.dtype).at[dest].set(a_w[order].astype(x.dtype))
    block_start = jnp.arange(n_blocks, dtype=jnp.int32) * MOE_BLOCK
    block_exp = jnp.minimum(jnp.sum(block_start[:, None] >= pend[None, :], axis=1), N_EXPERTS - 1)
    x_pad = jnp.concatenate([xt, jnp.zeros((1, D), xt.dtype)], axis=0)
    xb = x_pad[row_tok].reshape(n_blocks, MOE_BLOCK, D)

    def expert_block(args):
        xi, e = args
        return (jax.nn.silu(xi @ w1[e]) * (xi @ w3[e])) @ w2[e]

    yb = lax.map(expert_block, (xb, block_exp)).reshape(n_rows, D)
    y = jnp.zeros((n_tok + 1, D), x.dtype).at[row_tok].add(yb * row_w[:, None])[:n_tok]
    return y.reshape(B, T, D)

def setup_inputs(seed: int = 0) -> dict:
    key = jax.random.key(seed)
    ks = jax.random.split(key, 21)
    nrm = lambda k, shape, s: jax.random.normal(k, shape, jnp.float32) * s
    D = D_MODEL
    return {
        "x": nrm(ks[0], (BATCH, SEQ, D), 1.0),
        "mem": nrm(ks[1], (BATCH, N_MEM, D), 1.0),
        "mem_norm": 1.0 + nrm(ks[2], (D,), 0.02),
        "final_norm": 1.0 + nrm(ks[3], (D,), 0.02),
        "norm_mix": 1.0 + nrm(ks[4], (DEPTH, D), 0.02),
        "norm_ffn": 1.0 + nrm(ks[5], (DEPTH, D), 0.02),
        "w_mem_kv": nrm(ks[6], (DEPTH, D, 2 * MEM_DIM), D ** -0.5),
        "w_out": nrm(ks[7], (DEPTH, D, D), D ** -0.5),
        "na_w_in": nrm(ks[8], (N_NA_LAYERS, D, NA_IN), D ** -0.5),
        "na_rpb": nrm(ks[9], (N_NA_LAYERS, NA_HEADS, 2 * NA_WIN_H - 1, 2 * NA_WIN_W - 1), 0.1),
        "gla_w_in": nrm(ks[10], (N_GLA_LAYERS, D, GLA_IN), D ** -0.5),
        "gla_gate_up": nrm(ks[11], (N_GLA_LAYERS, 2, GLA_GATE_RANK, GLA_HEADS * GLA_DK), GLA_GATE_RANK ** -0.5),
        "gla_gate_bias": nrm(ks[12], (N_GLA_LAYERS, 2, GLA_HEADS * GLA_DK), 0.1),
        "gla_out_norm": 1.0 + nrm(ks[13], (N_GLA_LAYERS, GLA_DV), 0.02),
        "moe_w_group": nrm(ks[14], (DEPTH, D, N_GROUPS), D ** -0.5),
        "moe_b_group": nrm(ks[15], (DEPTH, N_GROUPS), 0.01),
        "moe_w_router": nrm(ks[16], (DEPTH, D, N_EXPERTS), D ** -0.5),
        "moe_b_router": nrm(ks[17], (DEPTH, N_EXPERTS), 0.01),
        "moe_w1": nrm(ks[18], (DEPTH, N_EXPERTS, D, EXPERT_FF), D ** -0.5),
        "moe_w3": nrm(ks[19], (DEPTH, N_EXPERTS, D, EXPERT_FF), D ** -0.5),
        "moe_w2": nrm(ks[20], (DEPTH, N_EXPERTS, EXPERT_FF, D), EXPERT_FF ** -0.5),
    }

def reference(x, mem, mem_norm, final_norm, norm_mix, norm_ffn, w_mem_kv, w_out,
              na_w_in, na_rpb, gla_w_in, gla_gate_up, gla_gate_bias, gla_out_norm,
              moe_w_group, moe_b_group, moe_w_router, moe_b_router, moe_w1, moe_w3, moe_w2):
    B, T, _ = x.shape
    mem_n = rms_norm(mem, mem_norm)
    for i in range(DEPTH):
        h = rms_norm(x, norm_mix[i])
        mkv = mem_n @ w_mem_kv[i]
        j = i // 2
        if i % 2 == 0:
            u = h @ na_w_in[j]
            q, k, v, mq = jnp.split(u, [MIX_DIM, 2 * MIX_DIM, 3 * MIX_DIM], axis=-1)
            hd = lambda a: a.reshape(B, T, NA_HEADS, HEAD_DIM)
            mix = neighbourhood_attention(hd(q), hd(k), hd(v), na_rpb[j])
        else:
            mix, mq = gla_mixer(h @ gla_w_in[j], gla_gate_up[j], gla_gate_bias[j], gla_out_norm[j])
        att = memory_attention(mq, mkv)
        x = x + jnp.concatenate([mix, att], axis=-1) @ w_out[i]
        x = x + hierarchical_moe(rms_norm(x, norm_ffn[i]), moe_w_group[i], moe_b_group[i],
                                 moe_w_router[i], moe_b_router[i], moe_w1[i], moe_w3[i], moe_w2[i])
    return rms_norm(x, final_norm)


_drawn_inputs = setup_inputs


def setup_inputs(seed=0):
    import zlib

    import numpy as np

    out = dict(_drawn_inputs(seed))
    spreads = {}
    factors = {'mem_norm': 8.0,
     'final_norm': 27.043,
     'moe_b_group': 29.672,
     'na_rpb': 4.206,
     'gla_gate_up': 4.6,
     'gla_gate_bias': 8.0,
     'gla_out_norm': 31.44,
     'moe_b_router': 8.0,
     'norm_ffn': 2.672}
    for name, (base, spread) in spreads.items():
        noise = np.random.default_rng([zlib.crc32(name.encode()), seed]).standard_normal(out[name].shape)
        drawn = base * np.exp(spread * noise) if base else spread * noise
        out[name] = __import__('jax').numpy.asarray(drawn.astype(out[name].dtype))
    for name, factor in factors.items():
        out[name] = (out[name] * factor).astype(out[name].dtype)
    return out
```

```python
from contextlib import ExitStack

import concourse.bass as bass
from concourse import mybir

F32 = mybir.dt.float32
I32 = mybir.dt.int32
ALU = mybir.AluOpType
ACT = mybir.ActivationFunctionType
AX_X = mybir.AxisListType.X

P = 128
D = 1024
T = 256
TT = T // P
KC = D // P
EPS = 1e-6
GRID = 64
DH = 64
MIX = 768
NPAIR = 6
MPAIR = 2
RPB_H, RPB_W = 15, 31
NA_DR = 6
HG, DK, DV, CH = 4, 96, 192, 64
NCH = T // CH
NG, EG = 4, 8
NE = NG * EG
FF = 512
E4 = 4
CAP = 32
NQ = NE // E4
SELS = 2 * NQ + 2
FILLS = 12
SLOTS = 6
SLOT = 4096
BIG = 1e30

C_ID, C_ONE, C_TRI, C_IOTA, C_IOTAM, C_THR, C_NAM, C_MF, C_MB = 0, 128, 256, 384, 416, 448, 456, 520, 584
C_FLIP = 648
C_END = 776
RPC = 2 * NPAIR * NA_DR * GRID // 512
N1 = NPAIR + MPAIR
SMALL = 16 * 18


def make_consts():
    import numpy as np

    c = np.zeros((P, C_END), np.float32)
    c[:, C_ID:C_ID + P] = np.eye(P)
    c[:, C_ONE:C_ONE + P] = 1.0
    c[:, C_TRI:C_TRI + P] = np.triu(np.ones((P, P)), 1)
    c[:, C_IOTA:C_IOTA + 32] = np.arange(32)
    c[:, C_IOTAM:C_IOTAM + 32] = np.arange(32) - 64
    c[:, C_THR:C_THR + 8] = CAP * (np.arange(8) + 1)
    col = np.arange(P) % GRID
    start = np.clip(col - 8, 0, GRID - 16)
    key = np.arange(GRID)
    inside = (key[None] >= start[:, None]) & (key[None] < start[:, None] + 16)
    c[:, C_NAM:C_NAM + GRID] = np.where(inside, 0.0, -BIG)
    j = np.arange(P) % CH
    i = np.arange(CH)
    c[:, C_MF:C_MF + CH] = i[None] >= j[:, None]
    c[:, C_MB:C_MB + CH] = i[None] <= j[:, None]
    c[:, C_FLIP:C_FLIP + P] = np.kron(np.eye(2), np.eye(GRID)[::-1])
    return c


def build(nc, x, mem, mem_norm, final_norm, norm_mix, norm_ffn, w_mem_kv, w_out, na_w_in, na_rpb, gla_w_in,
          gla_gate_up, gla_gate_bias, gla_out_norm, moe_w_group, moe_b_group, moe_w_router, moe_b_router,
          moe_w1, moe_w3, moe_w2, consts, out):
    with ExitStack() as ctx:
        def sb(name, shape, dt=F32):
            return ctx.enter_context(nc.sbuf_tensor(name, shape, dt))

        def sem(name):
            return ctx.enter_context(nc.semaphore(name))

        ring = sb("ring", [P, SLOTS * SLOT])
        cst = sb("cst", [P, C_END])
        gcol = sb("gcol", [P, 5, KC])
        wgrp = sb("wgrp", [P, 2, KC, NG])
        wrtr = sb("wrtr", [P, 2, KC, NE])
        rbias = sb("rbias", [P, 2, NG + NE])
        gnorm = sb("gnorm", [P, DV])
        gup = sb("gup", [32, 2, HG * DK])
        gbias = sb("gbias", [DK, 2, HG])
        xres = sb("xres", [P, TT, D])
        xs = sb("xs", [P, TT, D])
        hT = sb("hT", [P, KC, T])
        mixT = sb("mixT", [P, KC, T])
        kTm = sb("kTm", [P, 2, MPAIR, T])
        vm = sb("vm", [P, 2, TT, MPAIR * P])
        st = sb("st", [P, 96])
        st_dec = sb("st_dec", [DK, 2, HG * NCH])
        nround = sb("nround", [P, 2], I32)
        roundf = sb("roundf", [P, 1])
        ARENA = 15360
        arena = sb("arena", [P, ARENA])

        def cut(off, *dims, parts=P):
            n = 1
            for v in dims:
                n *= v
            assert off + n <= ARENA
            v = arena[0:parts, off:off + n]
            if len(dims) == 1:
                return v
            names = "abcde"[:len(dims)]
            return v.rearrange(f"p ({' '.join(names)}) -> p {' '.join(names)}",
                               **{names[i]: dims[i] for i in range(1, len(dims))})

        ps = ctx.enter_context(nc.psum_tensor("ps", [P, 8, 512], F32))

        ident = cst[:, C_ID:C_ID + P]
        ones = cst[:, C_ONE:C_ONE + P]
        tri = cst[:, C_TRI:C_TRI + P]
        iota = cst[:, C_IOTA:C_IOTA + 32]
        iotam = cst[:, C_IOTAM:C_IOTAM + 32]

        rpbt = cut(0, 2 * NPAIR, NA_DR, GRID)
        v0 = cut(4608, TT, MIX)
        qk = cut(6144, 2, 2, T)
        mqT0 = cut(7168, MPAIR, T)
        prob0 = cut(7680, 2, TT, T)
        pT0 = cut(8704, 2, TT, T)
        rpbraw = cut(8704, 2 * NPAIR, NA_DR, GRID)
        memT = cut(ARENA - 2048, KC, T)
        v1 = cut(0, TT, MIX)
        g1 = cut(1536, TT, MIX)
        qT = cut(3072, HG, T, parts=DK)
        kT = cut(4096, HG, T, parts=DK)
        bcum = cut(5120, 2, HG * T, parts=DK)
        qi = cut(7168, 2, HG * T, parts=DK)
        ki = cut(9216, 2, HG * T, parts=DK)
        qs = cut(11264, 2, HG * T, parts=DK)
        ks = cut(13312, 2, HG * T, parts=DK)
        mqT1 = mixT[:, 6:8, :]
        prob1 = hT[:, 0:4, :].rearrange("p (h a) k -> p h a k", h=2)
        pT1 = hT[:, 4:8, :].rearrange("p (h a) k -> p h a k", h=2)
        ksT = xs[:, :, :].rearrange("p a d -> p (a d)")[:, 0:2 * TT * HG * DK].rearrange(
            "p (d a h c) -> p d a h c", d=2, a=TT, h=HG)
        rT = xs[0:32, :, :].rearrange("p a d -> p (a d)")[:, 1792:2048]
        amask = cut(3072, 2, HG, TT, CH)
        asum = cut(4096, HG, TT, CH)
        state = cut(5120, 2, 3, HG, DV, parts=DK)
        sig1 = mixT[:, 0:6, :].rearrange("p c t -> p (c t)").rearrange("p (a n) -> p a n", a=TT)
        ppos = cut(0, TT, NE + E4)
        wtok = cut(80, TT, NE + E4)
        sel = cut(160, TT, E4, CAP)
        selw = cut(416, TT, E4, CAP)
        selwT = cut(672, TT, P)
        xsel = cut(928, KC, P)
        sg = cut(1952, FF)
        act = cut(2464, FF)
        actT = cut(2976, FF // P, P)
        yb = cut(3488, D)
        lg = cut(4512, TT, NG + NE)
        t4a = cut(4600, TT, NG)
        goh = cut(4608, TT, NG)
        gpen = cut(4616, TT, NG)
        me = cut(4624, TT, NE)
        oh1 = cut(4688, TT, NE)
        oh2 = cut(4752, TT, NE)
        t32a = cut(4816, TT, NE)
        t32b = cut(4880, TT, NE)
        msk = cut(4944, TT, NE)
        sc = cut(5008, 16, TT)
        cmp8 = cut(5040, 8)
        ntmp = cut(5048, 2)
        fnorm = cut(6144, D)
        fin = cut(7168, TT, D)

        mixT_as_tokens = mixT[:, :, :].rearrange("p c t -> p (c t)").rearrange("p (a d) -> p a d", a=TT)
        sqj = hT[:, :, :].rearrange("p c t -> p (c t)")

        def norm_src(i):
            return mixT_as_tokens if i == 0 else xres

        s_x, s_mem, s_cst, s_rpb, s_small = sem("x_in"), sem("mem_in"), sem("const_in"), sem("rpb_in"), sem("small_in")
        s_gup0 = sem("gup_zeroed")
        s_fn = sem("final_norm_in")
        s_out = sem("out_written")
        ring_in = [sem(f"ring_in{i}") for i in range(SLOTS)]
        ring_used = sem("ring_used")
        dchain = sem("dve_chain")
        sp_spare = sem("sp_spare")
        fin_ready = sem("final_ready")
        next_round = sem("next_round")
        n_sq = sem("squares")
        n_var = sem("variance")
        n_sd = sem("deviation")
        n_xs = sem("scaled")
        n_tr = sem("transposed")
        n_hT = sem("normed")
        kv_mm = [sem(f"memkv_mm{i}") for i in range(2)]
        kv_cp = [sem(f"memkv_cp{i}") for i in range(2)]
        v_mm = [sem(f"v_mm{i}") for i in range(2)]
        v_cp = [sem(f"v_cp{i}") for i in range(2)]
        mq_cp = [sem(f"mq_cp{i}") for i in range(2)]
        qk_mm, qk_cp = sem("qk_mm"), sem("qk_cp")
        at_sc = sem("scores")
        at_mx = sem("negmax")
        at_ex = sem("exps")
        at_p = sem("probs")
        at_tr = sem("probsT_mm")
        at_pT = sem("probsT")
        at_o = sem("pv_mm")
        at_oT = sem("mixT")
        s_mask, rp_mm = sem("rpb_masked"), sem("rpb_turned")
        res = [sem(f"mixed{i}") for i in range(2)]
        r_mm, r_cp, z_mm, z_sb = sem("rank_mm"), sem("rank_cp"), sem("z_mm"), sem("z_biased")
        gq_mm, gq_cp = sem("gla_qk_mm"), sem("gla_qk_cp")
        g_cp, g_ex, g_silu = sem("g_cp"), sem("g_exp"), sem("g_silu")
        l_na, l_ex, l_ln = sem("neg_abs"), sem("ls_exp"), sem("ls_ln")
        d_b, d_mid, d_last = sem("b_cum"), sem("b_minus_mid"), sem("last_minus_b")
        e_done = sem("decay_exps")
        q_in, k_in, q_st, k_st = sem("q_intra"), sem("k_intra"), sem("q_state"), sem("k_state")
        kst_mm, kst_cp = sem("k_stateT_mm"), sem("k_stateT")
        a_mm, a_cp = sem("a_mm"), sem("a_masked")
        u_mm, u_st = sem("u_mm"), sem("state_ready")
        o_mm, o_sq, o_var, o_sd, o_mix = sem("o_mm"), sem("o_squares"), sem("o_variance"), sem("o_dev"), sem("o_mix")
        m_tr, m_cp = sem("mix_tr"), sem("mix_cp")
        resets = sem("scan_resets")
        rt_mm = [sem(f"logits{i}") for i in range(2)]
        rt_d = [sem(f"exp_in{i}") for i in range(2)]
        rt_e = [sem(f"exp_out{i}") for i in range(2)]
        rt_m = [sem(f"routed{i}") for i in range(2)]
        rt_p = [sem(f"positions{i}") for i in range(2)]
        rt_n = [sem(f"rounds{i}") for i in range(2)]
        moe_done = [sem(f"moe_done{i}") for i in range(2)]

        class Quads:

            def __init__(self, tag):
                self.sel_ready = sem(f"sel_ready_{tag}")
                self.selT_mm = sem(f"selT_mm_{tag}")
                self.gathered = sem(f"gathered_{tag}")
                self.xsel_ready = sem(f"xsel_ready_{tag}")
                self.selwT_ready = sem(f"selwT_ready_{tag}")
                self.exp_done = sem(f"exp_done_{tag}")
                self.silu = sem(f"silu_{tag}")
                self.act_ready = sem(f"act_ready_{tag}")
                self.actT_mm = sem(f"actT_mm_{tag}")
                self.actT_ready = sem(f"actT_ready_{tag}")
                self.yb_ready = sem(f"yb_ready_{tag}")
                self.scattered = sem(f"scattered_{tag}")
                self.added = sem(f"added_{tag}")

        PRE0 = 9
        PRE1 = PRE0 + NQ * FILLS + 8
        fills_of = [[0] * SLOTS for _ in range(2)]

        def rows(w, c0, c1):
            return w.rearrange("(p k) n -> p k n", k=KC)[:, :, c0:c1]

        def region(slot, off, n, k):
            a = ring[:, slot * SLOT + off:slot * SLOT + off + n * k]
            return a.rearrange("p (k n) -> p k n", k=k)

        win0, win1 = na_w_in[0], gla_w_in[0]
        kvw = [region(0, 0, 512, KC), region(2, 0, 512, KC)]
        vw0 = region(1, 0, MIX, KC)
        mqw0 = region(1, MIX * KC, 256, KC)
        qkw = [[region(3 + p // 2, (p % 2) * 2048 + t * 1024, P, KC) for t in range(2)] for p in range(NPAIR)]
        wow = [[region(s, 0, D, 4) for s in (0, 1)], [region(s, 0, D, 4) for s in (3, 4)]]
        rw1 = region(3, 0, 288, KC)
        qkw1 = region(4, 0, MIX, KC)
        vgw1 = region(0, 0, 2 * MIX, KC)
        wo_src = [[w_out[l][512 * i:512 * i + 512, :].rearrange("(c p) n -> p c n", p=P) for i in range(2)]
                  for l in range(2)]

        stream0 = [(0, 0, kvw[0], rows(w_mem_kv[0], 0, 512)),
                   (1, 0, vw0, rows(win0, 2 * MIX, 3 * MIX)),
                   (2, 0, mqw0, rows(win0, 3 * MIX, 3 * MIX + 256))]
        for p in range(NPAIR):
            for t in range(2):
                stream0.append((3 + p // 2, 0, qkw[p][t], rows(win0, t * MIX + p * P, t * MIX + p * P + P)))
        stream0 += [(0, 1, wow[0][0], wo_src[0][0]), (1, 3, wow[0][1], wo_src[0][1]),
                    (2, 3, kvw[1], rows(w_mem_kv[1], 0, 512))]
        B1 = PRE0 + NQ * FILLS
        stream1 = [(3, B1 - 5, rw1, rows(win1, 3 * MIX, 3 * MIX + 288)),
                   (5, B1 - 3, qkw1, rows(win1, 0, MIX)),
                   (2, B1, vgw1, rows(win1, MIX, 3 * MIX)),
                   (3, B1 + 1, wow[1][0], wo_src[1][0]),
                   (4, B1 + 3, wow[1][1], wo_src[1][1])]

        count = [0] * SLOTS
        arrive0, arrive1 = [], []
        for slot, _, _, _ in stream0:
            count[slot] += 16
            arrive0.append((ring_in[slot], count[slot]))
        base0 = list(count)
        for s in range(SLOTS):
            count[s] += 16 * NQ * (FILLS // SLOTS)
        for slot, _, _, _ in stream1:
            count[slot] += 16
            arrive1.append((ring_in[slot], count[slot]))
        base1 = list(count)
        first, more = Quads("first"), Quads("more")

        class Run:

            def __init__(self, sig, slot0, ring_in, ring_used, in_base, used_base):
                self.sig, self.slot0, self.ring_in, self.ring_used = sig, slot0, ring_in, ring_used
                self.in_base, self.used_base = in_base, used_base

        main = [Run(first, PRE0 % SLOTS, ring_in, ring_used, base0, PRE0),
                Run(first, PRE1 % SLOTS, ring_in, ring_used, base1, PRE1)]
        more_in, more_used = [sem(f"more_in{i}") for i in range(SLOTS)], sem("more_used")
        extra = Run(more, 0, more_in, more_used, [0] * SLOTS, SLOTS)

        w1v = [moe_w1[l].rearrange("e (p k) f -> p e (k f)", k=KC) for l in range(2)]
        w3v = [moe_w3[l].rearrange("e (p k) f -> p e (k f)", k=KC) for l in range(2)]
        w2v = [moe_w2[l].rearrange("e (j p) n -> j p e n", p=P) for l in range(2)]

        def rounds(eng, l):
            hi = eng.value_load(nround[0:1, l:l + 1], min_val=0, max_val=(l + 1) * (T // CAP - 1))
            return (eng.value_load(nround[0:1, 0:1], min_val=0, max_val=T // CAP - 1) if l else 0), hi

        block = ctx.enter_context(nc.Block())

        @block.sync
        def _(sp):
            sp.dma_start(xres[:], x[0].rearrange("(a p) d -> p a d", p=P)).then_inc(s_x, 16)

            def fill(stream):
                for slot, need, dst, src in stream:
                    if need:
                        sp.wait_ge(ring_used, need)
                    sp.dma_start(dst, src).then_inc(ring_in[slot], 16)

            def quad_fills(rn, l, q, g):
                for f in range(FILLS):
                    slot = (rn.slot0 + f) % SLOTS
                    sp.wait_ge(rn.ring_used, q * FILLS + (rn.used_base + f - SLOTS + 1))
                    dst = ring[:, slot * SLOT:(slot + 1) * SLOT].rearrange("p (e n) -> p e n", e=E4)
                    w = (w1v, w3v)[f // 4][l] if f < 8 else None
                    if f < 8:
                        src = w[:, bass.ds(g * E4, E4), (f % 4) * 1024:(f % 4) * 1024 + 1024]
                    else:
                        src = w2v[l][f - 8][:, bass.ds(g * E4, E4), :]
                    sp.dma_start(dst, src).then_inc(rn.ring_in[slot], 16)

            def experts(l):
                with sp.Fori(0, NQ) as g:
                    quad_fills(main[l], l, g, g)
                sp.wait_ge(rt_n[l], 1)
                lo, hi = rounds(sp, l)
                with sp.If(hi > lo):
                    sp.wait_ge(ring_used, main[l].used_base + NQ * FILLS)
                    with sp.Fori(lo, hi) as r:
                        with sp.Fori(0, NQ) as g:
                            quad_fills(extra, l, r * NQ + g, g)
                    sp.wait_ge(moe_done[l], 1)
                    sp.sem_inc(sp_spare, 1)

            sp.sem_inc(more_used, SLOTS)
            fill(stream0)
            experts(0)
            fill(stream1)
            experts(1)
            sp.wait_ge(s_out, 32)

        
        @block.gpsimd
        def _(pool):
            nc.gpsimd.memset(gup[:], 0.0).then_inc(s_gup0, 1)
            for r in range(2):
                for i in range(NA_DR):
                    src = bass.AP(tensor=na_rpb.tensor, offset=na_rpb.offset + (i + 5 - r) * RPB_W + 15 - (GRID - 1),
                                  ap=[[1, GRID], [RPB_H * RPB_W, 2 * NPAIR], [1, GRID]])
                    pool.dma_start(rpbraw[64 * r:64 * r + 64, :, i, :], src).then_inc(s_rpb, 16)
            pool.wait_ge(moe_done[0], 1)
            kc = ks.rearrange("p d (n c) -> p d n c", c=CH)
            nc.gpsimd.memset(ks, 1.0).then_inc(resets, 1)
            pool.wait_ge(resets, 1)
            nc.gpsimd.memset(kc[:, 0, :, 0:1], 0.0).then_inc(resets, 1)
            nc.gpsimd.memset(kc[:, 1, :, CH - 1:CH], 0.0).then_inc(resets, 1)

        @block.tensor
        def _(pe):
            def arrived(a):
                pe.wait_ge(*a)

            def transposes(i, src):
                for a in range(TT):
                    pe.wait_ge(n_xs, TT * i + a + 1)
                    for k in range(KC):
                        t = pe.transpose(ps[:, 2 * a + k // 4, (k % 4) * P:(k % 4) * P + P], src[:, a, k::KC], ident)
                    t.then_inc(n_tr, 1)

            def mem_kv(l):
                w = kvw[l]
                arrived(arrive0[(0, 17)[l]])
                for m in range(MPAIR):
                    for k in range(KC):
                        t = pe.matmul(ps[:, 6, m * T:(m + 1) * T], w[:, k, m * P:(m + 1) * P], memT[:, k, :],
                                      start=k == 0, stop=k == KC - 1)
                t.then_inc(kv_mm[l], 1)
                for a in range(TT):
                    for k in range(KC):
                        t = pe.matmul(ps[:, 7, a * 256:a * 256 + 256], memT[:, k, a * P:(a + 1) * P], w[:, k, 256:512],
                                      start=k == 0, stop=k == KC - 1)
                t.then_inc(ring_used, 1)

            def token_rows(w, banks, n0, k_last=None):
                for a in range(TT):
                    for half in range(2):
                        for k in range(KC):
                            t = pe.matmul(ps[:, banks + 2 * a + half, 0:384], hT[:, k, a * P:(a + 1) * P],
                                          w[:, k, n0 + 384 * half:n0 + 384 * half + 384],
                                          start=k == 0, stop=k == KC - 1)
                return t

            def scores(l, p, q_of, k_of):
                for a in range(TT):
                    for h in range(2):
                        r = slice(64 * h, 64 * h + 64)
                        t = pe.matmul(ps[:, 2 + h, a * T:(a + 1) * T], q_of[r, a * P:(a + 1) * P], k_of[r, :],
                                      start=True, stop=True)
                t.then_inc(at_sc, 1)

            def weighted(l, p, prob, pT, v_of, n):
                pe.wait_ge(at_p, n + 1)
                for h in range(2):
                    for a in range(TT):
                        for kt in range(TT):
                            t = pe.transpose(ps[:, 4 + h, kt * T + a * P:kt * T + a * P + P],
                                             prob[:, h, a, kt * P:(kt + 1) * P], ident)
                t.then_inc(at_tr, 1)
                pe.wait_ge(at_pT, n + 1)
                for h in range(2):
                    for kt in range(TT):
                        t = pe.matmul(ps[64 * h:64 * h + 64, 6, 0:T], v_of(h, kt), pT[:, h, kt, :],
                                      start=kt == 0, stop=kt == TT - 1)
                t.then_inc(at_o, 1)

            def out_proj(l, i0):
                for c in range(KC):
                    if c % 4 == 0:
                        arrived((arrive0, arrive1)[l][i0 + c // 4])
                    for a in range(TT):
                        for half in range(2):
                            t = pe.matmul(ps[:, 2 + 2 * a + half, :], mixT[:, c, a * P:(a + 1) * P],
                                          wow[l][c // 4][:, c % 4, 512 * half:512 * half + 512],
                                          start=c == 0, stop=c == KC - 1)
                    if c % 4 == 3:
                        t.then_inc(ring_used, 1)

            def route(l):
                pe.wait_ge(n_hT, TT * (2 * l + 3))
                for a in range(TT):
                    for w, c0, c1 in ((wgrp, 0, NG), (wrtr, NG, NG + NE)):
                        for k in range(KC):
                            t = pe.matmul(ps[:, 4, a * 64 + c0:a * 64 + c1], hT[:, k, a * P:(a + 1) * P], w[:, l, k, :],
                                          start=k == 0, stop=k == KC - 1)
                t.then_inc(rt_mm[l], 1)
                pe.wait_ge(rt_m[l], 1)
                pe.matmul(ps[:, 5, 0:NE], tri, msk[:, 0, :], start=True, stop=True)
                pe.matmul(ps[:, 5, NE:2 * NE], ones, msk[:, 0, :], start=True, stop=False)
                pe.matmul(ps[:, 5, NE:2 * NE], tri, msk[:, 1, :], start=False, stop=True)
                pe.matmul(ps[:, 5, 2 * NE:3 * NE], ones, msk[:, 0, :], start=True, stop=False)
                pe.matmul(ps[:, 5, 2 * NE:3 * NE], ones, msk[:, 1, :], start=False, stop=True).then_inc(rt_p[l], 1)

            def quad(rn, c, q, sel_count):
                pe.wait_ge(rn.sig.sel_ready, sel_count)
                for a in range(TT):
                    t = pe.transpose(ps[:, 2, a * P:(a + 1) * P], selw[:, a].rearrange("p e s -> p (e s)"), ident)
                t.then_inc(rn.sig.selT_mm, 1)
                for k in range(KC):
                    for a in range(TT):
                        t = pe.matmul(ps[:, k // 4, (k % 4) * P:(k % 4) * P + P], xs[:, a, k::KC],
                                      sel[:, a].rearrange("p e s -> p (e s)"), start=a == 0, stop=a == TT - 1)
                t.then_inc(rn.sig.gathered, 1)
                pe.wait_ge(rn.sig.xsel_ready, c * 2 + 2)
                for f in range(8):
                    slot = (rn.slot0 + f) % SLOTS
                    pe.wait_ge(rn.ring_in[slot], (q * 2 + (f // SLOTS + 1)) * 16 + rn.in_base[slot])
                    for kk in range(2):
                        k = 2 * (f % 4) + kk
                        for e in range(E4):
                            o = slot * SLOT + e * 1024 + kk * FF
                            t = pe.matmul(ps[32 * e:32 * e + 32, 4 + f // 4, :], xsel[:, k, 32 * e:32 * e + 32],
                                          ring[:, o:o + FF], start=k == 0, stop=k == KC - 1, tile_position=(0, 32 * e))
                    t.then_inc(rn.ring_used, 1)
                pe.wait_ge(rn.sig.act_ready, c + 1)
                for j in range(4):
                    t = pe.transpose(ps[:, 3, j * P:(j + 1) * P], act[:, j * P:(j + 1) * P], ident)
                t.then_inc(rn.sig.actT_mm, 1)
                pe.wait_ge(rn.sig.actT_ready, c + 1)
                for j in range(4):
                    f = 8 + j
                    slot = (rn.slot0 + f) % SLOTS
                    pe.wait_ge(rn.ring_in[slot], (q * 2 + (f // SLOTS + 1)) * 16 + rn.in_base[slot])
                    for half in range(2):
                        for e in range(E4):
                            o = slot * SLOT + e * D + half * 512
                            t = pe.matmul(ps[32 * e:32 * e + 32, 6 + half, :], actT[:, j, 32 * e:32 * e + 32],
                                          ring[:, o:o + 512], start=j == 0, stop=j == 3, tile_position=(0, 32 * e))
                    t.then_inc(rn.ring_used, 1)
                pe.wait_ge(rn.sig.selwT_ready, c + 1)
                pe.wait_ge(rn.sig.yb_ready, c * 2 + 2)
                for a in range(TT):
                    for half in range(2):
                        t = pe.matmul(ps[:, 4 + 2 * a + half, :], selwT[:, a, :], yb[:, half * 512:half * 512 + 512],
                                      start=True, stop=True)
                t.then_inc(rn.sig.scattered, 1)

            def experts(l):
                with pe.Fori(0, NQ) as q:
                    quad(main[l], q + l * NQ, q, q * 2 + (l * SELS + 2))
                lo, hi = rounds(pe, l)
                with pe.If(hi > lo):
                    with pe.Fori(lo, hi) as r:
                        with pe.Fori(0, NQ) as g:
                            quad(extra, r * NQ + g, r * NQ + g, r * SELS + g * 2 + 2)

            pe.wait_ge(s_cst, 16)
            transposes(0, mixT_as_tokens)
            pe.wait_ge(n_hT, TT * 1)
            mem_kv(0)
            transposes(1, xs)
            pe.wait_ge(s_rpb, 16 * 2 * NA_DR)
            for c in range(RPC):
                if c >= 2:
                    pe.wait_ge(s_mask, c - 1)
                pe.matmul(ps[:, 4 + c % 2, :], cst[:, C_FLIP:C_FLIP + P],
                          rpbraw.rearrange("p h i c -> p (h i c)")[:, c * 512:(c + 1) * 512],
                          start=True, stop=True).then_inc(rp_mm, 1)
            pe.wait_ge(s_mask, RPC)
            pe.wait_ge(n_hT, TT * 2)
            arrived(arrive0[1])
            pe.wait_ge(kv_cp[0], 2)
            token_rows(vw0, 4, 0).then_inc(v_mm[0], 1)
            arrived(arrive0[2])
            for m in range(MPAIR):
                for k in range(KC):
                    t = pe.matmul(ps[:, 0, m * T:(m + 1) * T], mqw0[:, k, m * P:(m + 1) * P], hT[:, k, :],
                                  start=k == 0, stop=k == KC - 1)
            t.then_inc(ring_used, 2)
            pe.wait_ge(v_cp[0], TT)
            pe.wait_ge(mq_cp[0], 1)

            def v_na(p):
                return lambda h, kt: v0[:, kt, p * P + 64 * h:p * P + 64 * h + 64]

            def v_mem(l, m):
                return lambda h, kt: vm[:, l, kt, m * P + 64 * h:m * P + 64 * h + 64]

            for p in range(NPAIR):
                if p % 2 == 0:
                    arrived(arrive0[3 + 2 * p + 3])
                if p >= 2:
                    pe.wait_ge(qk_cp, p - 1)
                for t_ in range(2):
                    for k in range(KC):
                        t = pe.matmul(ps[:, p % 2, t_ * T:(t_ + 1) * T], qkw[p][t_][:, k, :], hT[:, k, :],
                                      start=k == 0, stop=k == KC - 1)
                t.then_inc(qk_mm if p % 2 == 0 else ring_used, 1)
                if p >= 1:
                    if p >= 2:
                        pe.wait_ge(at_oT, p - 1)
                    weighted(0, p - 1, prob0, pT0, v_na(p - 1), p - 1)
                pe.wait_ge(qk_cp, p + 1)
                scores(0, p, qk[:, p % 2, 0, :], qk[:, p % 2, 1, :])
            for n in range(NPAIR, NPAIR + MPAIR):
                pe.wait_ge(at_oT, n - 1)
                weighted(0, n - 1, prob0, pT0, v_na(n - 1) if n == NPAIR else v_mem(0, 0), n - 1)
                m = n - NPAIR
                scores(0, n, mqT0[:, m, :], kTm[:, 0, m, :])
            pe.wait_ge(at_oT, NPAIR + MPAIR - 1)
            weighted(0, NPAIR + 1, prob0, pT0, v_mem(0, 1), NPAIR + 1)
            pe.wait_ge(at_oT, NPAIR + MPAIR)
            out_proj(0, 15)
            mem_kv(1)
            transposes(2, xs)
            route(0)
            pe.wait_ge(rt_n[0], 1)
            experts(0)

            transposes(3, xs)
            pe.wait_ge(n_hT, TT * 4)
            arrived(arrive1[0])
            for k in range(KC):
                t = pe.matmul(ps[0:32, 4, 0:T], rw1[:, k, 0:32], hT[:, k, :], start=k == 0, stop=k == KC - 1)
            t.then_inc(r_mm, 1)
            for m in range(MPAIR):
                for k in range(KC):
                    t = pe.matmul(ps[:, 5, m * T:(m + 1) * T], rw1[:, k, 32 + m * P:32 + (m + 1) * P], hT[:, k, :],
                                  start=k == 0, stop=k == KC - 1)
            t.then_inc(ring_used, 1)
            pe.wait_ge(r_cp, 1)
            pe.wait_ge(s_small, SMALL)
            for d in range(2):
                for h in range(HG):
                    t = pe.matmul(ps[0:DK, 2 * d + h // 2, (h % 2) * T:(h % 2) * T + T],
                                  gup[:, d, h * DK:(h + 1) * DK], rT, start=True, stop=True)
            t.then_inc(z_mm, 1)
            arrived(arrive1[1])
            pe.wait_ge(mq_cp[1], 1)
            for h in range(HG):
                for t_ in range(2):
                    for k in range(KC):
                        t = pe.matmul(ps[0:DK, 4 + h, t_ * T:(t_ + 1) * T],
                                      qkw1[:, k, t_ * 384 + h * DK:t_ * 384 + (h + 1) * DK], hT[:, k, :],
                                      start=k == 0, stop=k == KC - 1)
                if h < HG - 1:
                    t.then_inc(gq_mm, 1)
            t.then_inc(ring_used, 2)
            pe.wait_ge(z_sb, 2)
            arrived(arrive1[2])
            token_rows(vgw1, 0, 0).then_inc(v_mm[1], 1)
            pe.wait_ge(gq_cp, 2 * HG)
            token_rows(vgw1, 4, MIX).then_inc(ring_used, 3)
            pe.wait_ge(v_cp[1], TT)
            pe.wait_ge(g_cp, TT)
            scores(1, N1, mqT1[:, 0, :], kTm[:, 1, 0, :])
            weighted(1, 0, prob1, pT1, v_mem(1, 0), N1)
            scores(1, N1 + 1, mqT1[:, 1, :], kTm[:, 1, 1, :])
            pe.wait_ge(at_oT, NPAIR + MPAIR + 1)
            weighted(1, 1, prob1, pT1, v_mem(1, 1), N1 + 1)
            pe.wait_ge(at_oT, NPAIR + 2 * MPAIR)
            pe.wait_ge(k_st, 2)
            for d in range(2):
                for a in range(TT):
                    for h in range(HG):
                        t = pe.transpose(ps[:, 2 * d + a, h * DK:(h + 1) * DK],
                                         ks[:, d, h * T + a * P:h * T + a * P + P], ident[0:DK, 0:DK])
            t.then_inc(kst_mm, 1)
            pe.wait_ge(q_in, 2)
            pe.wait_ge(k_in, 2)
            for d in range(2):
                for h in range(HG):
                    for n in range(NCH):
                        c = slice(h * T + n * CH, h * T + (n + 1) * CH)
                        r = (n % 2) * 64
                        t = pe.matmul(ps[r:r + 64, 4 + d, (h * TT + n // 2) * CH:(h * TT + n // 2 + 1) * CH],
                                      ki[:, d, c], qi[:, d, c], start=True, stop=True)
                t.then_inc(a_mm, 1)
            pe.wait_ge(kst_cp, 4)
            i = 0
            for step in range(3):
                for d in range(2):
                    n = step if d == 0 else NCH - 1 - step
                    bank = (6, 0)[i % 2]
                    if i >= 2:
                        pe.wait_ge(u_st, i - 1)
                    r = (n % 2) * 64
                    for h in range(HG):
                        t = pe.matmul(ps[0:DK, bank + h // 2, (h % 2) * DV:(h % 2 + 1) * DV],
                                      ksT[r:r + 64, d, n // 2, h, :], v1[r:r + 64, n // 2, h * DV:(h + 1) * DV],
                                      start=True, stop=True)
                    t.then_inc(u_mm, 1)
                    i += 1
            pe.wait_ge(a_cp, 1)
            pe.wait_ge(q_st, 2)
            pe.wait_ge(u_st, 6)
            for a in range(TT):
                for h in range(HG):
                    for half in range(2):
                        n = 2 * a + half
                        r = 64 * half
                        o = ps[r:r + 64, 2 + 2 * a + h // 2, (h % 2) * DV:(h % 2 + 1) * DV]
                        c = slice(h * T + n * CH, h * T + (n + 1) * CH)
                        inter = ([(0, n - 1)] if n > 0 else []) + ([(1, NCH - 2 - n)] if n < NCH - 1 else [])
                        pe.matmul(o, asum[r:r + 64, h, a, :], v1[r:r + 64, a, h * DV:(h + 1) * DV],
                                  start=True, stop=False)
                        for j, (d, s) in enumerate(inter):
                            t = pe.matmul(o, qs[:, d, c], state[:, d, s, h, :], start=False, stop=j == len(inter) - 1)
                t.then_inc(o_mm, 1)
            for a in range(TT):
                pe.wait_ge(o_mix, a + 1)
                for c in range(6):
                    i = a * 6 + c
                    t = pe.transpose(ps[:, (6, 7, 0)[i // 4], (i % 4) * P:(i % 4) * P + P], g1[:, a, c * P:(c + 1) * P],
                                     ident)
            t.then_inc(m_tr, 1)
            pe.wait_ge(m_cp, 3)
            out_proj(1, 3)
            transposes(4, xs)
            route(1)
            pe.wait_ge(rt_n[1], 1)
            experts(1)

        @block.scalar
        def _(act_e):
            act_e.dma_start(mixT_as_tokens, mem[0].rearrange("(a p) d -> p a d", p=P)).then_inc(s_mem, 16)
            act_e.dma_start(cst[:], consts).then_inc(s_cst, 16)
            small = [(gcol[:, 0, :], mem_norm.rearrange("(p k) -> p k", k=KC))]
            for l in range(2):
                small += [(gcol[:, 1 + 2 * l, :], norm_mix[l].rearrange("(p k) -> p k", k=KC)),
                          (gcol[:, 2 + 2 * l, :], norm_ffn[l].rearrange("(p k) -> p k", k=KC)),
                          (wgrp[:, l], moe_w_group[l].rearrange("(p k) n -> p k n", k=KC)),
                          (wrtr[:, l], moe_w_router[l].rearrange("(p k) n -> p k n", k=KC)),
                          (rbias[:, l, 0:NG], moe_b_group[l:l + 1, :].to_broadcast([P, NG])),
                          (rbias[:, l, NG:NG + NE], moe_b_router[l:l + 1, :].to_broadcast([P, NE]))]
            small += [(gnorm[:], gla_out_norm[0:1, :].to_broadcast([P, DV]))]
            for d in range(2):
                small += [(gup[16 * d:16 * d + 16, d, :], gla_gate_up[0, d])]
            assert SMALL == 16 * (len(small) + 2)
            act_e.wait_ge(s_gup0, 1)
            for dst, src in small:
                act_e.dma_start(dst, src).then_inc(s_small, 16)
            with nc.allow_non_contiguous_dma(reason="768 gate biases, feature on the partition"):
                for d in range(2):
                    act_e.dma_start(gbias[:, d, :], gla_gate_bias[0, d].rearrange("(h p) -> p h", p=DK)).then_inc(s_small, 16)
            def norm(i):
                src = norm_src(i)
                for a in range(TT):
                    nc.scalar.activation(xs[:, a, :], src[:, a, :], ACT.Square,
                                         accum_out=st[:, 2 * i + a:2 * i + a + 1]).then_inc(n_sq, 1)
                act_e.wait_ge(n_var, i + 1)
                nc.scalar.activation(st[:, 24 + 2 * i:26 + 2 * i], st[:, 12 + 2 * i:14 + 2 * i], ACT.Sqrt).then_inc(n_sd, 1)

            def copy_kv(l):
                act_e.wait_ge(kv_mm[l], 1)
                nc.scalar.copy(kTm[:, l].rearrange("p m t -> p (m t)"), ps[:, 6, :]).then_inc(kv_cp[l], 1)
                act_e.wait_ge(ring_used, (1, PRE0)[l])
                nc.scalar.copy(vm[:, l].rearrange("p a n -> p (a n)"), ps[:, 7, :]).then_inc(kv_cp[l], 1)

            def exps(l, n, prob, raw):
                act_e.wait_ge(at_mx, n + 1)
                for h in range(2):
                    for a in range(TT):
                        i = 2 * h + a
                        src = ps[:, 2 + h, a * T:(a + 1) * T] if raw else prob[:, h, a, :]
                        nc.scalar.activation(prob[:, h, a, :], src, ACT.Exp, bias=st[:, 40 + i:41 + i],
                                             scale=DH ** -0.5 if raw else 1.0,
                                             accum_out=st[:, 44 + i:45 + i]).then_inc(at_ex, 1)

            def copy_pT(l, n, pT):
                act_e.wait_ge(at_tr, n + 1)
                nc.scalar.copy(pT.rearrange("p h a k -> p (h a k)"),
                               ps[:, 4:6, :].rearrange("p b n -> p (b n)")).then_inc(at_pT, 1)

            def copy_o(l, n, c):
                act_e.wait_ge(at_o, n + 1)
                nc.scalar.copy(mixT[:, c, :], ps[:, 6, 0:T]).then_inc(at_oT, 1)

            def route(l):
                act_e.wait_ge(rt_d[l], 1)
                nc.scalar.activation(t4a, t4a, ACT.Exp).then_inc(rt_e[l], 1)
                act_e.wait_ge(rt_d[l], 2)
                nc.scalar.activation(sc[:, 6, :], sc[:, 5, :], ACT.Exp).then_inc(rt_e[l], 1)

            def quad(rn, c, q):
                act_e.wait_ge(rn.sig.selT_mm, c + 1)
                nc.scalar.copy(selwT.rearrange("p a t -> p (a t)"), ps[:, 2, 0:T]).then_inc(rn.sig.selwT_ready, 1)
                act_e.wait_ge(rn.ring_used, q * FILLS + (rn.used_base + 4))
                nc.scalar.activation(sg, ps[:, 4, :], ACT.Exp, scale=-1.0).then_inc(rn.sig.exp_done, 1)
                act_e.wait_ge(rn.sig.actT_mm, c + 1)
                nc.scalar.copy(actT.rearrange("p j s -> p (j s)"), ps[:, 3, :]).then_inc(rn.sig.actT_ready, 1)
                act_e.wait_ge(rn.ring_used, q * FILLS + (rn.used_base + 12))
                for half in range(2):
                    nc.scalar.copy(yb[:, half * 512:half * 512 + 512], ps[:, 6 + half, :]).then_inc(rn.sig.yb_ready, 1)

            def experts(l):
                with act_e.Fori(0, NQ) as q:
                    quad(main[l], q + l * NQ, q)
                act_e.wait_ge(rt_n[l], 1)
                lo, hi = rounds(act_e, l)
                with act_e.If(hi > lo):
                    with act_e.Fori(lo, hi) as r:
                        with act_e.Fori(0, NQ) as g:
                            quad(extra, r * NQ + g, r * NQ + g)

            act_e.wait_ge(s_mem, 16)
            norm(0)
            act_e.wait_ge(s_x, 16)
            norm(1)
            copy_kv(0)
            act_e.wait_ge(v_mm[0], 1)
            for a in range(TT):
                nc.scalar.copy(v0[:, a, :].rearrange("p (b n) -> p b n", b=2), ps[:, 4 + 2 * a:6 + 2 * a, 0:384]).then_inc(v_cp[0], 1)
            act_e.wait_ge(ring_used, 3)
            nc.scalar.copy(mqT0.rearrange("p m t -> p (m t)"), ps[:, 0, :]).then_inc(mq_cp[0], 1)
            for p in range(NPAIR):
                if p % 2 == 0:
                    act_e.wait_ge(qk_mm, p // 2 + 1)
                else:
                    act_e.wait_ge(ring_used, 3 + (p + 1) // 2)
                nc.scalar.copy(qk[:, p % 2].rearrange("p q t -> p (q t)"), ps[:, p % 2, :]).then_inc(qk_cp, 1)
                if p >= 1:
                    copy_pT(0, p - 1, pT0)
                    copy_o(0, p - 1, p - 1)
                exps(0, p, prob0, False)
            for n in range(NPAIR, NPAIR + MPAIR):
                copy_pT(0, n - 1, pT0)
                copy_o(0, n - 1, n - 1)
                exps(0, n, prob0, True)
            copy_pT(0, NPAIR + 1, pT0)
            copy_o(0, NPAIR + 1, NPAIR + 1)
            act_e.wait_ge(res[0], TT)
            norm(2)
            copy_kv(1)
            route(0)
            experts(0)

            act_e.wait_ge(moe_done[0], 1)
            norm(3)
            act_e.wait_ge(r_mm, 1)
            nc.scalar.copy(rT, ps[0:32, 4, 0:T]).then_inc(r_cp, 1)
            act_e.wait_ge(ring_used, B1 + 1)
            nc.scalar.copy(mqT1.rearrange("p m t -> p (m t)"), ps[:, 5, :]).then_inc(mq_cp[1], 1)
            act_e.wait_ge(l_na, 1)
            nc.scalar.activation(ki, ki, ACT.Exp).then_inc(l_ex, 1)
            act_e.wait_ge(l_ex, 1)
            nc.scalar.activation(ki, ki, ACT.Ln, bias=1.0).then_inc(l_ln, 1)
            for h in range(HG):
                if h < HG - 1:
                    act_e.wait_ge(gq_mm, h + 1)
                else:
                    act_e.wait_ge(ring_used, B1 + 3)
                nc.scalar.mul(qT[:, h, :], ps[0:DK, 4 + h, 0:T], DK ** -0.5).then_inc(gq_cp, 1)
                nc.scalar.copy(kT[:, h, :], ps[0:DK, 4 + h, T:2 * T]).then_inc(gq_cp, 1)
            act_e.wait_ge(d_b, 2)
            nc.scalar.activation(qs, bcum, ACT.Exp, scale=1 / 16).then_inc(e_done, 1)
            act_e.wait_ge(d_mid, 2)
            nc.scalar.activation(ki, qi, ACT.Exp, scale=-1 / 16).then_inc(e_done, 1)
            act_e.wait_ge(e_done, 2)
            nc.scalar.activation(qi, qi, ACT.Exp, scale=1 / 16).then_inc(e_done, 1)
            act_e.wait_ge(d_last, 2)
            nc.scalar.activation(ks, ks, ACT.Exp, scale=1 / 16).then_inc(e_done, 1)
            act_e.wait_ge(v_mm[1], 1)
            for a in range(TT):
                nc.scalar.copy(v1[:, a, :].rearrange("p (b n) -> p b n", b=2), ps[:, 2 * a:2 * a + 2, 0:384]).then_inc(v_cp[1], 1)
            act_e.wait_ge(ring_used, B1 + 6)
            for a in range(TT):
                nc.scalar.copy(g1[:, a, :].rearrange("p (b n) -> p b n", b=2), ps[:, 4 + 2 * a:6 + 2 * a, 0:384]).then_inc(g_cp, 1)
            act_e.wait_ge(g_cp, TT)
            nc.scalar.activation(sig1, g1, ACT.Exp, scale=-1.0).then_inc(g_ex, 1)
            exps(1, N1, prob1, True)
            copy_pT(1, N1, pT1)
            copy_o(1, N1, 6)
            exps(1, N1 + 1, prob1, True)
            copy_pT(1, N1 + 1, pT1)
            copy_o(1, N1 + 1, 7)
            act_e.wait_ge(kst_mm, 1)
            for d in range(2):
                for a in range(TT):
                    nc.scalar.copy(ksT[:, d, a].rearrange("p h c -> p (h c)"), ps[:, 2 * d + a, 0:HG * DK]).then_inc(kst_cp, 1)
            for a in range(TT):
                act_e.wait_ge(o_mm, a + 1)
                for h in range(HG):
                    i = HG * a + h
                    nc.scalar.activation(sqj[:, i * DV:(i + 1) * DV], ps[:, 2 + 2 * a + h // 2, (h % 2) * DV:(h % 2 + 1) * DV],
                                         ACT.Square, accum_out=st[:, 64 + i:65 + i]).then_inc(o_sq, 1)
            act_e.wait_ge(o_var, 1)
            nc.scalar.activation(st[:, 80:88], st[:, 72:80], ACT.Sqrt).then_inc(o_sd, 1)
            act_e.wait_ge(m_tr, 1)
            for b, bank in enumerate((6, 7, 0)):
                for j in range(4):
                    a, c = divmod(4 * b + j, 6)
                    ins = nc.scalar.copy(mixT[:, c, a * P:(a + 1) * P], ps[:, bank, j * P:(j + 1) * P])
                ins.then_inc(m_cp, 1)
            act_e.wait_ge(res[1], TT)
            norm(4)
            route(1)
            experts(1)
            act_e.dma_start(fnorm, final_norm.rearrange("(o d) -> o d", o=1).to_broadcast([P, D])).then_inc(s_fn, 16)
            act_e.wait_ge(moe_done[1], 1)
            norm(5)
            for a in range(TT):
                act_e.wait_ge(fin_ready, a + 1)
                act_e.dma_start(out[0, a * P:(a + 1) * P, :], fin[:, a, :]).then_inc(s_out, 16)
            act_e.wait_ge(s_out, 32)

        @block.vector
        def _(dve):
            V = nc.vector
            cnt = [0]

            def link(ins):
                cnt[0] += 1
                ins.then_inc(dchain, 1)
                dve.wait_ge(dchain, cnt[0])

            def norm_scale(i):
                dve.wait_ge(n_sq, TT * (i + 1))
                V.tensor_scalar(st[:, 12 + 2 * i:14 + 2 * i], st[:, 2 * i:2 * i + 2], 1.0 / D, EPS, ALU.mult, ALU.add).then_inc(n_var, 1)
                dve.wait_ge(n_sd, i + 1)
                link(V.reciprocal(st[:, 48 + 2 * i:50 + 2 * i], st[:, 24 + 2 * i:26 + 2 * i]))
                return st[:, 48 + 2 * i:50 + 2 * i]

            def norm(i, dst, hdst):
                r = norm_scale(i)
                for a in range(TT):
                    V.tensor_scalar(dst[:, a, :], norm_src(i)[:, a, :], r[:, a:a + 1], None, ALU.mult).then_inc(n_xs, 1)
                if i == 0:
                    dve.wait_ge(s_small, SMALL)
                for a in range(TT):
                    dve.wait_ge(n_tr, TT * i + a + 1)
                    V.tensor_tensor(hdst[:, :, a * P:(a + 1) * P],
                                    ps[:, 2 * a:2 * a + 2, :].rearrange("p b (k t) -> p (b k) t", t=P),
                                    gcol[:, i, :].unsqueeze(2).to_broadcast([P, KC, P]), ALU.mult).then_inc(n_hT, 1)

            def softmax_max(l, n, prob, raw):
                dve.wait_ge(at_sc, n + 1)
                if raw:
                    link(V.tensor_reduce(st[:, 36:40].rearrange("p (h a) -> p h a", h=2),
                                         ps[:, 2:4, :].rearrange("p h (a k) -> p h a k", a=TT), AX_X, ALU.max))
                    V.tensor_scalar(st[:, 40:44], st[:, 36:40], -DH ** -0.5, None, ALU.mult).then_inc(at_mx, 1)
                    return
                for h in range(2):
                    for a in range(TT):
                        bias = rpbt[:, 2 * n + h, 2 - 2 * a:6 - 2 * a, :].rearrange("p r c -> p (r c)")
                        link(V.scalar_tensor_tensor(prob[:, h, a, :], ps[:, 2 + h, a * T:(a + 1) * T], DH ** -0.5, bias,
                                                    ALU.mult, ALU.add))
                link(V.tensor_reduce(st[:, 36:40].rearrange("p (h a) -> p h a", h=2), prob, AX_X, ALU.max))
                V.tensor_scalar(st[:, 40:44], st[:, 36:40], -1.0, None, ALU.mult).then_inc(at_mx, 1)

            def softmax_div(l, n, prob):
                dve.wait_ge(at_ex, 4 * (n + 1))
                link(V.reciprocal(st[:, 60:64], st[:, 44:48]))
                V.tensor_tensor(prob.rearrange("p h a k -> p (h a) k"), prob.rearrange("p h a k -> p (h a) k"),
                                st[:, 60:64].unsqueeze(2).to_broadcast([P, 4, T]), ALU.mult).then_inc(at_p, 1)

            def add_mixed(l):
                dve.wait_ge(ring_used, (PRE0 - 1, B1 + 8)[l])
                for a in range(TT):
                    V.tensor_tensor(xres[:, a, :], xres[:, a, :], ps[:, 2 + 2 * a:4 + 2 * a, :].rearrange("p b n -> p (b n)"),
                                    ALU.add).then_inc(res[l], 1)

            def one_hot(dst, vals, top, n, tmp):
                link(V.tensor_tensor(tmp, vals, top.unsqueeze(2).to_broadcast([P, TT, n]), ALU.is_equal))
                im = iotam[:, 0:n].unsqueeze(1).to_broadcast([P, TT, n])
                link(V.tensor_tensor(tmp, tmp, im, ALU.mult))
                link(V.tensor_reduce(sc[:, 15, :], tmp, AX_X, ALU.min))
                link(V.tensor_tensor(dst, im, sc[:, 15, :].unsqueeze(2).to_broadcast([P, TT, n]), ALU.is_equal))

            def route(l):
                dve.wait_ge(rt_mm[l], 1)
                link(V.tensor_tensor(lg, ps[:, 4, 0:128].rearrange("p (a n) -> p a n", a=TT)[:, :, 0:NG + NE],
                                     rbias[:, l, :].unsqueeze(1).to_broadcast([P, TT, NG + NE]), ALU.add))
                lgg, lge = lg[:, :, 0:NG], lg[:, :, NG:NG + NE]
                link(V.tensor_reduce(sc[:, 0, :], lgg, AX_X, ALU.max))
                V.tensor_tensor(t4a, lgg, sc[:, 0, :].unsqueeze(2).to_broadcast([P, TT, NG]), ALU.subtract).then_inc(rt_d[l], 1)
                one_hot(goh, lgg, sc[:, 0, :], NG, gpen)
                link(V.tensor_scalar(gpen, goh, BIG, -BIG, ALU.mult, ALU.add))
                for a in range(TT):
                    for src, dst, by, op in ((lge, me, goh, ALU.mult), (me, me, gpen, ALU.add)):
                        link(V.tensor_tensor(dst[:, a, :].rearrange("p (g e) -> p g e", g=NG),
                                             src[:, a, :].rearrange("p (g e) -> p g e", g=NG),
                                             by[:, a, :].unsqueeze(2).to_broadcast([P, NG, EG]), op))
                link(V.tensor_reduce(sc[:, 3, :], me, AX_X, ALU.max))
                one_hot(oh1, me, sc[:, 3, :], NE, t32a)
                link(V.scalar_tensor_tensor(t32b, oh1, -2 * BIG, me, ALU.mult, ALU.add))
                link(V.tensor_reduce(sc[:, 4, :], t32b, AX_X, ALU.max))
                V.tensor_tensor(sc[:, 5, :], sc[:, 4, :], sc[:, 3, :], ALU.subtract).then_inc(rt_d[l], 1)
                one_hot(oh2, t32b, sc[:, 4, :], NE, t32a)
                V.tensor_tensor(msk, oh1, oh2, ALU.add).then_inc(rt_m[l], 1)
                dve.wait_ge(rt_e[l], 2)
                link(V.tensor_reduce(sc[:, 1, :], t4a, AX_X, ALU.add))
                link(V.tensor_scalar(sc[:, 7, :], sc[:, 6, :], 1.0, None, ALU.add))
                link(V.tensor_tensor(sc[:, 8, :], sc[:, 7, :], sc[:, 1, :], ALU.mult))
                link(V.reciprocal(sc[:, 9, :], sc[:, 8, :]))
                link(V.tensor_tensor(sc[:, 10, :], sc[:, 9, :], sc[:, 6, :], ALU.mult))
                link(V.memset(wtok, 0.0))
                link(V.memset(ppos, 1000.0))
                link(V.tensor_tensor(t32a, oh1, sc[:, 9, :].unsqueeze(2).to_broadcast([P, TT, NE]), ALU.mult))
                link(V.tensor_tensor(t32b, oh2, sc[:, 10, :].unsqueeze(2).to_broadcast([P, TT, NE]), ALU.mult))
                link(V.tensor_tensor(wtok[:, :, 0:NE], t32a, t32b, ALU.add))
                dve.wait_ge(rt_p[l], 1)
                dve.wait_ge(rt_m[l], 1)
                link(V.tensor_scalar(t32a, msk, -1000.0, 1000.0, ALU.mult, ALU.add))
                link(V.tensor_tensor(ppos[:, :, 0:NE], t32a, ps[:, 5, 0:2 * NE].rearrange("p (a e) -> p a e", a=TT), ALU.add))
                link(V.tensor_reduce(ntmp[:, 0:1], ps[:, 5, 2 * NE:3 * NE], AX_X, ALU.max))
                link(V.tensor_tensor(cmp8, ntmp[:, 0:1].to_broadcast([P, 8]), cst[:, C_THR:C_THR + 8], ALU.is_gt))
                link(V.tensor_reduce(ntmp[:, 1:2], cmp8, AX_X, ALU.add))
                if l == 0:
                    link(V.tensor_copy(roundf[:], ntmp[:, 1:2]))
                    V.tensor_copy(nround[:, 0:1], ntmp[:, 1:2]).then_inc(rt_n[l], 1)
                else:
                    V.tensor_tensor(nround[:, 1:2], roundf[:], ntmp[:, 1:2], ALU.add).then_inc(rt_n[l], 1)

            def select(rn, g):
                V.tensor_tensor(sel, iota.unsqueeze(1).unsqueeze(1).to_broadcast([P, TT, E4, CAP]),
                                ppos[:, :, bass.ds(g * E4, E4)].unsqueeze(3).to_broadcast([P, TT, E4, CAP]),
                                ALU.is_equal).then_inc(rn.sig.sel_ready, 1)

            def select_w(rn, g, count):
                dve.wait_ge(rn.sig.sel_ready, count)
                V.tensor_tensor(selw, sel, wtok[:, :, bass.ds(g * E4, E4)].unsqueeze(3).to_broadcast([P, TT, E4, CAP]),
                                ALU.mult).then_inc(rn.sig.sel_ready, 1)

            def quad(rn, l, c, q, g, sel_count):
                dve.wait_ge(rn.sig.gathered, c + 1)
                for b in range(2):
                    V.tensor_tensor(xsel[:, 4 * b:4 * b + 4, :], ps[:, b, :].rearrange("p (k t) -> p k t", t=P),
                                    gcol[:, 2 + 2 * l, 4 * b:4 * b + 4].unsqueeze(2).to_broadcast([P, 4, P]),
                                    ALU.mult).then_inc(rn.sig.xsel_ready, 1)
                select(rn, g + 1)
                select_w(rn, g + 1, sel_count + 1)
                dve.wait_ge(rn.sig.exp_done, c + 1)
                V.tensor_scalar(sg, sg, 1.0, None, ALU.add).then_inc(rn.sig.silu, 1)
                dve.wait_ge(rn.sig.silu, c * 3 + 1)
                V.reciprocal(sg, sg).then_inc(rn.sig.silu, 1)
                dve.wait_ge(rn.sig.silu, c * 3 + 2)
                V.tensor_tensor(sg, sg, ps[:, 4, :], ALU.mult).then_inc(rn.sig.silu, 1)
                dve.wait_ge(rn.sig.silu, c * 3 + 3)
                dve.wait_ge(rn.ring_used, q * FILLS + (rn.used_base + 8))
                V.tensor_tensor(act, sg, ps[:, 5, :], ALU.mult).then_inc(rn.sig.act_ready, 1)
                dve.wait_ge(rn.sig.scattered, c + 1)
                for a in range(TT):
                    V.tensor_tensor(xres[:, a, :], xres[:, a, :], ps[:, 4 + 2 * a:6 + 2 * a, :].rearrange("p b n -> p (b n)"),
                                    ALU.add).then_inc(rn.sig.added, 1)
                dve.wait_ge(rn.sig.added, c * 2 + 2)

            def experts(l):
                dve.wait_ge(rt_n[l], 1)
                select(main[l], 0)
                select_w(main[l], 0, l * SELS + 1)
                with dve.Fori(0, NQ) as q:
                    quad(main[l], l, q + l * NQ, q, q, q * 2 + (l * SELS + 2))
                lo, hi = rounds(dve, l)
                with dve.If(hi > lo):
                    with dve.Fori(lo, hi) as r:
                        V.tensor_scalar(ppos, ppos, -float(CAP), None, ALU.add).then_inc(next_round, 1)
                        dve.wait_ge(next_round, r + 1)
                        select(extra, 0)
                        select_w(extra, 0, r * SELS + 1)
                        with dve.Fori(0, NQ) as g:
                            quad(extra, l, r * NQ + g, r * NQ + g, g, r * SELS + g * 2 + 2)
                V.tensor_copy(ntmp[:, 0:1], xres[:, 0, 0:1]).then_inc(moe_done[l], 1)

            dve.wait_ge(s_mem, 16)
            dve.wait_ge(s_cst, 16)
            norm(0, mixT_as_tokens, memT)
            dve.wait_ge(s_x, 16)
            norm(1, xs, hT)
            for c in range(RPC):
                dve.wait_ge(rp_mm, c + 1)
                V.tensor_tensor(rpbt.rearrange("p h i c -> p (h i) c")[:, 8 * c:8 * c + 8, :],
                                ps[:, 4 + c % 2, :].rearrange("p (i c) -> p i c", c=GRID),
                                cst[:, C_NAM:C_NAM + GRID].unsqueeze(1).to_broadcast([P, 8, GRID]),
                                ALU.add).then_inc(s_mask, 1)
            dve.wait_ge(s_mask, RPC)
            for n in range(NPAIR + MPAIR):
                softmax_max(0, n, prob0, n >= NPAIR)
                softmax_div(0, n, prob0)
            add_mixed(0)
            dve.wait_ge(res[0], TT)
            norm(2, xs, hT)
            route(0)
            experts(0)

            dve.wait_ge(moe_done[0], 1)
            norm(3, xs, hT)
            dve.wait_ge(z_mm, 1)
            for d in range(2):
                V.tensor_tensor(qs[:, d].rearrange("p (h t) -> p h t", t=T),
                                ps[0:DK, 2 * d:2 * d + 2, :].rearrange("p b (h t) -> p (b h) t", t=T),
                                gbias[:, d, :].unsqueeze(2).to_broadcast([DK, HG, T]), ALU.add).then_inc(z_sb, 1)
            dve.wait_ge(z_sb, 2)
            V.scalar_tensor_tensor(ki, qs, -1.0, qs, ALU.mult, ALU.min).then_inc(l_na, 1)
            dve.wait_ge(l_ln, 1)
            link(V.scalar_tensor_tensor(qi, qs, 0.0, ki, ALU.min, ALU.subtract))
            dve.wait_ge(resets, 3)
            V.tensor_tensor_scan(bcum[:, 0], ks[:, 0], qi[:, 0], 0.0, ALU.mult, ALU.add).then_inc(d_b, 1)
            V.tensor_tensor_scan(bcum[:, 1][:, ::-1], ks[:, 1][:, ::-1], qi[:, 1][:, ::-1], 0.0, ALU.mult, ALU.add).then_inc(d_b, 1)
            dve.wait_ge(d_b, 2)

            def chunked(t, d):
                return t[:, d].rearrange("p (n c) -> p n c", c=CH)

            MID, LAST = (CH // 2 - 1, CH // 2), (CH - 1, 0)
            for d in range(2):
                b = chunked(bcum, d)
                V.tensor_tensor(chunked(qi, d), b, b[:, :, MID[d]:MID[d] + 1].to_broadcast([DK, HG * NCH, CH]),
                                ALU.subtract).then_inc(d_mid, 1)
            for d in range(2):
                b = chunked(bcum, d)
                V.tensor_tensor(chunked(ks, d), b[:, :, LAST[d]:LAST[d] + 1].to_broadcast([DK, HG * NCH, CH]), b,
                                ALU.subtract).then_inc(d_last, 1)
            dve.wait_ge(gq_cp, 2 * HG)
            for i, (e, by, s) in enumerate(((qs, qT, None), (ki, kT, k_in), (qi, qT, q_in), (ks, kT, k_st))):
                dve.wait_ge(e_done, i + 1)
                if i == 0:
                    for d in range(2):
                        link(V.tensor_copy(st_dec[:, d, :].unsqueeze(2), chunked(qs, d)[:, :, LAST[d]:LAST[d] + 1]))
                    s = q_st
                for d in range(2):
                    V.tensor_tensor(e[:, d], e[:, d], by.rearrange("p h t -> p (h t)"), ALU.mult).then_inc(s, 1)
            dve.wait_ge(g_ex, 1)
            link(V.tensor_scalar(sig1, sig1, 1.0, None, ALU.add))
            link(V.reciprocal(sig1, sig1))
            link(V.tensor_tensor(g1, g1, sig1, ALU.mult))
            V.tensor_tensor(g1.rearrange("p a (h v) -> p (a h) v", v=DV), g1.rearrange("p a (h v) -> p (a h) v", v=DV),
                            gnorm[:].unsqueeze(1).to_broadcast([P, TT * HG, DV]), ALU.mult).then_inc(g_silu, 1)
            for m in range(MPAIR):
                softmax_max(1, N1 + m, prob1, True)
                softmax_div(1, N1 + m, prob1)
            dve.wait_ge(a_mm, 2)
            for d in range(2):
                link(V.tensor_tensor(amask[:, d].rearrange("p h a c -> p (h a) c"),
                                     ps[:, 4 + d, :].rearrange("p (h c) -> p h c", c=CH),
                                     cst[:, (C_MF, C_MB)[d]:(C_MF, C_MB)[d] + CH].unsqueeze(1).to_broadcast([P, HG * TT, CH]),
                                     ALU.mult))
            V.tensor_tensor(asum, amask[:, 0], amask[:, 1], ALU.add).then_inc(a_cp, 1)
            i = 0
            for step in range(3):
                for d in range(2):
                    n = step if d == 0 else NCH - 1 - step
                    bank = (6, 0)[i % 2]
                    dve.wait_ge(u_mm, i + 1)
                    u = ps[0:DK, bank:bank + 2, 0:2 * DV].rearrange("p b (h v) -> p b h v", h=2)
                    new = state[:, d, step].rearrange("p (b h) v -> p b h v", h=2)
                    if step == 0:
                        V.tensor_copy(new, u).then_inc(u_st, 1)
                    else:
                        dve.wait_ge(u_st, i)
                        for h in range(HG):
                            ins = V.scalar_tensor_tensor(state[:, d, step, h, :], state[:, d, step - 1, h, :],
                                                         st_dec[:, d, h * NCH + n:h * NCH + n + 1], u[:, h // 2, h % 2, :],
                                                         ALU.mult, ALU.add)
                        ins.then_inc(u_st, 1)
                    i += 1
            dve.wait_ge(o_sq, TT * HG)
            V.tensor_scalar(st[:, 72:80], st[:, 64:72], 1.0 / DV, EPS, ALU.mult, ALU.add).then_inc(o_var, 1)
            dve.wait_ge(o_sd, 1)
            link(V.reciprocal(st[:, 88:96], st[:, 80:88]))
            for a in range(TT):
                o = ps[:, 2 + 2 * a:4 + 2 * a, 0:2 * DV].rearrange("p b (h v) -> p b h v", h=2)
                r = st[:, 88 + HG * a:88 + HG * a + HG].rearrange("p (b h) -> p b h", h=2)
                link(V.tensor_tensor(sig1[:, a].rearrange("p (b h v) -> p b h v", b=2, h=2), o,
                                     r.unsqueeze(3).to_broadcast([P, 2, 2, DV]), ALU.mult))
                V.tensor_tensor(g1[:, a, :], g1[:, a, :], sig1[:, a, :], ALU.mult).then_inc(o_mix, 1)
            add_mixed(1)
            dve.wait_ge(res[1], TT)
            norm(4, xs, hT)
            route(1)
            experts(1)
            dve.wait_ge(moe_done[1], 1)
            dve.wait_ge(s_fn, 16)
            r = norm_scale(5)
            for a in range(TT):
                V.scalar_tensor_tensor(fin[:, a, :], xres[:, a, :], r[:, a:a + 1], fnorm, ALU.mult, ALU.mult).then_inc(fin_ready, 1)


def kernel(**inputs):
    import numpy as np
    import concourse.bacc as bacc
    from concourse.bass_utils import run_bass_kernel_spmd as run

    nc = bacc.Bacc("TRN2", target_bir_lowering=False, num_devices=1)
    arrays, args = {}, []
    data = dict(inputs)
    data["consts"] = make_consts()
    for name in NAMES:
        a = np.ascontiguousarray(data[name])
        arrays[f"in_{name}"] = a
        args.append(nc.dram_tensor(f"in_{name}", a.shape, mybir.dt.from_np(a.dtype), kind="ExternalInput").ap())
    o = nc.dram_tensor("out_0", (1, T, D), F32, kind="ExternalOutput").ap()
    build(nc, *args, o)
    r = run(nc, [arrays], core_ids=[0])
    return r.results[0]["out_0"]


NAMES = ["x", "mem", "mem_norm", "final_norm", "norm_mix", "norm_ffn", "w_mem_kv", "w_out", "na_w_in", "na_rpb",
         "gla_w_in", "gla_gate_up", "gla_gate_bias", "gla_out_norm", "moe_w_group", "moe_b_group", "moe_w_router",
         "moe_b_router", "moe_w1", "moe_w3", "moe_w2", "consts"]
```

```python
from contextlib import ExitStack

import concourse.bass as bass
from concourse import mybir

F32 = mybir.dt.float32
I32 = mybir.dt.int32
ALU = mybir.AluOpType
ACT = mybir.ActivationFunctionType
AX_X = mybir.AxisListType.X

P = 128
D = 1024
T = 256
TT = T // P
KC = D // P
EPS = 1e-6
GRID = 64
DH = 64
MIX = 768
NPAIR = 6
MPAIR = 2
RPB_H, RPB_W = 15, 31
NA_DR = 6
HG, DK, DV, CH = 4, 96, 192, 64
NCH = T // CH
NG, EG = 4, 8
NE = NG * EG
FF = 512
E4 = 4
CAP = 32
NQ = NE // E4
SELS = 2 * NQ + 2
FILLS = 12
SLOTS = 6
SLOT = 4096
BIG = 1e30

C_ID, C_ONE, C_TRI, C_IOTA, C_IOTAM, C_THR, C_NAM, C_MF, C_MB = 0, 128, 256, 384, 416, 448, 456, 520, 584
C_FLIP = 648
C_END = 776
RPC = 2 * NPAIR * NA_DR * GRID // 512
NBANK = {0: (0, 2), 1: (4, 6), 2: (4, 6), 3: (0, 2), 4: (6, 0)}
KVB, WOB, OB, KSTB, RTB = (0, 6), ((0, 2), (4, 2)), (2, 0), (0, 1, 7, 6), (0, 4)
i_xs = {0: 0, 1: 1, 3: 2}
N1 = NPAIR + MPAIR
SMALL = 16 * 13


def make_consts():
    import numpy as np

    c = np.zeros((P, C_END), np.float32)
    c[:, C_ID:C_ID + P] = np.eye(P)
    c[:, C_ONE:C_ONE + P] = 1.0
    c[:, C_TRI:C_TRI + P] = np.triu(np.ones((P, P)), 1)
    c[:, C_IOTA:C_IOTA + 32] = np.arange(32)
    c[:, C_IOTAM:C_IOTAM + 32] = np.arange(32) - 64
    c[:, C_THR:C_THR + 8] = CAP * (np.arange(8) + 1)
    col = np.arange(P) % GRID
    start = np.clip(col - 8, 0, GRID - 16)
    key = np.arange(GRID)
    inside = (key[None] >= start[:, None]) & (key[None] < start[:, None] + 16)
    c[:, C_NAM:C_NAM + GRID] = np.where(inside, 0.0, -BIG)
    j = np.arange(P) % CH
    i = np.arange(CH)
    c[:, C_MF:C_MF + CH] = i[None] >= j[:, None]
    c[:, C_MB:C_MB + CH] = i[None] <= j[:, None]
    c[:, C_FLIP:C_FLIP + P] = np.kron(np.eye(2), np.eye(GRID)[::-1])
    return c


def build(nc, x, mem, mem_norm, final_norm, norm_mix, norm_ffn, w_mem_kv, w_out, na_w_in, na_rpb, gla_w_in,
          gla_gate_up, gla_gate_bias, gla_out_norm, moe_w_group, moe_b_group, moe_w_router, moe_b_router,
          moe_w1, moe_w3, moe_w2, consts, out):
    with ExitStack() as ctx:
        def sb(name, shape, dt=F32):
            return ctx.enter_context(nc.sbuf_tensor(name, shape, dt))

        def sem(name):
            return ctx.enter_context(nc.semaphore(name))

        ring = sb("ring", [P, SLOTS * SLOT])
        cst = sb("cst", [P, C_END])
        gcol = sb("gcol", [P, 5, KC])
        wlog = sb("wlog", [P, 2, KC, NG + NE])
        rbias = sb("rbias", [P, 2, NG + NE])
        gnorm = sb("gnorm", [P, DV])
        gup = sb("gup", [32, 2, HG * DK])
        gbias = sb("gbias", [DK, 2, HG])
        xres = sb("xres", [P, TT, D])
        xs = sb("xs", [P, TT, D])
        hT = sb("hT", [P, KC, T])
        mixT = sb("mixT", [P, KC, T])
        kTm = sb("kTm", [P, 2, MPAIR, T])
        vm = sb("vm", [P, 2, TT, MPAIR * P])
        st = sb("st", [P, 96])
        st_dec = sb("st_dec", [DK, 2, HG * NCH])
        nround = sb("nround", [P, 2], I32)
        roundf = sb("roundf", [P, 1])
        ARENA = 15360
        arena = sb("arena", [P, ARENA])

        def cut(off, *dims, parts=P):
            n = 1
            for v in dims:
                n *= v
            assert off + n <= ARENA
            v = arena[0:parts, off:off + n]
            if len(dims) == 1:
                return v
            names = "abcde"[:len(dims)]
            return v.rearrange(f"p ({' '.join(names)}) -> p {' '.join(names)}",
                               **{names[i]: dims[i] for i in range(1, len(dims))})

        ps = ctx.enter_context(nc.psum_tensor("ps", [P, 8, 512], F32))

        ident = cst[:, C_ID:C_ID + P]
        ones = cst[:, C_ONE:C_ONE + P]
        tri = cst[:, C_TRI:C_TRI + P]
        iota = cst[:, C_IOTA:C_IOTA + 32]
        iotam = cst[:, C_IOTAM:C_IOTAM + 32]

        rpbt = cut(0, 2 * NPAIR, NA_DR, GRID)
        v0 = cut(4608, TT, MIX)
        qk = cut(6144, 2, 2, T)
        mqT0 = cut(7168, MPAIR, T)
        prob0 = cut(7680, 2, TT, T)
        pT0 = xs[:, 0, :].rearrange("p (h a k) -> p h a k", h=2, a=TT)
        rpbraw = cut(8704, 2 * NPAIR, NA_DR, GRID)
        memT = cut(ARENA - 2048, KC, T)
        v1 = cut(0, TT, MIX)
        g1 = cut(1536, TT, MIX)
        qT = cut(3072, HG, T, parts=DK)
        kT = cut(4096, HG, T, parts=DK)
        bcum = cut(5120, 2, HG * T, parts=DK)
        qi = cut(7168, 2, HG * T, parts=DK)
        ki = cut(9216, 2, HG * T, parts=DK)
        qs = cut(11264, 2, HG * T, parts=DK)
        ks = cut(13312, 2, HG * T, parts=DK)
        mqT1 = mixT[:, 6:8, :]
        prob1 = mixT[:, 0:4, :].rearrange("p (h a) k -> p h a k", h=2)
        pT1 = cut(3072, 2, TT, T)
        ksT = xs[:, :, :].rearrange("p a d -> p (a d)")[:, 0:2 * TT * HG * DK].rearrange(
            "p (d a h c) -> p d a h c", d=2, a=TT, h=HG)
        rT = xs[0:32, :, :].rearrange("p a d -> p (a d)")[:, 1792:2048]
        amask = cut(3072, 2, HG, TT, CH)
        asum = cut(4096, HG, TT, CH)
        state = cut(5120, 2, 3, HG, DV, parts=DK)
        sig1 = cut(13312, TT, MIX)
        ppos = cut(0, TT, NE + E4)
        wtok = cut(80, TT, NE + E4)
        sel = cut(160, TT, E4, CAP)
        selw = cut(416, TT, E4, CAP)
        selwT = cut(672, TT, P)
        xsel = cut(928, KC, P)
        sg = cut(1952, FF)
        act = cut(2464, FF)
        actT = cut(2976, FF // P, P)
        yb = cut(3488, D)
        lg = cut(4512, TT, NG + NE)
        t4a = cut(4600, TT, NG)
        goh = cut(4608, TT, NG)
        gpen = cut(4616, TT, NG)
        me = cut(4624, TT, NE)
        oh1 = cut(4688, TT, NE)
        oh2 = cut(4752, TT, NE)
        t32a = cut(4816, TT, NE)
        t32b = cut(4880, TT, NE)
        msk = cut(4944, TT, NE)
        sc = cut(5008, 16, TT)
        cmp8 = cut(5040, 8)
        ntmp = cut(5048, 2)
        fnorm = cut(6144, D)
        fin = cut(7168, TT, D)

        mixT_as_tokens = mixT[:, :, :].rearrange("p c t -> p (c t)").rearrange("p (a d) -> p a d", a=TT)
        sqj = hT[:, :, :].rearrange("p c t -> p (c t)")

        def norm_src(i):
            return mixT_as_tokens if i == 0 else xres

        s_x, s_mem, s_cst, s_rpb, s_small = sem("x_in"), sem("mem_in"), sem("const_in"), sem("rpb_in"), sem("small_in")
        s_gain = sem("gains_in")
        s_gup0 = sem("gup_zeroed")
        s_fn = sem("final_norm_in")
        s_out = sem("out_written")
        ring_in = [sem(f"ring_in{i}") for i in range(SLOTS)]
        ring_used = sem("ring_used")
        dchain = sem("dve_chain")
        sp_spare = sem("sp_spare")
        fin_ready = sem("final_ready")
        next_round = sem("next_round")
        n_sq = sem("squares")
        n_var = sem("variance")
        n_sd = sem("deviation")
        n_xs = sem("scaled")
        n_tr = sem("transposed")
        n_hT = sem("normed")
        kv_mm = [sem(f"memkv_mm{i}") for i in range(2)]
        kv_cp = [sem(f"memkv_cp{i}") for i in range(2)]
        v_mm = [sem(f"v_mm{i}") for i in range(2)]
        v_cp = [sem(f"v_cp{i}") for i in range(2)]
        mq_cp = [sem(f"mq_cp{i}") for i in range(2)]
        qk_mm, qk_cp = sem("qk_mm"), sem("qk_cp")
        at_sc = sem("scores")
        at_mx = sem("negmax")
        at_ex = sem("exps")
        at_p = sem("probs")
        at_tr = sem("probsT_mm")
        at_pT = sem("probsT")
        at_o = sem("pv_mm")
        at_oT = sem("mixT")
        s_mask, rp_mm = sem("rpb_masked"), sem("rpb_turned")
        res = [sem(f"mixed{i}") for i in range(2)]
        wo_mm = sem("wout_tile0")
        mq_mm = sem("mq_mm")
        r_mm, r_cp, z_mm, z_sb = sem("rank_mm"), sem("rank_cp"), sem("z_mm"), sem("z_biased")
        gq_mm, gq_cp = sem("gla_qk_mm"), sem("gla_qk_cp")
        g_mm, g_cp, g_ex = sem("g_mm"), sem("g_cp"), sem("g_sigmoid")
        l_na, l_ex, l_ln = sem("neg_abs"), sem("ls_exp"), sem("ls_ln")
        d_b, d_mid, d_last = sem("b_cum"), sem("b_minus_mid"), sem("last_minus_b")
        e_done = sem("decay_exps")
        q_in, k_in, q_st, k_st = sem("q_intra"), sem("k_intra"), sem("q_state"), sem("k_state")
        kst_mm, kst_cp = sem("k_stateT_mm"), sem("k_stateT")
        a_mm, a_cp = sem("a_mm"), sem("a_masked")
        u_mm, u_st = sem("u_mm"), sem("state_ready")
        o_mm, o_sq, o_var, o_sd, o_mix = sem("o_mm"), sem("o_squares"), sem("o_variance"), sem("o_dev"), sem("o_mix")
        m_tr, m_cp = sem("mix_tr"), sem("mix_cp")
        resets = sem("scan_resets")
        rt_mm = [sem(f"logits{i}") for i in range(2)]
        rt_d = [sem(f"exp_in{i}") for i in range(2)]
        rt_e = [sem(f"exp_out{i}") for i in range(2)]
        rt_m = [sem(f"routed{i}") for i in range(2)]
        rt_p = [sem(f"positions{i}") for i in range(2)]
        rt_n = [sem(f"rounds{i}") for i in range(2)]
        moe_done = [sem(f"moe_done{i}") for i in range(2)]

        class Quads:

            def __init__(self, tag):
                self.sel_ready = sem(f"sel_ready_{tag}")
                self.selT_mm = sem(f"selT_mm_{tag}")
                self.gathered = sem(f"gathered_{tag}")
                self.xsel_ready = sem(f"xsel_ready_{tag}")
                self.selwT_ready = sem(f"selwT_ready_{tag}")
                self.exp_done = sem(f"exp_done_{tag}")
                self.silu = sem(f"silu_{tag}")
                self.act_ready = sem(f"act_ready_{tag}")
                self.actT_mm = sem(f"actT_mm_{tag}")
                self.actT_ready = sem(f"actT_ready_{tag}")
                self.yb_ready = sem(f"yb_ready_{tag}")
                self.scattered = sem(f"scattered_{tag}")
                self.added = sem(f"added_{tag}")

        PRE0 = 8
        PRE1 = PRE0 + NQ * FILLS + 9

        def rows(w, c0, c1):
            return w.rearrange("(p k) n -> p k n", k=KC)[:, :, c0:c1]

        def region(slot, off, n, k):
            a = ring[:, slot * SLOT + off:slot * SLOT + off + n * k]
            return a.rearrange("p (k n) -> p k n", k=k)

        win0, win1 = na_w_in[0], gla_w_in[0]
        kvw = [region(0, 0, 512, KC), region(2, 0, 512, KC)]
        vw0 = region(1, 0, MIX, KC)
        mqw0 = region(1, MIX * KC, 256, KC)
        qkw = [[region(3 + p // 2, (p % 2) * 2048 + t * 1024, P, KC) for t in range(2)] for p in range(NPAIR)]
        wow = [[region(s, 0, D, 4) for s in (0, 1)], [region(s, 0, D, 4) for s in (3, 4)]]
        rw1 = region(3, 0, 288, KC)
        qkw1 = region(4, 0, MIX, KC)
        vgw1 = region(0, 0, 2 * MIX, KC)
        wo_src = [[w_out[l][512 * i:512 * i + 512, :].rearrange("(c p) n -> p c n", p=P) for i in range(2)]
                  for l in range(2)]

        stream0 = [(0, 0, kvw[0], rows(w_mem_kv[0], 0, 512)),
                   (1, 0, vw0, rows(win0, 2 * MIX, 3 * MIX)),
                   (2, 0, mqw0, rows(win0, 3 * MIX, 3 * MIX + 256))]
        for p in range(NPAIR):
            for t in range(2):
                stream0.append((3 + p // 2, 0, qkw[p][t], rows(win0, t * MIX + p * P, t * MIX + p * P + P)))
        stream0 += [(0, 1, wow[0][0], wo_src[0][0]), (1, 3, wow[0][1], wo_src[0][1])]
        B1 = PRE0 + NQ * FILLS
        stream1 = [(2, B1 - 5, kvw[1], rows(w_mem_kv[1], 0, 512)),
                   (3, B1 - 4, rw1, rows(win1, 3 * MIX, 3 * MIX + 288)),
                   (5, B1 - 2, qkw1, rows(win1, 0, MIX)),
                   (2, B1 + 1, vgw1, rows(win1, MIX, 3 * MIX)),
                   (3, B1 + 2, wow[1][0], wo_src[1][0]),
                   (4, B1 + 3, wow[1][1], wo_src[1][1])]

        count = [0] * SLOTS
        arrive0, arrive1 = [], []
        for slot, _, _, _ in stream0:
            count[slot] += 16
            arrive0.append((ring_in[slot], count[slot]))
        base0 = list(count)
        for s in range(SLOTS):
            count[s] += 16 * NQ * (FILLS // SLOTS)
        for slot, _, _, _ in stream1:
            count[slot] += 16
            arrive1.append((ring_in[slot], count[slot]))
        base1 = list(count)
        first, more = Quads("first"), Quads("more")

        class Run:

            def __init__(self, sig, slot0, ring_in, ring_used, in_base, used_base):
                self.sig, self.slot0, self.ring_in, self.ring_used = sig, slot0, ring_in, ring_used
                self.in_base, self.used_base = in_base, used_base

        main = [Run(first, PRE0 % SLOTS, ring_in, ring_used, base0, PRE0),
                Run(first, PRE1 % SLOTS, ring_in, ring_used, base1, PRE1)]
        more_in, more_used = [sem(f"more_in{i}") for i in range(SLOTS)], sem("more_used")
        extra = Run(more, 0, more_in, more_used, [0] * SLOTS, SLOTS)

        w1v = [moe_w1[l].rearrange("e (p k) f -> p e (k f)", k=KC) for l in range(2)]
        w3v = [moe_w3[l].rearrange("e (p k) f -> p e (k f)", k=KC) for l in range(2)]
        w2v = [moe_w2[l].rearrange("e (j p) n -> j p e n", p=P) for l in range(2)]

        def rounds(eng, l):
            hi = eng.value_load(nround[0:1, l:l + 1], min_val=0, max_val=(l + 1) * (T // CAP - 1))
            return (eng.value_load(nround[0:1, 0:1], min_val=0, max_val=T // CAP - 1) if l else 0), hi

        block = ctx.enter_context(nc.Block())

        @block.sync
        def _(sp):
            sp.dma_start(xres[:], x[0].rearrange("(a p) d -> p a d", p=P)).then_inc(s_x, 16)

            def fill(stream):
                for slot, need, dst, src in stream:
                    if need:
                        sp.wait_ge(ring_used, need)
                    sp.dma_start(dst, src).then_inc(ring_in[slot], 16)

            def quad_fills(rn, l, q, g):
                for f in range(FILLS):
                    slot = (rn.slot0 + f) % SLOTS
                    sp.wait_ge(rn.ring_used, q * FILLS + (rn.used_base + f - SLOTS + 1))
                    dst = ring[:, slot * SLOT:(slot + 1) * SLOT].rearrange("p (e n) -> p e n", e=E4)
                    w = (w1v, w3v)[f // 4][l] if f < 8 else None
                    if f < 8:
                        src = w[:, bass.ds(g * E4, E4), (f % 4) * 1024:(f % 4) * 1024 + 1024]
                    else:
                        src = w2v[l][f - 8][:, bass.ds(g * E4, E4), :]
                    sp.dma_start(dst, src).then_inc(rn.ring_in[slot], 16)

            def experts(l):
                with sp.Fori(0, NQ) as g:
                    quad_fills(main[l], l, g, g)
                sp.wait_ge(rt_n[l], 1)
                lo, hi = rounds(sp, l)
                with sp.If(hi > lo):
                    sp.wait_ge(ring_used, main[l].used_base + NQ * FILLS)
                    with sp.Fori(lo, hi) as r:
                        with sp.Fori(0, NQ) as g:
                            quad_fills(extra, l, r * NQ + g, g)
                    sp.wait_ge(moe_done[l], 1)
                    sp.sem_inc(sp_spare, 1)

            sp.sem_inc(more_used, SLOTS)
            fill(stream0)
            experts(0)
            fill(stream1)
            experts(1)
            sp.wait_ge(s_out, 32)

        
        @block.gpsimd
        def _(pool):
            nc.gpsimd.memset(gup[:], 0.0).then_inc(s_gup0, 1)
            pool.wait_ge(ring_in[1], 16)
            for r in range(2):
                for i in range(NA_DR):
                    src = bass.AP(tensor=na_rpb.tensor, offset=na_rpb.offset + (i + 5 - r) * RPB_W + 15 - (GRID - 1),
                                  ap=[[1, GRID], [RPB_H * RPB_W, 2 * NPAIR], [1, GRID]])
                    pool.dma_start(rpbraw[64 * r:64 * r + 64, :, i, :], src).then_inc(s_rpb, 16)
            pool.wait_ge(moe_done[0], 1)
            pool.wait_ge(ring_used, B1 + 1)
            kc = ks.rearrange("p d (n c) -> p d n c", c=CH)
            nc.gpsimd.memset(ks, 1.0).then_inc(resets, 1)
            pool.wait_ge(resets, 1)
            nc.gpsimd.memset(kc[:, 0, :, 0:1], 0.0).then_inc(resets, 1)
            nc.gpsimd.memset(kc[:, 1, :, CH - 1:CH], 0.0).then_inc(resets, 1)

        @block.tensor
        def _(pe):
            def arrived(a):
                pe.wait_ge(*a)

            def transpose_tile(i, src, a, bank):
                for k in range(KC):
                    t = pe.transpose(ps[:, bank + k // 4, (k % 4) * P:(k % 4) * P + P], src[:, a, k::KC], ident)
                t.then_inc(n_tr, 1)

            def transposes(i, src):
                for a in range(TT):
                    pe.wait_ge(n_xs, TT * i_xs[i] + a + 1)
                    transpose_tile(i, src, a, NBANK[i][a])

            def mem_kv(l):
                w = kvw[l]
                arrived((arrive0, arrive1)[l][0])
                for m in range(MPAIR):
                    for k in range(KC):
                        t = pe.matmul(ps[:, KVB[l], m * T:(m + 1) * T], w[:, k, m * P:(m + 1) * P], memT[:, k, :],
                                      start=k == 0, stop=k == KC - 1)
                t.then_inc(kv_mm[l], 1)
                for a in range(TT):
                    for k in range(KC):
                        t = pe.matmul(ps[:, KVB[l] + 1, a * 256:a * 256 + 256], memT[:, k, a * P:(a + 1) * P], w[:, k, 256:512],
                                      start=k == 0, stop=k == KC - 1)
                t.then_inc(ring_used, 1)

            def token_rows(w, n0, a, half, bank):
                for k in range(KC):
                    t = pe.matmul(ps[:, bank, 0:384], hT[:, k, a * P:(a + 1) * P],
                                  w[:, k, n0 + 384 * half:n0 + 384 * half + 384], start=k == 0, stop=k == KC - 1)
                return t

            def scores(l, p, q_of, k_of):
                for a in range(TT):
                    for h in range(2):
                        r = slice(64 * h, 64 * h + 64)
                        t = pe.matmul(ps[:, 2 + h, a * T:(a + 1) * T], q_of[r, a * P:(a + 1) * P], k_of[r, :],
                                      start=True, stop=True)
                t.then_inc(at_sc, 1)

            def weighted(l, p, prob, pT, v_of, n):
                pe.wait_ge(at_p, n + 1)
                for h in range(2):
                    for a in range(TT):
                        for kt in range(TT):
                            t = pe.transpose(ps[:, 4 + h, kt * T + a * P:kt * T + a * P + P],
                                             prob[:, h, a, kt * P:(kt + 1) * P], ident)
                t.then_inc(at_tr, 1)
                pe.wait_ge(at_pT, n + 1)
                for h in range(2):
                    for kt in range(TT):
                        t = pe.matmul(ps[64 * h:64 * h + 64, 6, 0:T], v_of(h, kt), pT[:, h, kt, :],
                                      start=kt == 0, stop=kt == TT - 1)
                t.then_inc(at_o, 1)

            def out_proj(l, a, chunks, last):
                for c in chunks:
                    for half in range(2):
                        t = pe.matmul(ps[:, WOB[l][a] + half, :], mixT[:, c, a * P:(a + 1) * P],
                                      wow[l][c // 4][:, c % 4, 512 * half:512 * half + 512],
                                      start=c == 6, stop=c == last)
                return t

            def route(l):
                rb = RTB[l]
                pe.wait_ge(s_small, SMALL)
                for a in range(TT):
                    pe.wait_ge(n_hT, TT * (2 * l + 2) + a + 1)
                    for k in range(KC):
                        t = pe.matmul(ps[:, rb, a * 64:a * 64 + NG + NE], hT[:, k, a * P:(a + 1) * P], wlog[:, l, k, :],
                                      start=k == 0, stop=k == KC - 1)
                t.then_inc(rt_mm[l], 1)
                pe.wait_ge(rt_m[l], 1)
                pe.matmul(ps[:, rb + 1, 0:NE], tri, msk[:, 0, :], start=True, stop=True)
                pe.matmul(ps[:, rb + 1, NE:2 * NE], ones, msk[:, 0, :], start=True, stop=False)
                pe.matmul(ps[:, rb + 1, NE:2 * NE], tri, msk[:, 1, :], start=False, stop=True)
                pe.matmul(ps[:, rb + 1, 2 * NE:3 * NE], ones, msk[:, 0, :], start=True, stop=False)
                pe.matmul(ps[:, rb + 1, 2 * NE:3 * NE], ones, msk[:, 1, :], start=False, stop=True).then_inc(rt_p[l], 1)

            def quad(rn, c, q, sel_count):
                pe.wait_ge(rn.sig.sel_ready, sel_count)
                for k in range(KC):
                    for a in range(TT):
                        t = pe.matmul(ps[:, k // 4, (k % 4) * P:(k % 4) * P + P], xs[:, a, k::KC],
                                      sel[:, a].rearrange("p e s -> p (e s)"), start=a == 0, stop=a == TT - 1)
                t.then_inc(rn.sig.gathered, 1)
                pe.wait_ge(rn.sig.sel_ready, sel_count + 1)
                for a in range(TT):
                    t = pe.transpose(ps[:, 2, a * P:(a + 1) * P], selw[:, a].rearrange("p e s -> p (e s)"), ident)
                t.then_inc(rn.sig.selT_mm, 1)
                pe.wait_ge(rn.sig.xsel_ready, c * 2 + 2)
                for f in range(8):
                    slot = (rn.slot0 + f) % SLOTS
                    pe.wait_ge(rn.ring_in[slot], (q * 2 + (f // SLOTS + 1)) * 16 + rn.in_base[slot])
                    for kk in range(2):
                        k = 2 * (f % 4) + kk
                        for e in range(E4):
                            o = slot * SLOT + e * 1024 + kk * FF
                            t = pe.matmul(ps[32 * e:32 * e + 32, 4 + f // 4, :], xsel[:, k, 32 * e:32 * e + 32],
                                          ring[:, o:o + FF], start=k == 0, stop=k == KC - 1, tile_position=(0, 32 * e))
                    t.then_inc(rn.ring_used, 1)
                pe.wait_ge(rn.sig.act_ready, c + 1)
                for j in range(4):
                    t = pe.transpose(ps[:, 3, j * P:(j + 1) * P], act[:, j * P:(j + 1) * P], ident)
                t.then_inc(rn.sig.actT_mm, 1)
                pe.wait_ge(rn.sig.actT_ready, c + 1)
                for j in range(4):
                    f = 8 + j
                    slot = (rn.slot0 + f) % SLOTS
                    pe.wait_ge(rn.ring_in[slot], (q * 2 + (f // SLOTS + 1)) * 16 + rn.in_base[slot])
                    for half in range(2):
                        for e in range(E4):
                            o = slot * SLOT + e * D + half * 512
                            t = pe.matmul(ps[32 * e:32 * e + 32, 6 + half, :], actT[:, j, 32 * e:32 * e + 32],
                                          ring[:, o:o + 512], start=j == 0, stop=j == 3, tile_position=(0, 32 * e))
                    t.then_inc(rn.ring_used, 1)
                pe.wait_ge(rn.sig.selwT_ready, c + 1)
                pe.wait_ge(rn.sig.yb_ready, c * 2 + 2)
                for a in range(TT):
                    for half in range(2):
                        t = pe.matmul(ps[:, 4 + 2 * a + half, :], selwT[:, a, :], yb[:, half * 512:half * 512 + 512],
                                      start=True, stop=True)
                t.then_inc(rn.sig.scattered, 1)

            def experts(l):
                with pe.Fori(0, NQ) as q:
                    quad(main[l], q + l * NQ, q, q * 2 + (l * SELS + 1))
                pe.wait_ge(rt_n[l], 1)
                lo, hi = rounds(pe, l)
                with pe.If(hi > lo):
                    with pe.Fori(lo, hi) as r:
                        with pe.Fori(0, NQ) as g:
                            quad(extra, r * NQ + g, r * NQ + g, r * SELS + g * 2 + 1)

            def v_na(p):
                return lambda h, kt: v0[:, kt, p * P + 64 * h:p * P + 64 * h + 64]

            def v_mem(l, m):
                return lambda h, kt: vm[:, l, kt, m * P + 64 * h:m * P + 64 * h + 64]

            pe.wait_ge(s_cst, 16)
            transposes(0, mixT_as_tokens)
            transposes(1, xs)
            pe.wait_ge(n_hT, TT)
            mem_kv(0)
            pe.wait_ge(n_hT, TT * 2)
            arrived(arrive0[2])
            for m in range(MPAIR):
                for k in range(KC):
                    t = pe.matmul(ps[:, 2, m * T:(m + 1) * T], mqw0[:, k, m * P:(m + 1) * P], hT[:, k, :],
                                  start=k == 0, stop=k == KC - 1)
            t.then_inc(mq_mm, 1)
            pe.wait_ge(mq_cp[0], 1)
            pe.wait_ge(kv_cp[0], 2)
            scores(0, 0, mqT0[:, 0, :], kTm[:, 0, 0, :])
            arrived(arrive0[1])
            for m in range(MPAIR):
                if m == 1:
                    pe.wait_ge(v_cp[0], 1)
                token_rows(vw0, 0, m, 0, 0)
                t = token_rows(vw0, 0, m, 1, 1)
                t.then_inc((v_mm[0], ring_used)[m], m + 1)
                if m == 1:
                    pe.wait_ge(at_oT, 1)
                weighted(0, m, prob0, pT0, v_mem(0, m), m)
                if m == 0:
                    scores(0, 1, mqT0[:, 1, :], kTm[:, 0, 1, :])
            pe.wait_ge(s_rpb, 16 * 2 * NA_DR)
            pe.wait_ge(at_oT, 2)
            for c in range(RPC):
                if c >= 2:
                    pe.wait_ge(s_mask, c - 1)
                pe.matmul(ps[:, 6 + c % 2, :], cst[:, C_FLIP:C_FLIP + P],
                          rpbraw.rearrange("p h i c -> p (h i c)")[:, c * 512:(c + 1) * 512],
                          start=True, stop=True).then_inc(rp_mm, 1)
            pe.wait_ge(v_cp[0], TT)
            for p in range(NPAIR):
                n = MPAIR + p
                if p % 2 == 0:
                    arrived(arrive0[3 + 2 * p + 3])
                if p >= 2:
                    pe.wait_ge(qk_cp, p - 1)
                for t_ in range(2):
                    for k in range(KC):
                        t = pe.matmul(ps[:, p % 2, t_ * T:(t_ + 1) * T], qkw[p][t_][:, k, :], hT[:, k, :],
                                      start=k == 0, stop=k == KC - 1)
                t.then_inc(qk_mm if p % 2 == 0 else ring_used, 1)
                if p >= 1:
                    if p >= 2:
                        pe.wait_ge(at_oT, n - 1)
                    else:
                        pe.wait_ge(s_mask, RPC)
                    weighted(0, n - 1, prob0, pT0, v_na(p - 1), n - 1)
                pe.wait_ge(qk_cp, p + 1)
                scores(0, n, qk[:, p % 2, 0, :], qk[:, p % 2, 1, :])
            arrived(arrive0[15])
            arrived(arrive0[16])
            pe.wait_ge(at_oT, N1 - 1)
            out_proj(0, 0, (6, 7, 0, 1, 2, 3, 4), 5)
            weighted(0, N1 - 1, prob0, pT0, v_na(NPAIR - 1), N1 - 1)
            pe.wait_ge(at_oT, N1)
            out_proj(0, 0, (5,), 5).then_inc(wo_mm, 1)
            out_proj(0, 1, (6, 7, 0, 1, 2), 5)
            pe.wait_ge(res[0], 1)
            transpose_tile(2, xres, 0, NBANK[2][0])
            out_proj(0, 1, (3, 4, 5), 5).then_inc(ring_used, 2)
            pe.wait_ge(res[0], 2)
            transpose_tile(2, xres, 1, NBANK[2][1])
            route(0)
            experts(0)

            pe.wait_ge(moe_done[0], 1)
            mem_kv(1)
            transposes(3, xs)
            pe.wait_ge(n_hT, TT * 4)
            arrived(arrive1[1])
            for k in range(KC):
                t = pe.matmul(ps[0:32, 4, 0:T], rw1[:, k, 0:32], hT[:, k, :], start=k == 0, stop=k == KC - 1)
            t.then_inc(r_mm, 1)
            for m in range(MPAIR):
                for k in range(KC):
                    t = pe.matmul(ps[:, 5, m * T:(m + 1) * T], rw1[:, k, 32 + m * P:32 + (m + 1) * P], hT[:, k, :],
                                  start=k == 0, stop=k == KC - 1)
            t.then_inc(ring_used, 1)
            pe.wait_ge(r_cp, 1)
            for d in range(2):
                for h in range(HG):
                    t = pe.matmul(ps[0:DK, 2 * d + h // 2, (h % 2) * T:(h % 2) * T + T],
                                  gup[:, d, h * DK:(h + 1) * DK], rT, start=True, stop=True)
            t.then_inc(z_mm, 1)
            arrived(arrive1[2])
            pe.wait_ge(mq_cp[1], 1)
            pe.wait_ge(kv_cp[1], 2)
            for h in range(HG):
                for t_ in range(2):
                    for k in range(KC):
                        t = pe.matmul(ps[0:DK, 4 + h, t_ * T:(t_ + 1) * T],
                                      qkw1[:, k, t_ * 384 + h * DK:t_ * 384 + (h + 1) * DK], hT[:, k, :],
                                      start=k == 0, stop=k == KC - 1)
                if h < HG - 1:
                    t.then_inc(gq_mm, 1)
            t.then_inc(ring_used, 2)
            pe.wait_ge(z_sb, 2)
            scores(1, N1, mqT1[:, 0, :], kTm[:, 1, 0, :])
            arrived(arrive1[3])
            for i in range(2 * TT):
                if i >= 2:
                    pe.wait_ge(v_cp[1], i - 1)
                token_rows(vgw1, 0, i // 2, i % 2, i % 2).then_inc(v_mm[1], 1)
            pe.wait_ge(gq_cp, 2 * HG)
            weighted(1, N1, prob1, pT1, v_mem(1, 0), N1)
            scores(1, N1 + 1, mqT1[:, 1, :], kTm[:, 1, 1, :])
            pe.wait_ge(k_st, 2)
            pe.wait_ge(v_cp[1], 2 * TT)
            pe.wait_ge(at_oT, N1 + 1)
            for d in range(2):
                for a in range(TT):
                    for h in range(HG):
                        t = pe.transpose(ps[:, KSTB[2 * d + a], h * DK:(h + 1) * DK],
                                         ks[:, d, h * T + a * P:h * T + a * P + P], ident[0:DK, 0:DK])
                    t.then_inc(kst_mm, 1)

            def out_gate(i):
                if i >= 2:
                    pe.wait_ge(g_cp, i - 1)
                t = token_rows(vgw1, MIX, i // 2, i % 2, i % 2)
                if i == 3:
                    t.then_inc(ring_used, 3)
                else:
                    t.then_inc(g_mm, 1)

            def update(i):
                step, d = i // 2, i % 2
                n = step if d == 0 else NCH - 1 - step
                if i >= 2:
                    pe.wait_ge(u_st, i - 1)
                r = (n % 2) * 64
                for h in range(HG):
                    t = pe.matmul(ps[0:DK, 4 + 2 * d + h // 2, (h % 2) * DV:(h % 2 + 1) * DV],
                                  ksT[r:r + 64, d, n // 2, h, :], v1[r:r + 64, n // 2, h * DV:(h + 1) * DV],
                                  start=True, stop=True)
                t.then_inc(u_mm, 1)

            pe.wait_ge(kst_cp, 4)
            out_gate(0)
            weighted(1, N1 + 1, prob1, pT1, v_mem(1, 1), N1 + 1)
            pe.wait_ge(q_in, 2)
            pe.wait_ge(k_in, 2)
            for d in range(2):
                for h in range(HG):
                    for n in range(NCH):
                        c = slice(h * T + n * CH, h * T + (n + 1) * CH)
                        r = (n % 2) * 64
                        t = pe.matmul(ps[r:r + 64, 2 + d, (h * TT + n // 2) * CH:(h * TT + n // 2 + 1) * CH],
                                      ki[:, d, c], qi[:, d, c], start=True, stop=True)
                t.then_inc(a_mm, 1)
            pe.wait_ge(at_oT, N1 + 2)
            update(0)
            update(1)
            out_gate(1)
            update(2)
            update(3)
            out_gate(2)
            update(4)
            update(5)
            out_gate(3)
            pe.wait_ge(a_cp, 1)
            pe.wait_ge(q_st, 2)
            pe.wait_ge(u_st, 6)
            pe.wait_ge(g_cp, 4)
            for a in range(TT):
                for h in range(HG):
                    for half in range(2):
                        n = 2 * a + half
                        r = 64 * half
                        o = ps[r:r + 64, OB[a] + h // 2, (h % 2) * DV:(h % 2 + 1) * DV]
                        c = slice(h * T + n * CH, h * T + (n + 1) * CH)
                        inter = ([(0, n - 1)] if n > 0 else []) + ([(1, NCH - 2 - n)] if n < NCH - 1 else [])
                        pe.matmul(o, asum[r:r + 64, h, a, :], v1[r:r + 64, a, h * DV:(h + 1) * DV],
                                  start=True, stop=False)
                        for j, (d, s_) in enumerate(inter):
                            t = pe.matmul(o, qs[:, d, c], state[:, d, s_, h, :], start=False, stop=j == len(inter) - 1)
                t.then_inc(o_mm, 1)
            for a in range(TT):
                pe.wait_ge(o_mix, a + 1)
                for c in range(6):
                    t = pe.transpose(ps[:, (6, 0)[a] + c // 4, (c % 4) * P:(c % 4) * P + P], g1[:, a, c * P:(c + 1) * P],
                                     ident)
                t.then_inc(m_tr, 1)
                pe.wait_ge(m_cp, 2 * a + 2)
                if a == 0:
                    arrived(arrive1[4])
                    arrived(arrive1[5])
                    out_proj(1, 0, (6, 7, 0, 1, 2, 3, 4, 5), 5).then_inc(wo_mm, 1)
            out_proj(1, 1, (6, 7, 0, 1, 2), 5)
            pe.wait_ge(res[1], 1)
            transpose_tile(4, xres, 0, NBANK[4][0])
            out_proj(1, 1, (3, 4, 5), 5).then_inc(ring_used, 2)
            pe.wait_ge(res[1], 2)
            transpose_tile(4, xres, 1, NBANK[4][1])
            route(1)
            experts(1)

        @block.scalar
        def _(act_e):
            act_e.dma_start(cst[:], consts).then_inc(s_cst, 16)
            act_e.dma_start(mixT_as_tokens, mem[0].rearrange("(a p) d -> p a d", p=P)).then_inc(s_mem, 16)
            gains = [(gcol[:, 0, :], mem_norm.rearrange("(p k) -> p k", k=KC))]
            small = []
            for l in range(2):
                gains += [(gcol[:, 1 + 2 * l, :], norm_mix[l].rearrange("(p k) -> p k", k=KC)),
                          (gcol[:, 2 + 2 * l, :], norm_ffn[l].rearrange("(p k) -> p k", k=KC))]
                small += [(wlog[:, l, :, 0:NG], moe_w_group[l].rearrange("(p k) n -> p k n", k=KC)),
                          (wlog[:, l, :, NG:NG + NE], moe_w_router[l].rearrange("(p k) n -> p k n", k=KC)),
                          (rbias[:, l, 0:NG], moe_b_group[l:l + 1, :].to_broadcast([P, NG])),
                          (rbias[:, l, NG:NG + NE], moe_b_router[l:l + 1, :].to_broadcast([P, NE]))]
            small += [(gnorm[:], gla_out_norm[0:1, :].to_broadcast([P, DV]))]
            for d in range(2):
                small += [(gup[16 * d:16 * d + 16, d, :], gla_gate_up[0, d])]
            assert SMALL == 16 * (len(small) + 2)
            for dst, src in gains:
                act_e.dma_start(dst, src).then_inc(s_gain, 16)
            act_e.wait_ge(s_gup0, 1)
            for dst, src in small:
                act_e.dma_start(dst, src).then_inc(s_small, 16)
            with nc.allow_non_contiguous_dma(reason="768 gate biases, feature on the partition"):
                for d in range(2):
                    act_e.dma_start(gbias[:, d, :], gla_gate_bias[0, d].rearrange("(h p) -> p h", p=DK)).then_inc(s_small, 16)
            def norm(i):
                src = norm_src(i)
                for a in range(TT):
                    if i in (2, 4):
                        act_e.wait_ge(res[i // 2 - 1], a + 1)
                    nc.scalar.activation(xs[:, a, :], src[:, a, :], ACT.Square,
                                         accum_out=st[:, 2 * i + a:2 * i + a + 1]).then_inc(n_sq, 1)
                act_e.wait_ge(n_var, i + 1)
                nc.scalar.activation(st[:, 24 + 2 * i:26 + 2 * i], st[:, 12 + 2 * i:14 + 2 * i], ACT.Sqrt).then_inc(n_sd, 1)

            def copy_kv(l):
                act_e.wait_ge(kv_mm[l], 1)
                nc.scalar.copy(kTm[:, l].rearrange("p m t -> p (m t)"), ps[:, KVB[l], :]).then_inc(kv_cp[l], 1)
                act_e.wait_ge(ring_used, (1, B1 + 1)[l])
                nc.scalar.copy(vm[:, l].rearrange("p a n -> p (a n)"), ps[:, KVB[l] + 1, :]).then_inc(kv_cp[l], 1)

            def exps(l, n, prob, raw):
                act_e.wait_ge(at_mx, n + 1)
                for h in range(2):
                    for a in range(TT):
                        i = 2 * h + a
                        src = ps[:, 2 + h, a * T:(a + 1) * T] if raw else prob[:, h, a, :]
                        nc.scalar.activation(prob[:, h, a, :], src, ACT.Exp, bias=st[:, 40 + i:41 + i],
                                             scale=DH ** -0.5 if raw else 1.0,
                                             accum_out=st[:, 44 + i:45 + i]).then_inc(at_ex, 1)

            def copy_pT(l, n, pT):
                act_e.wait_ge(at_tr, n + 1)
                nc.scalar.copy(pT.rearrange("p h a k -> p (h a k)"),
                               ps[:, 4:6, :].rearrange("p b n -> p (b n)")).then_inc(at_pT, 1)

            def copy_o(l, n, c):
                act_e.wait_ge(at_o, n + 1)
                nc.scalar.copy(mixT[:, c, :], ps[:, 6, 0:T]).then_inc(at_oT, 1)

            def route(l):
                act_e.wait_ge(rt_d[l], 1)
                nc.scalar.activation(t4a, t4a, ACT.Exp).then_inc(rt_e[l], 1)
                act_e.wait_ge(rt_d[l], 2)
                nc.scalar.activation(sc[:, 6, :], sc[:, 5, :], ACT.Exp).then_inc(rt_e[l], 1)

            def quad(rn, c, q):
                act_e.wait_ge(rn.sig.selT_mm, c + 1)
                nc.scalar.copy(selwT.rearrange("p a t -> p (a t)"), ps[:, 2, 0:T]).then_inc(rn.sig.selwT_ready, 1)
                act_e.wait_ge(rn.ring_used, q * FILLS + (rn.used_base + 4))
                nc.scalar.activation(sg, ps[:, 4, :], ACT.Sigmoid).then_inc(rn.sig.exp_done, 1)
                act_e.wait_ge(rn.sig.actT_mm, c + 1)
                nc.scalar.copy(actT.rearrange("p j s -> p (j s)"), ps[:, 3, :]).then_inc(rn.sig.actT_ready, 1)
                act_e.wait_ge(rn.ring_used, q * FILLS + (rn.used_base + 12))
                for half in range(2):
                    nc.scalar.copy(yb[:, half * 512:half * 512 + 512], ps[:, 6 + half, :]).then_inc(rn.sig.yb_ready, 1)

            def experts(l):
                with act_e.Fori(0, NQ) as q:
                    quad(main[l], q + l * NQ, q)
                act_e.wait_ge(rt_n[l], 1)
                lo, hi = rounds(act_e, l)
                with act_e.If(hi > lo):
                    with act_e.Fori(lo, hi) as r:
                        with act_e.Fori(0, NQ) as g:
                            quad(extra, r * NQ + g, r * NQ + g)

            act_e.wait_ge(s_mem, 16)
            norm(0)
            act_e.wait_ge(s_x, 16)
            norm(1)
            copy_kv(0)
            act_e.wait_ge(mq_mm, 1)
            nc.scalar.copy(mqT0.rearrange("p m t -> p (m t)"), ps[:, 2, :]).then_inc(mq_cp[0], 1)
            for m in range(MPAIR):
                exps(0, m, prob0, True)
                if m == 0:
                    act_e.wait_ge(v_mm[0], 1)
                else:
                    act_e.wait_ge(ring_used, 3)
                nc.scalar.copy(v0[:, m, :].rearrange("p (b n) -> p b n", b=2), ps[:, 0:2, 0:384]).then_inc(v_cp[0], 1)
                copy_pT(0, m, pT0)
                copy_o(0, m, 6 + m)
            for p in range(NPAIR):
                n = MPAIR + p
                if p % 2 == 0:
                    act_e.wait_ge(qk_mm, p // 2 + 1)
                else:
                    act_e.wait_ge(ring_used, 3 + (p + 1) // 2)
                nc.scalar.copy(qk[:, p % 2].rearrange("p q t -> p (q t)"), ps[:, p % 2, :]).then_inc(qk_cp, 1)
                if p >= 1:
                    copy_pT(0, n - 1, pT0)
                    copy_o(0, n - 1, p - 1)
                exps(0, n, prob0, False)
            copy_pT(0, N1 - 1, pT0)
            copy_o(0, N1 - 1, NPAIR - 1)
            norm(2)
            route(0)
            experts(0)

            act_e.wait_ge(moe_done[0], 1)
            norm(3)
            copy_kv(1)
            act_e.wait_ge(r_mm, 1)
            nc.scalar.copy(rT, ps[0:32, 4, 0:T]).then_inc(r_cp, 1)
            act_e.wait_ge(ring_used, B1 + 2)
            nc.scalar.copy(mqT1.rearrange("p m t -> p (m t)"), ps[:, 5, :]).then_inc(mq_cp[1], 1)
            act_e.wait_ge(l_na, 1)
            nc.scalar.activation(ki, ki, ACT.Exp).then_inc(l_ex, 1)
            act_e.wait_ge(l_ex, 1)
            nc.scalar.activation(ki, ki, ACT.Ln, bias=1.0).then_inc(l_ln, 1)

            def copy_qk(h):
                if h < HG - 1:
                    act_e.wait_ge(gq_mm, h + 1)
                else:
                    act_e.wait_ge(ring_used, B1 + 4)
                nc.scalar.mul(qT[:, h, :], ps[0:DK, 4 + h, 0:T], DK ** -0.5).then_inc(gq_cp, 1)
                nc.scalar.copy(kT[:, h, :], ps[0:DK, 4 + h, T:2 * T]).then_inc(gq_cp, 1)

            copy_qk(0)
            copy_qk(1)
            act_e.wait_ge(d_b, 2)
            nc.scalar.activation(qs, bcum, ACT.Exp, scale=1 / 16).then_inc(e_done, 1)
            act_e.wait_ge(d_mid, 2)
            nc.scalar.activation(ki, qi, ACT.Exp, scale=-1 / 16).then_inc(e_done, 1)
            act_e.wait_ge(e_done, 2)
            nc.scalar.activation(qi, qi, ACT.Exp, scale=1 / 16).then_inc(e_done, 1)
            act_e.wait_ge(d_last, 2)
            nc.scalar.activation(ks, ks, ACT.Exp, scale=1 / 16).then_inc(e_done, 1)
            copy_qk(2)
            copy_qk(3)
            for i in range(2 * TT):
                act_e.wait_ge(v_mm[1], i + 1)
                nc.scalar.copy(v1[:, i // 2, (i % 2) * 384:(i % 2) * 384 + 384], ps[:, i % 2, 0:384]).then_inc(v_cp[1], 1)
            exps(1, N1, prob1, True)
            copy_pT(1, N1, pT1)
            copy_o(1, N1, 6)
            exps(1, N1 + 1, prob1, True)
            for i in range(4):
                act_e.wait_ge(kst_mm, i + 1)
                nc.scalar.copy(ksT[:, i // 2, i % 2].rearrange("p h c -> p (h c)"),
                               ps[:, KSTB[i], 0:HG * DK]).then_inc(kst_cp, 1)

            def copy_gate(i):
                if i < 3:
                    act_e.wait_ge(g_mm, i + 1)
                else:
                    act_e.wait_ge(ring_used, B1 + 7)
                nc.scalar.copy(g1[:, i // 2, (i % 2) * 384:(i % 2) * 384 + 384], ps[:, i % 2, 0:384]).then_inc(g_cp, 1)

            copy_gate(0)
            copy_pT(1, N1 + 1, pT1)
            copy_o(1, N1 + 1, 7)
            copy_gate(1)
            act_e.wait_ge(g_cp, 2)
            nc.scalar.activation(sig1[:, 0, :], g1[:, 0, :], ACT.Sigmoid).then_inc(g_ex, 1)
            copy_gate(2)
            copy_gate(3)
            act_e.wait_ge(g_cp, 4)
            nc.scalar.activation(sig1[:, 1, :], g1[:, 1, :], ACT.Sigmoid).then_inc(g_ex, 1)
            for a in range(TT):
                act_e.wait_ge(o_mm, a + 1)
                for h in range(HG):
                    i = HG * a + h
                    nc.scalar.activation(sqj[:, i * DV:(i + 1) * DV], ps[:, OB[a] + h // 2, (h % 2) * DV:(h % 2 + 1) * DV],
                                         ACT.Square, accum_out=st[:, 64 + i:65 + i]).then_inc(o_sq, 1)
                act_e.wait_ge(o_var, a + 1)
                nc.scalar.activation(st[:, 80 + HG * a:84 + HG * a], st[:, 72 + HG * a:76 + HG * a], ACT.Sqrt).then_inc(o_sd, 1)
            for a in range(TT):
                act_e.wait_ge(m_tr, a + 1)
                for b, n in ((0, 4), (1, 2)):
                    nc.scalar.copy(mixT[:, 4 * b:4 * b + n, a * P:(a + 1) * P],
                                   ps[:, (6, 0)[a] + b, 0:n * P].rearrange("p (c t) -> p c t", t=P)).then_inc(m_cp, 1)
            norm(4)
            route(1)
            experts(1)
            act_e.dma_start(fnorm, final_norm.rearrange("(o d) -> o d", o=1).to_broadcast([P, D])).then_inc(s_fn, 16)
            act_e.wait_ge(moe_done[1], 1)
            norm(5)
            for a in range(TT):
                act_e.wait_ge(fin_ready, a + 1)
                act_e.dma_start(out[0, a * P:(a + 1) * P, :], fin[:, a, :]).then_inc(s_out, 16)
            act_e.wait_ge(s_out, 32)

        @block.vector
        def _(dve):
            V = nc.vector
            cnt = [0]

            def link(ins):
                cnt[0] += 1
                ins.then_inc(dchain, 1)
                dve.wait_ge(dchain, cnt[0])

            def norm_scale(i):
                dve.wait_ge(n_sq, TT * (i + 1))
                V.tensor_scalar(st[:, 12 + 2 * i:14 + 2 * i], st[:, 2 * i:2 * i + 2], 1.0 / D, EPS, ALU.mult, ALU.add).then_inc(n_var, 1)
                dve.wait_ge(n_sd, i + 1)
                link(V.reciprocal(st[:, 48 + 2 * i:50 + 2 * i], st[:, 24 + 2 * i:26 + 2 * i]))
                return st[:, 48 + 2 * i:50 + 2 * i]

            def columns(i, a, hdst):
                dve.wait_ge(n_tr, TT * i + a + 1)
                b = NBANK[i][a]
                V.tensor_tensor(hdst[:, :, a * P:(a + 1) * P],
                                ps[:, b:b + 2, :].rearrange("p b (k t) -> p (b k) t", t=P),
                                gcol[:, i, :].unsqueeze(2).to_broadcast([P, KC, P]), ALU.mult).then_inc(n_hT, 1)

            def norm(i, dst, hdst):
                r = norm_scale(i)
                for a in range(TT):
                    V.tensor_scalar(dst[:, a, :], norm_src(i)[:, a, :], r[:, a:a + 1], None, ALU.mult).then_inc(n_xs, 1)
                if i == 0:
                    dve.wait_ge(s_gain, 16 * 5)
                for a in range(TT):
                    columns(i, a, hdst)

            def softmax_max(l, n, prob, raw):
                dve.wait_ge(at_sc, n + 1)
                if raw:
                    link(V.tensor_reduce(st[:, 36:40].rearrange("p (h a) -> p h a", h=2),
                                         ps[:, 2:4, :].rearrange("p h (a k) -> p h a k", a=TT), AX_X, ALU.max))
                    V.tensor_scalar(st[:, 40:44], st[:, 36:40], -DH ** -0.5, None, ALU.mult).then_inc(at_mx, 1)
                    return
                for h in range(2):
                    for a in range(TT):
                        bias = rpbt[:, 2 * (n - MPAIR) + h, 2 - 2 * a:6 - 2 * a, :].rearrange("p r c -> p (r c)")
                        link(V.scalar_tensor_tensor(prob[:, h, a, :], ps[:, 2 + h, a * T:(a + 1) * T], DH ** -0.5, bias,
                                                    ALU.mult, ALU.add))
                link(V.tensor_reduce(st[:, 36:40].rearrange("p (h a) -> p h a", h=2), prob, AX_X, ALU.max))
                V.tensor_scalar(st[:, 40:44], st[:, 36:40], -1.0, None, ALU.mult).then_inc(at_mx, 1)

            def softmax_div(l, n, prob):
                dve.wait_ge(at_ex, 4 * (n + 1))
                link(V.reciprocal(st[:, 60:64], st[:, 44:48]))
                V.tensor_tensor(prob.rearrange("p h a k -> p (h a) k"), prob.rearrange("p h a k -> p (h a) k"),
                                st[:, 60:64].unsqueeze(2).to_broadcast([P, 4, T]), ALU.mult).then_inc(at_p, 1)

            def add_mixed(l):
                i = 2 * l + 2
                for a in range(TT):
                    if a == 0:
                        dve.wait_ge(wo_mm, l + 1)
                    else:
                        dve.wait_ge(ring_used, (PRE0, B1 + 9)[l])
                    V.tensor_tensor(xres[:, a, :], xres[:, a, :],
                                    ps[:, WOB[l][a]:WOB[l][a] + 2, :].rearrange("p b n -> p (b n)"),
                                    ALU.add).then_inc(res[l], 1)
                    if a == 0:
                        columns(i, 0, hT)
                columns(i, 1, hT)

            def one_hot(dst, vals, top, n, tmp):
                link(V.tensor_tensor(tmp, vals, top.unsqueeze(2).to_broadcast([P, TT, n]), ALU.is_equal))
                im = iotam[:, 0:n].unsqueeze(1).to_broadcast([P, TT, n])
                link(V.tensor_tensor(tmp, tmp, im, ALU.mult))
                link(V.tensor_reduce(sc[:, 15, :], tmp, AX_X, ALU.min))
                link(V.tensor_tensor(dst, im, sc[:, 15, :].unsqueeze(2).to_broadcast([P, TT, n]), ALU.is_equal))

            def route(l):
                i = 2 * l + 2
                rms = norm_scale(i)
                if l == 0:
                    dve.wait_ge(s_small, SMALL)
                dve.wait_ge(rt_mm[l], 1)
                for a in range(TT):
                    link(V.scalar_tensor_tensor(lg[:, a, :], ps[:, RTB[l], a * 64:a * 64 + NG + NE], rms[:, a:a + 1],
                                                rbias[:, l, :], ALU.mult, ALU.add))
                lgg, lge = lg[:, :, 0:NG], lg[:, :, NG:NG + NE]
                link(V.tensor_reduce(sc[:, 0, :], lgg, AX_X, ALU.max))
                V.tensor_tensor(t4a, lgg, sc[:, 0, :].unsqueeze(2).to_broadcast([P, TT, NG]), ALU.subtract).then_inc(rt_d[l], 1)
                one_hot(goh, lgg, sc[:, 0, :], NG, gpen)
                link(V.tensor_scalar(gpen, goh, BIG, -BIG, ALU.mult, ALU.add))
                for a in range(TT):
                    for src, dst, by, op in ((lge, me, goh, ALU.mult), (me, me, gpen, ALU.add)):
                        link(V.tensor_tensor(dst[:, a, :].rearrange("p (g e) -> p g e", g=NG),
                                             src[:, a, :].rearrange("p (g e) -> p g e", g=NG),
                                             by[:, a, :].unsqueeze(2).to_broadcast([P, NG, EG]), op))
                link(V.tensor_reduce(sc[:, 3, :], me, AX_X, ALU.max))
                one_hot(oh1, me, sc[:, 3, :], NE, t32a)
                link(V.scalar_tensor_tensor(t32b, oh1, -2 * BIG, me, ALU.mult, ALU.add))
                link(V.tensor_reduce(sc[:, 4, :], t32b, AX_X, ALU.max))
                V.tensor_tensor(sc[:, 5, :], sc[:, 4, :], sc[:, 3, :], ALU.subtract).then_inc(rt_d[l], 1)
                one_hot(oh2, t32b, sc[:, 4, :], NE, t32a)
                V.tensor_tensor(msk, oh1, oh2, ALU.add).then_inc(rt_m[l], 1)
                for a in range(TT):
                    link(V.tensor_scalar(xs[:, a, :], xres[:, a, :], rms[:, a:a + 1], None, ALU.mult))
                link(V.memset(ppos, 1000.0))
                link(V.tensor_scalar(t32a, msk, -1000.0, 1000.0, ALU.mult, ALU.add))
                dve.wait_ge(rt_p[l], 1)
                link(V.tensor_tensor(ppos[:, :, 0:NE], t32a,
                                     ps[:, RTB[l] + 1, 0:2 * NE].rearrange("p (a e) -> p a e", a=TT), ALU.add))
                link(V.tensor_reduce(ntmp[:, 0:1], ps[:, RTB[l] + 1, 2 * NE:3 * NE], AX_X, ALU.max))

            def gates(l):
                dve.wait_ge(rt_e[l], 2)
                link(V.tensor_reduce(sc[:, 1, :], t4a, AX_X, ALU.add))
                link(V.tensor_scalar(sc[:, 7, :], sc[:, 6, :], 1.0, None, ALU.add))
                link(V.tensor_tensor(sc[:, 8, :], sc[:, 7, :], sc[:, 1, :], ALU.mult))
                link(V.reciprocal(sc[:, 9, :], sc[:, 8, :]))
                link(V.tensor_tensor(sc[:, 10, :], sc[:, 9, :], sc[:, 6, :], ALU.mult))
                link(V.memset(wtok, 0.0))
                link(V.tensor_tensor(t32a, oh1, sc[:, 9, :].unsqueeze(2).to_broadcast([P, TT, NE]), ALU.mult))
                link(V.tensor_tensor(t32b, oh2, sc[:, 10, :].unsqueeze(2).to_broadcast([P, TT, NE]), ALU.mult))
                link(V.tensor_tensor(wtok[:, :, 0:NE], t32a, t32b, ALU.add))

            def further_rounds(l):
                link(V.tensor_tensor(cmp8, ntmp[:, 0:1].to_broadcast([P, 8]), cst[:, C_THR:C_THR + 8], ALU.is_gt))
                link(V.tensor_reduce(ntmp[:, 1:2], cmp8, AX_X, ALU.add))
                if l == 0:
                    link(V.tensor_copy(roundf[:], ntmp[:, 1:2]))
                    V.tensor_copy(nround[:, 0:1], ntmp[:, 1:2]).then_inc(rt_n[l], 1)
                else:
                    V.tensor_tensor(nround[:, 1:2], roundf[:], ntmp[:, 1:2], ALU.add).then_inc(rt_n[l], 1)

            def select(rn, g):
                V.tensor_tensor(sel, iota.unsqueeze(1).unsqueeze(1).to_broadcast([P, TT, E4, CAP]),
                                ppos[:, :, bass.ds(g * E4, E4)].unsqueeze(3).to_broadcast([P, TT, E4, CAP]),
                                ALU.is_equal).then_inc(rn.sig.sel_ready, 1)

            def select_w(rn, g, count):
                dve.wait_ge(rn.sig.sel_ready, count)
                V.tensor_tensor(selw, sel, wtok[:, :, bass.ds(g * E4, E4)].unsqueeze(3).to_broadcast([P, TT, E4, CAP]),
                                ALU.mult).then_inc(rn.sig.sel_ready, 1)

            def quad(rn, l, c, q, g, sel_count):
                dve.wait_ge(rn.sig.gathered, c + 1)
                for b in range(2):
                    V.tensor_tensor(xsel[:, 4 * b:4 * b + 4, :], ps[:, b, :].rearrange("p (k t) -> p k t", t=P),
                                    gcol[:, 2 + 2 * l, 4 * b:4 * b + 4].unsqueeze(2).to_broadcast([P, 4, P]),
                                    ALU.mult).then_inc(rn.sig.xsel_ready, 1)
                select(rn, g + 1)
                dve.wait_ge(rn.sig.selT_mm, c + 1)
                select_w(rn, g + 1, sel_count + 1)
                dve.wait_ge(rn.sig.exp_done, c + 1)
                V.tensor_tensor(sg, sg, ps[:, 4, :], ALU.mult).then_inc(rn.sig.silu, 1)
                dve.wait_ge(rn.sig.silu, c + 1)
                dve.wait_ge(rn.ring_used, q * FILLS + (rn.used_base + 8))
                V.tensor_tensor(act, sg, ps[:, 5, :], ALU.mult).then_inc(rn.sig.act_ready, 1)
                dve.wait_ge(rn.sig.scattered, c + 1)
                for a in range(TT):
                    V.tensor_tensor(xres[:, a, :], xres[:, a, :], ps[:, 4 + 2 * a:6 + 2 * a, :].rearrange("p b n -> p (b n)"),
                                    ALU.add).then_inc(rn.sig.added, 1)
                dve.wait_ge(rn.sig.added, c * 2 + 2)

            def experts(l):
                select(main[l], 0)
                gates(l)
                select_w(main[l], 0, l * SELS + 1)
                further_rounds(l)
                with dve.Fori(0, NQ) as q:
                    quad(main[l], l, q + l * NQ, q, q, q * 2 + (l * SELS + 2))
                dve.wait_ge(rt_n[l], 1)
                lo, hi = rounds(dve, l)
                with dve.If(hi > lo):
                    with dve.Fori(lo, hi) as r:
                        V.tensor_scalar(ppos, ppos, -float(CAP), None, ALU.add).then_inc(next_round, 1)
                        dve.wait_ge(next_round, r + 1)
                        select(extra, 0)
                        select_w(extra, 0, r * SELS + 1)
                        with dve.Fori(0, NQ) as g:
                            quad(extra, l, r * NQ + g, r * NQ + g, g, r * SELS + g * 2 + 2)
                V.tensor_copy(ntmp[:, 0:1], xres[:, 0, 0:1]).then_inc(moe_done[l], 1)

            dve.wait_ge(s_mem, 16)
            dve.wait_ge(s_cst, 16)
            norm(0, mixT_as_tokens, memT)
            dve.wait_ge(s_x, 16)
            norm(1, xs, hT)
            for n in range(MPAIR):
                softmax_max(0, n, prob0, True)
                softmax_div(0, n, prob0)
            for c in range(RPC):
                dve.wait_ge(rp_mm, c + 1)
                V.tensor_tensor(rpbt.rearrange("p h i c -> p (h i) c")[:, 8 * c:8 * c + 8, :],
                                ps[:, 6 + c % 2, :].rearrange("p (i c) -> p i c", c=GRID),
                                cst[:, C_NAM:C_NAM + GRID].unsqueeze(1).to_broadcast([P, 8, GRID]),
                                ALU.add).then_inc(s_mask, 1)
            dve.wait_ge(s_mask, RPC)
            for n in range(MPAIR, N1):
                softmax_max(0, n, prob0, False)
                softmax_div(0, n, prob0)
            add_mixed(0)
            route(0)
            experts(0)

            dve.wait_ge(moe_done[0], 1)
            norm(3, xs, hT)
            dve.wait_ge(z_mm, 1)
            for d in range(2):
                V.tensor_tensor(qs[:, d].rearrange("p (h t) -> p h t", t=T),
                                ps[0:DK, 2 * d:2 * d + 2, :].rearrange("p b (h t) -> p (b h) t", t=T),
                                gbias[:, d, :].unsqueeze(2).to_broadcast([DK, HG, T]), ALU.add).then_inc(z_sb, 1)
            dve.wait_ge(z_sb, 2)
            V.scalar_tensor_tensor(ki, qs, -1.0, qs, ALU.mult, ALU.min).then_inc(l_na, 1)
            dve.wait_ge(l_ln, 1)
            link(V.scalar_tensor_tensor(qi, qs, 0.0, ki, ALU.min, ALU.subtract))
            dve.wait_ge(resets, 3)
            V.tensor_tensor_scan(bcum[:, 0], ks[:, 0], qi[:, 0], 0.0, ALU.mult, ALU.add).then_inc(d_b, 1)
            V.tensor_tensor_scan(bcum[:, 1][:, ::-1], ks[:, 1][:, ::-1], qi[:, 1][:, ::-1], 0.0, ALU.mult, ALU.add).then_inc(d_b, 1)
            dve.wait_ge(d_b, 2)

            def chunked(t, d):
                return t[:, d].rearrange("p (n c) -> p n c", c=CH)

            MID, LAST = (CH // 2 - 1, CH // 2), (CH - 1, 0)
            for d in range(2):
                b = chunked(bcum, d)
                V.tensor_tensor(chunked(qi, d), b, b[:, :, MID[d]:MID[d] + 1].to_broadcast([DK, HG * NCH, CH]),
                                ALU.subtract).then_inc(d_mid, 1)
            for d in range(2):
                b = chunked(bcum, d)
                V.tensor_tensor(chunked(ks, d), b[:, :, LAST[d]:LAST[d] + 1].to_broadcast([DK, HG * NCH, CH]), b,
                                ALU.subtract).then_inc(d_last, 1)
            dve.wait_ge(gq_cp, 2 * HG)
            for i, (e, by, s) in enumerate(((qs, qT, None), (ki, kT, k_in), (qi, qT, q_in), (ks, kT, k_st))):
                dve.wait_ge(e_done, i + 1)
                if i == 0:
                    for d in range(2):
                        link(V.tensor_copy(st_dec[:, d, :].unsqueeze(2), chunked(qs, d)[:, :, LAST[d]:LAST[d] + 1]))
                    s = q_st
                for d in range(2):
                    V.tensor_tensor(e[:, d], e[:, d], by.rearrange("p h t -> p (h t)"), ALU.mult).then_inc(s, 1)
            for m in range(MPAIR):
                softmax_max(1, N1 + m, prob1, True)
                softmax_div(1, N1 + m, prob1)
            for d in range(2):
                dve.wait_ge(a_mm, d + 1)
                link(V.tensor_tensor(amask[:, d].rearrange("p h a c -> p (h a) c"),
                                     ps[:, 2 + d, :].rearrange("p (h c) -> p h c", c=CH),
                                     cst[:, (C_MF, C_MB)[d]:(C_MF, C_MB)[d] + CH].unsqueeze(1).to_broadcast([P, HG * TT, CH]),
                                     ALU.mult))
            V.tensor_tensor(asum, amask[:, 0], amask[:, 1], ALU.add).then_inc(a_cp, 1)

            def new_state(i):
                step, d = i // 2, i % 2
                n = step if d == 0 else NCH - 1 - step
                dve.wait_ge(u_mm, i + 1)
                u = ps[0:DK, 4 + 2 * d:6 + 2 * d, 0:2 * DV].rearrange("p b (h v) -> p b h v", h=2)
                if step == 0:
                    V.tensor_copy(state[:, d, step].rearrange("p (b h) v -> p b h v", h=2), u).then_inc(u_st, 1)
                    return
                dve.wait_ge(u_st, i - 1)
                for h in range(HG):
                    ins = V.scalar_tensor_tensor(state[:, d, step, h, :], state[:, d, step - 1, h, :],
                                                 st_dec[:, d, h * NCH + n:h * NCH + n + 1], u[:, h // 2, h % 2, :],
                                                 ALU.mult, ALU.add)
                ins.then_inc(u_st, 1)

            def gate(a):
                dve.wait_ge(g_ex, a + 1)
                link(V.tensor_tensor(g1[:, a, :], g1[:, a, :], sig1[:, a, :], ALU.mult))
                link(V.tensor_tensor(g1[:, a, :].rearrange("p (h v) -> p h v", v=DV),
                                     g1[:, a, :].rearrange("p (h v) -> p h v", v=DV),
                                     gnorm[:].unsqueeze(1).to_broadcast([P, HG, DV]), ALU.mult))

            for i in range(4):
                new_state(i)
            gate(0)
            new_state(4)
            new_state(5)
            gate(1)
            for a in range(TT):
                dve.wait_ge(o_sq, HG * (a + 1))
                V.tensor_scalar(st[:, 72 + HG * a:76 + HG * a], st[:, 64 + HG * a:68 + HG * a], 1.0 / DV, EPS,
                                ALU.mult, ALU.add).then_inc(o_var, 1)
                dve.wait_ge(o_sd, a + 1)
                link(V.reciprocal(st[:, 88 + HG * a:92 + HG * a], st[:, 80 + HG * a:84 + HG * a]))
                o = ps[:, OB[a]:OB[a] + 2, 0:2 * DV].rearrange("p b (h v) -> p b h v", h=2)
                r = st[:, 88 + HG * a:88 + HG * a + HG].rearrange("p (b h) -> p b h", h=2)
                link(V.tensor_tensor(sig1[:, a].rearrange("p (b h v) -> p b h v", b=2, h=2), o,
                                     r.unsqueeze(3).to_broadcast([P, 2, 2, DV]), ALU.mult))
                V.tensor_tensor(g1[:, a, :], g1[:, a, :], sig1[:, a, :], ALU.mult).then_inc(o_mix, 1)
            add_mixed(1)
            route(1)
            experts(1)
            dve.wait_ge(moe_done[1], 1)
            dve.wait_ge(s_fn, 16)
            r = norm_scale(5)
            for a in range(TT):
                V.scalar_tensor_tensor(fin[:, a, :], xres[:, a, :], r[:, a:a + 1], fnorm, ALU.mult, ALU.mult).then_inc(fin_ready, 1)


def kernel(**inputs):
    import numpy as np
    import concourse.bacc as bacc
    from concourse.bass_utils import run_bass_kernel_spmd as run

    nc = bacc.Bacc("TRN2", target_bir_lowering=False, num_devices=1)
    arrays, args = {}, []
    data = dict(inputs)
    data["consts"] = make_consts()
    for name in NAMES:
        a = np.ascontiguousarray(data[name])
        arrays[f"in_{name}"] = a
        args.append(nc.dram_tensor(f"in_{name}", a.shape, mybir.dt.from_np(a.dtype), kind="ExternalInput").ap())
    o = nc.dram_tensor("out_0", (1, T, D), F32, kind="ExternalOutput").ap()
    build(nc, *args, o)
    r = run(nc, [arrays], core_ids=[0])
    return r.results[0]["out_0"]


NAMES = ["x", "mem", "mem_norm", "final_norm", "norm_mix", "norm_ffn", "w_mem_kv", "w_out", "na_w_in", "na_rpb",
         "gla_w_in", "gla_gate_up", "gla_gate_bias", "gla_out_norm", "moe_w_group", "moe_b_group", "moe_w_router",
         "moe_b_router", "moe_w1", "moe_w3", "moe_w2", "consts"]
```

```python
from contextlib import ExitStack

import concourse.bass as bass
from concourse import mybir

F32 = mybir.dt.float32
I32 = mybir.dt.int32
ALU = mybir.AluOpType
ACT = mybir.ActivationFunctionType
AX_X = mybir.AxisListType.X

P = 128
D = 1024
T = 256
TT = T // P
KC = D // P
EPS = 1e-6
GRID = 64
DH = 64
MIX = 768
NPAIR = 6
MPAIR = 2
RPB_H, RPB_W = 15, 31
NA_DR = 6
HG, DK, DV, CH = 4, 96, 192, 64
NCH = T // CH
NG, EG = 4, 8
NE = NG * EG
FF = 512
E4 = 4
CAP = 32
NQ = NE // E4
SELS = 2 * NQ + 2
FILLS = 12
SLOT = 4096
RSLOTS = 6
SLOTS = 8
PAIRS = NQ // 2
LAPS = 2 * FILLS // SLOTS
BIG = 1e30

C_ID, C_ONE, C_TRI, C_IOTA, C_IOTAM, C_THR, C_NAM, C_MF, C_MB = 0, 128, 256, 384, 416, 448, 456, 520, 584
C_END = 648
NBANK = {0: (0, 2), 1: (4, 6), 2: (4, 6), 3: (0, 2), 4: (6, 0)}
KVB, WOB, OB, KSTB, RTB = (0, 2), ((0, 2), (4, 2)), (2, 0), (0, 1, 7, 6), (0, 4)
XS_NTH = {0: 0, 1: 1, 3: 2}
N1 = NPAIR + MPAIR
SMALL = 16 * 16


def make_consts():
    import numpy as np

    c = np.zeros((P, C_END), np.float32)
    c[:, C_ID:C_ID + P] = np.eye(P)
    c[:, C_ONE:C_ONE + P] = 1.0
    c[:, C_TRI:C_TRI + P] = np.triu(np.ones((P, P)), 1)
    c[:, C_IOTA:C_IOTA + 32] = np.arange(32)
    c[:, C_IOTAM:C_IOTAM + 32] = np.arange(32) - 64
    c[:, C_THR:C_THR + 8] = CAP * (np.arange(8) + 1)
    col = GRID - 1 - np.arange(P) % GRID
    start = np.clip(col - 8, 0, GRID - 16)
    key = np.arange(GRID)
    inside = (key[None] >= start[:, None]) & (key[None] < start[:, None] + 16)
    c[:, C_NAM:C_NAM + GRID] = np.where(inside, 0.0, -BIG)
    j = np.arange(P) % CH
    i = np.arange(CH)
    c[:, C_MF:C_MF + CH] = i[None] >= j[:, None]
    c[:, C_MB:C_MB + CH] = i[None] <= j[:, None]
    return c


def build(nc, x, mem, mem_norm, final_norm, norm_mix, norm_ffn, w_mem_kv, w_out, na_w_in, na_rpb, gla_w_in,
          gla_gate_up, gla_gate_bias, gla_out_norm, moe_w_group, moe_b_group, moe_w_router, moe_b_router,
          moe_w1, moe_w3, moe_w2, consts, out):
    with ExitStack() as ctx:
        def sb(name, shape, dt=F32):
            return ctx.enter_context(nc.sbuf_tensor(name, shape, dt))

        def sem(name):
            return ctx.enter_context(nc.semaphore(name))

        ring = sb("ring", [P, RSLOTS * SLOT])
        cst = sb("cst", [P, C_END])
        gcol = sb("gcol", [P, 5, KC])
        wlog = sb("wlog", [P, 2, KC, NG + NE])
        rbias = sb("rbias", [P, 2, NG + NE])
        gnorm = sb("gnorm", [P, DV])
        gup = sb("gup", [32, 2, HG * DK])
        gbias = sb("gbias", [DK, 2, HG])
        xres = sb("xres", [P, TT, D])
        xs = sb("xs", [P, TT, D])
        hT = sb("hT", [P, KC, T])
        mixT = sb("mixT", [P, KC, T])
        kTm = sb("kTm", [P, 2, MPAIR, T])
        vm = sb("vm", [P, 2, TT, MPAIR * P])
        st = sb("st", [P, 96])
        scrap = sb("scrap", [P, 2])
        st_dec = sb("st_dec", [DK, 2, HG * NCH])
        nround = sb("nround", [P, 2], I32)
        roundf = sb("roundf", [P, 1])
        ARENA = 15360
        arena = sb("arena", [P, ARENA])

        def cut(off, *dims, parts=P):
            n = 1
            for v in dims:
                n *= v
            assert off + n <= ARENA
            v = arena[0:parts, off:off + n]
            if len(dims) == 1:
                return v
            names = "abcde"[:len(dims)]
            return v.rearrange(f"p ({' '.join(names)}) -> p {' '.join(names)}",
                               **{names[i]: dims[i] for i in range(1, len(dims))})

        ps = ctx.enter_context(nc.psum_tensor("ps", [P, 8, 512], F32))

        ident = cst[:, C_ID:C_ID + P]
        ones = cst[:, C_ONE:C_ONE + P]
        tri = cst[:, C_TRI:C_TRI + P]
        iota = cst[:, C_IOTA:C_IOTA + 32]
        iotam = cst[:, C_IOTAM:C_IOTAM + 32]

        rpbt = cut(0, 2 * NPAIR, NA_DR, GRID)
        v0 = cut(4608, TT, MIX)
        qk = cut(6144, 2, 2, T)
        mqT0 = cut(7168, MPAIR, T)
        prob0 = cut(7680, 2, TT, T)
        pT0 = xs[:, 0, :].rearrange("p (h a k) -> p h a k", h=2, a=TT)
        memT = cut(ARENA - 2048, KC, T)
        v1 = cut(0, TT, MIX)
        g1 = cut(1536, TT, MIX)
        qT = cut(3072, HG, T, parts=DK)
        kT = cut(4096, HG, T, parts=DK)
        bcum = cut(5120, 2, HG * T, parts=DK)
        qi = cut(7168, 2, HG * T, parts=DK)
        ki = cut(9216, 2, HG * T, parts=DK)
        qs = cut(11264, 2, HG * T, parts=DK)
        ks = cut(13312, 2, HG * T, parts=DK)
        mqT1 = mixT[:, 6:8, :]
        prob1 = mixT[:, 0:4, :].rearrange("p (h a) k -> p h a k", h=2)
        pT1 = cut(3072, 2, TT, T)
        ksT = xs[:, :, :].rearrange("p a d -> p (a d)")[:, 0:2 * TT * HG * DK].rearrange(
            "p (d a h c) -> p d a h c", d=2, a=TT, h=HG)
        rT = xs[0:32, :, :].rearrange("p a d -> p (a d)")[:, 1792:2048]
        amask = cut(3072, 2, HG, TT, CH)
        asum = cut(4096, HG, TT, CH)
        state = cut(5120, 2, 3, HG, DV, parts=DK)
        sig1 = cut(13312, TT, MIX)
        ppos = cut(0, TT, NE + E4)
        wtok = cut(80, TT, NE + E4)
        sel = cut(160, TT, E4, CAP)
        selw = cut(416, TT, E4, CAP)
        selwT = cut(672, TT, P)
        xsel = cut(928, KC, P)
        sg = cut(1952, FF)
        act = cut(2464, FF)
        actT = cut(2976, FF // P, P)
        yb = cut(3488, D)
        lg = cut(4512, TT, NG + NE)
        t4a = cut(4600, TT, NG)
        goh = cut(4608, TT, NG)
        gpen = cut(4616, TT, NG)
        me = cut(4624, TT, NE)
        oh1 = cut(4688, TT, NE)
        oh2 = cut(4752, TT, NE)
        t32a = cut(4816, TT, NE)
        t32b = cut(4880, TT, NE)
        msk = cut(4944, TT, NE)
        sc = cut(5008, 16, TT)
        cmp8 = cut(5040, 8)
        ntmp = cut(5048, 2)

        mixT_as_tokens = mixT[:, :, :].rearrange("p c t -> p (c t)").rearrange("p (a d) -> p a d", a=TT)
        fin = hT[:, :, :].rearrange("p c t -> p (c t)").rearrange("p (a d) -> p a d", a=TT)
        fnorm = mixT[:, 0:4, :].rearrange("p c t -> p (c t)")
        arena_slots = cut(5120, SLOTS - RSLOTS, SLOT)
        sqj = hT[:, :, :].rearrange("p c t -> p (c t)")

        def norm_src(i):
            return mixT_as_tokens if i == 0 else xres

        s_x, s_mem, s_cst, s_rpb, s_small = sem("x_in"), sem("mem_in"), sem("const_in"), sem("rpb_in"), sem("small_in")
        s_gain = sem("gains_in")
        s_memv = sem("memory_v_weights_in")
        s_gup0 = sem("gup_zeroed")
        s_scrap = sem("scrap_written")
        s_fn = sem("final_norm_in")
        s_out = sem("out_written")
        ring_in = [sem(f"ring_in{i}") for i in range(SLOTS)]
        ring_used = sem("ring_used")
        dchain = sem("dve_chain")
        sp_spare = sem("sp_spare")
        fin_ready = sem("final_ready")
        next_round = sem("next_round")
        n_sq = sem("squares")
        n_var = sem("variance")
        n_sd = sem("deviation")
        n_xs = sem("scaled")
        n_tr = sem("transposed")
        n_hT = sem("normed")
        kv_mm = [sem(f"memkv_mm{i}") for i in range(2)]
        kv_cp = [sem(f"memkv_cp{i}") for i in range(2)]
        v_mm = [sem(f"v_mm{i}") for i in range(2)]
        v_cp = [sem(f"v_cp{i}") for i in range(2)]
        mq_cp = [sem(f"mq_cp{i}") for i in range(2)]
        qk_mm, qk_cp = sem("qk_mm"), sem("qk_cp")
        at_sc = sem("scores")
        at_mx = sem("negmax")
        at_ex = sem("exps")
        at_p = sem("probs")
        at_tr = sem("probsT_mm")
        at_pT = sem("probsT")
        at_o = sem("pv_mm")
        at_oT = sem("mixT")
        s_mask = sem("rpb_masked")
        res = [sem(f"mixed{i}") for i in range(2)]
        wo_mm = sem("wout_tile0")
        mq_mm = sem("mq_mm")
        r_mm, r_cp, z_mm, z_sb = sem("rank_mm"), sem("rank_cp"), sem("z_mm"), sem("z_biased")
        gq_mm, gq_cp = sem("gla_qk_mm"), sem("gla_qk_cp")
        g_mm, g_cp, g_ex = sem("g_mm"), sem("g_cp"), sem("g_sigmoid")
        l_na, l_ex, l_ln = sem("neg_abs"), sem("ls_exp"), sem("ls_ln")
        d_b, d_mid, d_last = sem("b_cum"), sem("b_minus_mid"), sem("last_minus_b")
        e_done = sem("decay_exps")
        q_in, k_in, q_st, k_st = sem("q_intra"), sem("k_intra"), sem("q_state"), sem("k_state")
        kst_mm, kst_cp = sem("k_stateT_mm"), sem("k_stateT")
        a_mm, a_cp = sem("a_mm"), sem("a_masked")
        u_mm, u_st = sem("u_mm"), sem("state_ready")
        o_mm, o_sq, o_var, o_sd, o_mix = sem("o_mm"), sem("o_squares"), sem("o_variance"), sem("o_dev"), sem("o_mix")
        m_tr, m_cp = sem("mix_tr"), sem("mix_cp")
        resets = sem("scan_resets")
        rt_mm = [sem(f"logits{i}") for i in range(2)]
        rt_d = [sem(f"exp_in{i}") for i in range(2)]
        rt_e = [sem(f"exp_out{i}") for i in range(2)]
        rt_m = [sem(f"routed{i}") for i in range(2)]
        rt_p = [sem(f"positions{i}") for i in range(2)]
        rt_n = [sem(f"rounds{i}") for i in range(2)]
        moe_done = [sem(f"moe_done{i}") for i in range(2)]

        class Quads:

            def __init__(self, tag):
                self.sel_ready = sem(f"sel_ready_{tag}")
                self.selT_mm = sem(f"selT_mm_{tag}")
                self.gathered = sem(f"gathered_{tag}")
                self.xsel_ready = sem(f"xsel_ready_{tag}")
                self.selwT_ready = sem(f"selwT_ready_{tag}")
                self.sig_done = sem(f"sigmoid_{tag}")
                self.silu = sem(f"silu_{tag}")
                self.act_ready = sem(f"act_ready_{tag}")
                self.actT_mm = sem(f"actT_mm_{tag}")
                self.actT_ready = sem(f"actT_ready_{tag}")
                self.yb_ready = sem(f"yb_ready_{tag}")
                self.scattered = sem(f"scattered_{tag}")
                self.added = sem(f"added_{tag}")

        PRE0 = 10
        B1 = PRE0 + NQ * FILLS + 1
        PRE1 = B1 + 10

        def rows(w, c0, c1):
            return w.rearrange("(p k) n -> p k n", k=KC)[:, :, c0:c1]

        def slot_view(slot):
            return ring[:, slot * SLOT:(slot + 1) * SLOT] if slot < RSLOTS else arena_slots[:, slot - RSLOTS, :]

        def region(slot, off, n, k):
            a = ring[:, slot * SLOT + off:slot * SLOT + off + n * k]
            return a.rearrange("p (k n) -> p k n", k=k)

        win0, win1 = na_w_in[0], gla_w_in[0]
        KV_FILL = FILLS
        kvw = [region(0, 0, 512, KC),
               slot_view((PRE0 + KV_FILL) % SLOTS).rearrange("p (k n) -> p k n", k=KC)]
        vw0 = region(1, 0, MIX, KC)
        mqw0 = region(1, MIX * KC, 256, KC)
        qkw = [[region(3 + p // 2, (p % 2) * 2048 + t * 1024, P, KC) for t in range(2)] for p in range(NPAIR)]
        wow = [[region(s, 0, D, 4) for s in (0, 1)], [region(s, 0, D, 4) for s in (3, 4)]]
        rw1 = region(3, 0, 288, KC)
        qkw1 = [[region(4, (3 * t + j) * P * KC, P, KC) for j in range(3)] for t in range(2)]
        vgw1 = region(0, 0, 2 * MIX, KC)
        wo_src = [[w_out[l][512 * i:512 * i + 512, :].rearrange("(c p) n -> p c n", p=P) for i in range(2)]
                  for l in range(2)]

        stream0 = [(0, 0, kvw[0][:, :, 0:256], rows(w_mem_kv[0], 0, 256)),
                   (1, 0, vw0, rows(win0, 2 * MIX, 3 * MIX)),
                   (2, 0, mqw0, rows(win0, 3 * MIX, 3 * MIX + 256))]
        for p in range(NPAIR):
            for t in range(2):
                stream0.append((3 + p // 2, 0, qkw[p][t], rows(win0, t * MIX + p * P, t * MIX + p * P + P)))
        stream0 += [(0, 1, wow[0][0], wo_src[0][0]), (1, 3, wow[0][1], wo_src[0][1])]
        stream1 = [(3, B1 - 7, rw1, rows(win1, 3 * MIX, 3 * MIX + 288)),
                   *[(5, B1 - 5, qkw1[t][j][:, :, c0:c0 + n], rows(win1, t * HG * DK + w0, t * HG * DK + w0 + n))
                     for t in range(2) for j in range(3) for c0, w0, n in ((0, j * DK, DK), (DK, 3 * DK + 32 * j, 32))],
                   (2, B1, vgw1, rows(win1, MIX, 3 * MIX)),
                   (3, B1 + 1, wow[1][0], wo_src[1][0]),
                   (4, B1 + 3, wow[1][1], wo_src[1][1])]

        count = [0] * SLOTS
        arrive0, arrive1 = [], []
        for slot, _, _, _ in stream0:
            count[slot] += 16
            arrive0.append((ring_in[slot], count[slot]))
        base0 = list(count)
        for n in range(NQ * FILLS + 1):
            count[(PRE0 + n) % SLOTS] += 16
        for slot, _, _, _ in stream1:
            count[slot] += 16
            arrive1.append((ring_in[slot], count[slot]))
        base1 = list(count)
        first, more = Quads("first"), Quads("more")

        class Run:

            def __init__(self, sig, slot0, ring_in, ring_used, in_base, used_base):
                self.sig, self.slot0, self.ring_in, self.ring_used = sig, slot0, ring_in, ring_used
                self.in_base, self.used_base = in_base, used_base

            def fill(self, pair, n):
                slot = (self.slot0 + n) % SLOTS
                return slot, pair * (LAPS * 16) + ((n // SLOTS + 1) * 16 + self.in_base[slot])

            def used(self, pair, n):
                return pair * (2 * FILLS) + (self.used_base + n)

        main = [Run(first, PRE0 % SLOTS, ring_in, ring_used, base0, PRE0),
                Run(first, 5, ring_in, ring_used, base1, PRE1)]
        more_in, more_used = [sem(f"more_in{i}") for i in range(SLOTS)], sem("more_used")
        extra = Run(more, 0, more_in, more_used, [0] * SLOTS, SLOTS)

        w1v = [moe_w1[l].rearrange("e (p k) f -> p e (k f)", k=KC) for l in range(2)]
        w3v = [moe_w3[l].rearrange("e (p k) f -> p e (k f)", k=KC) for l in range(2)]
        w2v = [moe_w2[l].rearrange("e (j p) n -> j p e n", p=P) for l in range(2)]

        def rounds(eng, l):
            hi = eng.value_load(nround[0:1, l:l + 1], min_val=0, max_val=(l + 1) * (T // CAP - 1))
            return (eng.value_load(nround[0:1, 0:1], min_val=0, max_val=T // CAP - 1) if l else 0), hi

        def small_loads():
            loads = [(gnorm[:], gla_out_norm[0:1, :].to_broadcast([P, DV])),
                     (gcol[:, 3, :], norm_mix[1].rearrange("(p k) -> p k", k=KC))]
            for l in range(2):
                loads += [(gcol[:, 2 + 2 * l, :], norm_ffn[l].rearrange("(p k) -> p k", k=KC)),
                          (wlog[:, l, :, 0:NG], moe_w_group[l].rearrange("(p k) n -> p k n", k=KC)),
                          (wlog[:, l, :, NG:NG + NE], moe_w_router[l].rearrange("(p k) n -> p k n", k=KC)),
                          (rbias[:, l, 0:NG], moe_b_group[l:l + 1, :].to_broadcast([P, NG])),
                          (rbias[:, l, NG:NG + NE], moe_b_router[l:l + 1, :].to_broadcast([P, NE]))]
            for d in range(2):
                loads += [(gup[16 * d:16 * d + 16, d, :], gla_gate_up[0, d])]
            assert SMALL == 16 * (len(loads) + 2)
            return loads

        block = ctx.enter_context(nc.Block())

        @block.sync
        def _(sp):
            sp.dma_start(mixT_as_tokens, mem[0].rearrange("(a p) d -> p a d", p=P)).then_inc(s_mem, 16)
            sp.dma_start(xres[:], x[0].rearrange("(a p) d -> p a d", p=P)).then_inc(s_x, 16)

            def fill(stream):
                for slot, need, dst, src in stream:
                    if need:
                        sp.wait_ge(ring_used, need)
                    sp.dma_start(dst, src).then_inc(ring_in[slot], 16)

            def quad_fills(rn, l, pair, g, n0):
                for f in range(FILLS):
                    slot, _ = rn.fill(pair, n0 + f)
                    sp.wait_ge(rn.ring_used, rn.used(pair, n0 + f - SLOTS + 1))
                    dst = slot_view(slot).rearrange("p (e n) -> p e n", e=E4)
                    if f < 8:
                        src = (w1v, w3v)[f // 4][l][:, bass.ds(g * E4, E4), (f % 4) * 1024:(f % 4) * 1024 + 1024]
                    else:
                        src = w2v[l][f - 8][:, bass.ds(g * E4, E4), :]
                    sp.dma_start(dst, src).then_inc(rn.ring_in[slot], 16)

            def experts(l):
                with sp.Fori(0, PAIRS - 1 if l == 0 else PAIRS) as pair:
                    for s in range(2):
                        quad_fills(main[l], l, pair, pair * 2 + s, s * FILLS)
                if l == 0:
                    last = PAIRS - 1
                    quad_fills(main[0], 0, last, NQ - 2, 0)
                    slot, _ = main[0].fill(last, KV_FILL)
                    sp.wait_ge(ring_used, main[0].used(last, KV_FILL - SLOTS + 1))
                    sp.dma_start(kvw[1], rows(w_mem_kv[1], 0, 512)).then_inc(ring_in[slot], 16)
                    quad_fills(main[0], 0, last, NQ - 1, FILLS + 1)
                sp.wait_ge(rt_n[l], 1)
                lo, hi = rounds(sp, l)
                with sp.If(hi > lo):
                    sp.wait_ge(ring_used, (B1, PRE1 + NQ * FILLS)[l])
                    with sp.Fori(lo, hi) as r:
                        with sp.Fori(0, PAIRS) as pair:
                            for s in range(2):
                                quad_fills(extra, l, r * PAIRS + pair, pair * 2 + s, s * FILLS)
                    sp.wait_ge(moe_done[l], 1)
                    sp.sem_inc(sp_spare, 1)

            sp.sem_inc(more_used, SLOTS)
            fill(stream0[0:1])
            sp.dma_start(kvw[0][:, :, 256:512], rows(w_mem_kv[0], 256, 512)).then_inc(s_memv, 16)
            fill(stream0[1:])
            experts(0)
            fill(stream1)
            experts(1)
            sp.wait_ge(s_out, 32)

        
        @block.gpsimd
        def _(pool):
            nc.gpsimd.memset(gup[:], 0.0).then_inc(s_gup0, 1)
            pool.wait_ge(s_gup0, 1)
            pool.wait_ge(ring_in[1], 16)
            for r in range(2):
                for i in range(NA_DR):
                    src = bass.AP(tensor=na_rpb.tensor, offset=na_rpb.offset + (i + 5 - r) * RPB_W + 15 - (GRID - 1),
                                  ap=[[1, GRID], [RPB_H * RPB_W, 2 * NPAIR], [1, GRID]])
                    pool.dma_start(rpbt[64 * r:64 * r + 64, :, i, :], src).then_inc(s_rpb, 16)
            pool.wait_ge(s_cst, 16)
            pool.wait_ge(s_rpb, 16 * 2 * NA_DR)
            rows_of = rpbt.rearrange("p h i c -> p (h i) c")
            nc.gpsimd.tensor_tensor(rows_of, rows_of, cst[:, C_NAM:C_NAM + GRID].unsqueeze(1).to_broadcast(
                [P, 2 * NPAIR * NA_DR, GRID]), ALU.add).then_inc(s_mask, 1)
            for dst, src in small_loads():
                pool.dma_start(dst, src).then_inc(s_small, 16)
            with nc.allow_non_contiguous_dma(reason="768 gate biases, feature on the partition"):
                for d in range(2):
                    pool.dma_start(gbias[:, d, :], gla_gate_bias[0, d].rearrange("(h p) -> p h", p=DK)).then_inc(s_small, 16)
            pool.wait_ge(moe_done[0], 1)
            kc = ks.rearrange("p d (n c) -> p d n c", c=CH)
            nc.gpsimd.memset(ks, 1.0).then_inc(resets, 1)
            pool.wait_ge(resets, 1)
            nc.gpsimd.memset(kc[:, 0, :, 0:1], 0.0).then_inc(resets, 1)
            nc.gpsimd.memset(kc[:, 1, :, CH - 1:CH], 0.0).then_inc(resets, 1)

        @block.tensor
        def _(pe):
            def arrived(a):
                pe.wait_ge(*a)

            def keep_warm(n, bank):
                for _ in range(n):
                    pe.matmul(ps[:, bank, :], ident, cst[:, 0:512], start=True, stop=True)

            def transpose_tile(i, src, a, bank):
                for k in range(KC):
                    t = pe.transpose(ps[:, bank + k // 4, (k % 4) * P:(k % 4) * P + P], src[:, a, k::KC], ident)
                t.then_inc(n_tr, 1)

            def transposes(i, src):
                for a in range(TT):
                    pe.wait_ge(n_xs, TT * XS_NTH[i] + a + 1)
                    transpose_tile(i, src, a, NBANK[i][a])

            def mem_kv(l):
                w = kvw[l]
                if l == 0:
                    arrived(arrive0[0])
                else:
                    slot, there = main[0].fill(PAIRS - 1, KV_FILL)
                    pe.wait_ge(ring_in[slot], there)
                for m in range(MPAIR):
                    for k in range(KC):
                        t = pe.matmul(ps[:, KVB[l], m * T:(m + 1) * T], w[:, k, m * P:(m + 1) * P], memT[:, k, :],
                                      start=k == 0, stop=k == KC - 1)
                t.then_inc(kv_mm[l], 1)
                if l == 0:
                    pe.wait_ge(s_memv, 16)
                for a in range(TT):
                    for k in range(KC):
                        t = pe.matmul(ps[:, KVB[l] + 1, a * 256:a * 256 + 256], memT[:, k, a * P:(a + 1) * P], w[:, k, 256:512],
                                      start=k == 0, stop=k == KC - 1)
                t.then_inc(ring_used, 1)

            def token_rows(w, n0, a, half, bank):
                for k in range(KC):
                    t = pe.matmul(ps[:, bank, 0:384], hT[:, k, a * P:(a + 1) * P],
                                  w[:, k, n0 + 384 * half:n0 + 384 * half + 384], start=k == 0, stop=k == KC - 1)
                return t

            def scores(l, p, q_of, k_of):
                for a in range(TT):
                    for h in range(2):
                        r = slice(64 * h, 64 * h + 64)
                        t = pe.matmul(ps[:, 2 + h, a * T:(a + 1) * T], q_of[r, a * P:(a + 1) * P], k_of[r, :],
                                      start=True, stop=True)
                t.then_inc(at_sc, 1)

            def probs_T(n, prob):
                pe.wait_ge(at_p, n + 1)
                for h in range(2):
                    for a in range(TT):
                        for kt in range(TT):
                            t = pe.transpose(ps[:, 4 + h, kt * T + a * P:kt * T + a * P + P],
                                             prob[:, h, a, kt * P:(kt + 1) * P], ident)
                t.then_inc(at_tr, 1)

            def weighted(n, pT, v_of):
                pe.wait_ge(at_pT, n + 1)
                for h in range(2):
                    for kt in range(TT):
                        t = pe.matmul(ps[64 * h:64 * h + 64, 6, 0:T], v_of(h, kt), pT[:, h, kt, :],
                                      start=kt == 0, stop=kt == TT - 1)
                t.then_inc(at_o, 1)

            def out_proj(l, a, chunks, last):
                for c in chunks:
                    for half in range(2):
                        t = pe.matmul(ps[:, WOB[l][a] + half, :], mixT[:, c, a * P:(a + 1) * P],
                                      wow[l][c // 4][:, c % 4, 512 * half:512 * half + 512],
                                      start=c == 6, stop=c == last)
                return t

            def logits(l, a):
                pe.wait_ge(s_small, SMALL)
                pe.wait_ge(n_hT, TT * (2 * l + 2) + a + 1)
                for k in range(KC):
                    t = pe.matmul(ps[:, RTB[l], a * 64:a * 64 + NG + NE], hT[:, k, a * P:(a + 1) * P], wlog[:, l, k, :],
                                  start=k == 0, stop=k == KC - 1)
                return t

            def route(l):
                rb = RTB[l]
                keep_warm(1, rb + 1)
                logits(l, 1).then_inc(rt_mm[l], 1)
                keep_warm(7, rb + 1)
                pe.wait_ge(rt_m[l], 1)
                pe.matmul(ps[:, rb + 1, 0:NE], tri, msk[:, 0, :], start=True, stop=True)
                pe.matmul(ps[:, rb + 1, NE:2 * NE], ones, msk[:, 0, :], start=True, stop=False)
                pe.matmul(ps[:, rb + 1, NE:2 * NE], tri, msk[:, 1, :], start=False, stop=True).then_inc(rt_p[l], 1)
                pe.matmul(ps[:, rb + 2, 0:NE], ones, msk[:, 0, :], start=True, stop=False)
                pe.matmul(ps[:, rb + 2, 0:NE], ones, msk[:, 1, :], start=False, stop=True).then_inc(rt_p[l], 1)

            def quad(rn, c, pair, n0, sel_count, warm=0):
                pe.wait_ge(rn.sig.sel_ready, sel_count)
                for k in range(KC):
                    for a in range(TT):
                        t = pe.matmul(ps[:, k // 4, (k % 4) * P:(k % 4) * P + P], xs[:, a, k::KC],
                                      sel[:, a].rearrange("p e s -> p (e s)"), start=a == 0, stop=a == TT - 1)
                t.then_inc(rn.sig.gathered, 1)
                pe.wait_ge(rn.sig.sel_ready, sel_count + 1)
                for a in range(TT):
                    t = pe.transpose(ps[:, 2, a * P:(a + 1) * P], selw[:, a].rearrange("p e s -> p (e s)"), ident)
                t.then_inc(rn.sig.selT_mm, 1)
                for f in range(8):
                    if f % 2 == 0 and f < 4:
                        pe.wait_ge(rn.sig.xsel_ready, c * 2 + f // 2 + 1)
                    slot, there = rn.fill(pair, n0 + f)
                    pe.wait_ge(rn.ring_in[slot], there)
                    for kk in range(2):
                        k = 2 * (f % 4) + kk
                        for e in range(E4):
                            o = e * 1024 + kk * FF
                            t = pe.matmul(ps[32 * e:32 * e + 32, 4 + f // 4, :], xsel[:, k, 32 * e:32 * e + 32],
                                          slot_view(slot)[:, o:o + FF], start=k == 0, stop=k == KC - 1, tile_position=(0, 32 * e))
                    t.then_inc(rn.ring_used, 1)
                pe.wait_ge(rn.sig.act_ready, c + 1)
                for j in range(4):
                    t = pe.transpose(ps[:, 3, j * P:(j + 1) * P], act[:, j * P:(j + 1) * P], ident)
                t.then_inc(rn.sig.actT_mm, 1)
                pe.wait_ge(rn.sig.actT_ready, c + 1)
                for j in range(4):
                    keep_warm(warm, 2)
                    f = 8 + j
                    slot, there = rn.fill(pair, n0 + f)
                    pe.wait_ge(rn.ring_in[slot], there)
                    for half in range(2):
                        for e in range(E4):
                            o = e * D + half * 512
                            t = pe.matmul(ps[32 * e:32 * e + 32, 6 + half, :], actT[:, j, 32 * e:32 * e + 32],
                                          slot_view(slot)[:, o:o + 512], start=j == 0, stop=j == 3, tile_position=(0, 32 * e))
                    t.then_inc(rn.ring_used, 1)
                keep_warm(warm // 2, 2)
                pe.wait_ge(rn.sig.selwT_ready, c + 1)
                pe.wait_ge(rn.sig.yb_ready, c * 2 + 2)
                for a in range(TT):
                    for half in range(2):
                        t = pe.matmul(ps[:, 4 + 2 * a + half, :], selwT[:, a, :], yb[:, half * 512:half * 512 + 512],
                                      start=True, stop=True)
                    t.then_inc(rn.sig.scattered, 1)

            def experts(l):
                with pe.Fori(0, PAIRS - 1) as pair:
                    for s in range(2):
                        quad(main[l], pair * 2 + (l * NQ + s), pair, s * FILLS, pair * 4 + (l * SELS + 1 + 2 * s))
                last = PAIRS - 1
                quad(main[l], l * NQ + NQ - 2, last, 0, l * SELS + 2 * NQ - 3)
                if l == 0:
                    mem_kv(1)
                    pe.wait_ge(kv_cp[1], 2)
                quad(main[l], l * NQ + NQ - 1, last, FILLS + (l == 0), l * SELS + 2 * NQ - 1, 2)
                if l == 0:
                    keep_warm(6, 2)
                pe.wait_ge(rt_n[l], 1)
                lo, hi = rounds(pe, l)
                with pe.If(hi > lo):
                    with pe.Fori(lo, hi) as r:
                        with pe.Fori(0, PAIRS) as pair:
                            for s in range(2):
                                quad(extra, r * NQ + pair * 2 + s, r * PAIRS + pair, s * FILLS,
                                     r * SELS + pair * 4 + (2 * s + 1))

            def v_na(p):
                return lambda h, kt: v0[:, kt, p * P + 64 * h:p * P + 64 * h + 64]

            def v_mem(l, m):
                return lambda h, kt: vm[:, l, kt, m * P + 64 * h:m * P + 64 * h + 64]

            pe.wait_ge(s_cst, 16)
            keep_warm(2, 7)
            transposes(0, mixT_as_tokens)
            transposes(1, xs)
            pe.wait_ge(n_hT, TT)
            mem_kv(0)
            pe.wait_ge(n_hT, TT * 2)
            arrived(arrive0[2])
            for m in range(MPAIR):
                for k in range(KC):
                    t = pe.matmul(ps[:, 2, m * T:(m + 1) * T], mqw0[:, k, m * P:(m + 1) * P], hT[:, k, :],
                                  start=k == 0, stop=k == KC - 1)
            t.then_inc(mq_mm, 1)
            pe.wait_ge(mq_cp[0], 1)
            pe.wait_ge(kv_cp[0], 2)
            scores(0, 0, mqT0[:, 0, :], kTm[:, 0, 0, :])
            arrived(arrive0[1])
            for m in range(MPAIR):
                if m == 1:
                    pe.wait_ge(v_cp[0], 1)
                token_rows(vw0, 0, m, 0, 0)
                t = token_rows(vw0, 0, m, 1, 1)
                t.then_inc((v_mm[0], ring_used)[m], m + 1)
                probs_T(m, prob0)
                if m == 0:
                    scores(0, 1, mqT0[:, 1, :], kTm[:, 0, 1, :])
                    weighted(0, pT0, v_mem(0, 0))
            pe.wait_ge(v_cp[0], TT)
            for p in range(NPAIR):
                n = MPAIR + p
                if p % 2 == 0:
                    arrived(arrive0[3 + 2 * p + 3])
                if p >= 2:
                    pe.wait_ge(qk_cp, 2 * (p - 1))
                for t_ in range(2):
                    for k in range(KC):
                        t = pe.matmul(ps[:, p % 2, t_ * T:(t_ + 1) * T], qkw[p][t_][:, k, :], hT[:, k, :],
                                      start=k == 0, stop=k == KC - 1)
                t.then_inc(qk_mm if p % 2 == 0 else ring_used, 1)
                if p >= 1:
                    probs_T(n - 1, prob0)
                else:
                    pe.wait_ge(at_oT, 1)
                    weighted(1, pT0, v_mem(0, 1))
                pe.wait_ge(qk_cp, 2 * (p + 1))
                scores(0, n, qk[:, p % 2, 0, :], qk[:, p % 2, 1, :])
                if p >= 1:
                    pe.wait_ge(at_oT, n - 1)
                    weighted(n - 1, pT0, v_na(p - 1))
            arrived(arrive0[15])
            arrived(arrive0[16])
            pe.wait_ge(at_oT, N1 - 2)
            out_proj(0, 0, (6, 7, 0, 1, 2, 3), 5)
            probs_T(N1 - 1, prob0)
            pe.wait_ge(at_oT, N1 - 1)
            out_proj(0, 0, (4,), 5)
            weighted(N1 - 1, pT0, v_na(NPAIR - 1))
            out_proj(0, 1, (6,), 5)
            pe.wait_ge(at_oT, N1)
            out_proj(0, 0, (5,), 5).then_inc(ring_used, 2)
            out_proj(0, 1, (7, 0, 1, 2), 5)
            pe.wait_ge(res[0], 1)
            transpose_tile(2, xres, 0, NBANK[2][0])
            out_proj(0, 1, (3, 4), 5)
            logits(0, 0)
            out_proj(0, 1, (5,), 5).then_inc(ring_used, 2)
            keep_warm(1, RTB[0] + 1)
            pe.wait_ge(res[0], 2)
            transpose_tile(2, xres, 1, NBANK[2][1])
            route(0)
            experts(0)

            pe.wait_ge(moe_done[0], 1)
            transposes(3, xs)
            pe.wait_ge(n_hT, TT * 4)
            arrived(arrive1[0])
            for k in range(KC):
                t = pe.matmul(ps[0:32, 4, 0:T], rw1[:, k, 0:32], hT[:, k, :], start=k == 0, stop=k == KC - 1)
            t.then_inc(r_mm, 1)
            for m in range(MPAIR):
                for k in range(KC):
                    t = pe.matmul(ps[:, 5, m * T:(m + 1) * T], rw1[:, k, 32 + m * P:32 + (m + 1) * P], hT[:, k, :],
                                  start=k == 0, stop=k == KC - 1)
            t.then_inc(ring_used, 1)
            pe.wait_ge(r_cp, 1)
            for d in range(2):
                for h in range(HG):
                    t = pe.matmul(ps[0:DK, 2 * d + h // 2, (h % 2) * T:(h % 2) * T + T],
                                  gup[:, d, h * DK:(h + 1) * DK], rT, start=True, stop=True)
            t.then_inc(z_mm, 1)
            arrived(arrive1[12])
            pe.wait_ge(mq_cp[1], 1)
            for j in range(3):
                for t_ in range(2):
                    for k in range(KC):
                        t = pe.matmul(ps[:, 4 + j, t_ * T:(t_ + 1) * T], qkw1[t_][j][:, k, :], hT[:, k, :],
                                      start=k == 0, stop=k == KC - 1)
                if j < 2:
                    t.then_inc(gq_mm, 1)
            t.then_inc(ring_used, 2)
            pe.wait_ge(z_sb, 2)
            scores(1, N1, mqT1[:, 0, :], kTm[:, 1, 0, :])
            arrived(arrive1[13])
            for i in range(2 * TT):
                if i >= 2:
                    pe.wait_ge(v_cp[1], i - 1)
                token_rows(vgw1, 0, i // 2, i % 2, i % 2).then_inc(v_mm[1], 1)
            pe.wait_ge(gq_cp, 4 * 3)
            probs_T(N1, prob1)
            scores(1, N1 + 1, mqT1[:, 1, :], kTm[:, 1, 1, :])
            weighted(N1, pT1, v_mem(1, 0))
            pe.wait_ge(k_st, 2)
            pe.wait_ge(v_cp[1], 2 * TT)
            for d in range(2):
                for a in range(TT):
                    if (d, a) == (1, 1):
                        pe.wait_ge(at_oT, N1 + 1)
                    for h in range(HG):
                        t = pe.transpose(ps[:, KSTB[2 * d + a], h * DK:(h + 1) * DK],
                                         ks[:, d, h * T + a * P:h * T + a * P + P], ident[0:DK, 0:DK])
                    t.then_inc(kst_mm, 1)

            def out_gate(i):
                if i >= 2:
                    pe.wait_ge(g_cp, i - 1)
                t = token_rows(vgw1, MIX, i // 2, i % 2, i % 2)
                t.then_inc(g_mm, 1)

            def update(i):
                step, d = i // 2, i % 2
                n = step if d == 0 else NCH - 1 - step
                if i >= 2:
                    pe.wait_ge(u_st, i - 1)
                r = (n % 2) * 64
                for h in range(HG):
                    t = pe.matmul(ps[0:DK, 4 + 2 * d + h // 2, (h % 2) * DV:(h % 2 + 1) * DV],
                                  ksT[r:r + 64, d, n // 2, h, :], v1[r:r + 64, n // 2, h * DV:(h + 1) * DV],
                                  start=True, stop=True)
                t.then_inc(u_mm, 1)

            pe.wait_ge(kst_cp, 1)
            out_gate(0)
            probs_T(N1 + 1, prob1)
            pe.wait_ge(q_in, 2)
            pe.wait_ge(k_in, 2)
            for d in range(2):
                for h in range(HG):
                    for n in range(NCH):
                        c = slice(h * T + n * CH, h * T + (n + 1) * CH)
                        r = (n % 2) * 64
                        t = pe.matmul(ps[r:r + 64, 2 + d, (h * TT + n // 2) * CH:(h * TT + n // 2 + 1) * CH],
                                      ki[:, d, c], qi[:, d, c], start=True, stop=True)
                t.then_inc(a_mm, 1)
            pe.wait_ge(kst_cp, 4)
            weighted(N1 + 1, pT1, v_mem(1, 1))
            out_gate(1)
            pe.wait_ge(at_oT, N1 + 2)
            update(0)
            update(1)
            update(2)
            update(3)
            out_gate(2)
            update(4)
            update(5)
            out_gate(3)
            pe.wait_ge(a_cp, 1)
            pe.wait_ge(q_st, 2)
            pe.wait_ge(u_st, 6)
            pe.wait_ge(g_cp, 4)
            for a in range(TT):
                for h in range(HG):
                    for half in range(2):
                        n = 2 * a + half
                        r = 64 * half
                        o = ps[r:r + 64, OB[a] + h // 2, (h % 2) * DV:(h % 2 + 1) * DV]
                        c = slice(h * T + n * CH, h * T + (n + 1) * CH)
                        inter = ([(0, n - 1)] if n > 0 else []) + ([(1, NCH - 2 - n)] if n < NCH - 1 else [])
                        pe.matmul(o, asum[r:r + 64, h, a, :], v1[r:r + 64, a, h * DV:(h + 1) * DV],
                                  start=True, stop=False)
                        for j, (d, s_) in enumerate(inter):
                            t = pe.matmul(o, qs[:, d, c], state[:, d, s_, h, :], start=False, stop=j == len(inter) - 1)
                if a == 0:
                    t.then_inc(o_mm, 1)
                else:
                    t.then_inc(ring_used, 5)
            arrived(arrive1[14])
            arrived(arrive1[15])

            def mix_columns(a):
                pe.wait_ge(o_mix, a + 1)
                for c in range(6):
                    t = pe.transpose(ps[:, (6, 0)[a] + c // 4, (c % 4) * P:(c % 4) * P + P], g1[:, a, c * P:(c + 1) * P],
                                     ident)
                t.then_inc(m_tr, 1)

            out_proj(1, 0, (6, 7), 5)
            mix_columns(0)
            out_proj(1, 1, (6, 7), 5)
            mix_columns(1)
            pe.wait_ge(m_cp, 2)
            out_proj(1, 0, (0, 1, 2, 3, 4, 5), 5).then_inc(wo_mm, 1)
            pe.wait_ge(m_cp, 4)
            out_proj(1, 1, (0, 1, 2), 5)
            pe.wait_ge(res[1], 1)
            transpose_tile(4, xres, 0, NBANK[4][0])
            out_proj(1, 1, (3, 4), 5)
            logits(1, 0)
            out_proj(1, 1, (5,), 5).then_inc(ring_used, 2)
            keep_warm(1, RTB[1] + 1)
            pe.wait_ge(res[1], 2)
            transpose_tile(4, xres, 1, NBANK[4][1])
            route(1)
            experts(1)

        @block.scalar
        def _(act_e):
            act_e.dma_start(cst[:], consts).then_inc(s_cst, 16)
            act_e.dma_start(gcol[:, 0, :], mem_norm.rearrange("(p k) -> p k", k=KC)).then_inc(s_gain, 16)
            act_e.dma_start(gcol[:, 1, :], norm_mix[0].rearrange("(p k) -> p k", k=KC)).then_inc(s_gain, 16)
            def table(func):
                nc.scalar.activation(scrap[:, 1:2], scrap[:, 0:1], func).then_inc(s_scrap, 1)

            def norm(i):
                src = norm_src(i)
                for a in range(TT):
                    if i in (2, 4):
                        act_e.wait_ge(res[i // 2 - 1], a + 1)
                    nc.scalar.activation(xs[:, a, :], src[:, a, :], ACT.Square,
                                         accum_out=st[:, 2 * i + a:2 * i + a + 1]).then_inc(n_sq, 1)
                act_e.wait_ge(n_var, i + 1)
                nc.scalar.activation(st[:, 24 + 2 * i:26 + 2 * i], st[:, 12 + 2 * i:14 + 2 * i], ACT.Sqrt).then_inc(n_sd, 1)

            def copy_kv(l):
                act_e.wait_ge(kv_mm[l], 1)
                nc.scalar.copy(kTm[:, l].rearrange("p m t -> p (m t)"), ps[:, KVB[l], :]).then_inc(kv_cp[l], 1)
                act_e.wait_ge(ring_used, (1, main[0].used(PAIRS - 1, KV_FILL + 1))[l])
                nc.scalar.copy(vm[:, l].rearrange("p a n -> p (a n)"), ps[:, KVB[l] + 1, :]).then_inc(kv_cp[l], 1)

            def exps(l, n, prob, raw):
                act_e.wait_ge(at_mx, n + 1)
                for h in range(2):
                    for a in range(TT):
                        i = 2 * h + a
                        src = ps[:, 2 + h, a * T:(a + 1) * T] if raw else prob[:, h, a, :]
                        nc.scalar.activation(prob[:, h, a, :], src, ACT.Exp, bias=st[:, 40 + i:41 + i],
                                             scale=DH ** -0.5 if raw else 1.0,
                                             accum_out=st[:, 44 + i:45 + i]).then_inc(at_ex, 1)

            def copy_pT(l, n, pT):
                act_e.wait_ge(at_tr, n + 1)
                nc.scalar.copy(pT.rearrange("p h a k -> p (h a k)"),
                               ps[:, 4:6, :].rearrange("p b n -> p (b n)")).then_inc(at_pT, 1)

            def by_row(t):
                return t.rearrange("p (r c) -> p r c", c=GRID)

            def copy_o(l, n, c):
                act_e.wait_ge(at_o, n + 1)
                if c < NPAIR:
                    nc.scalar.copy(by_row(mixT[:, c, :]), by_row(ps[:, 6, 0:T])[:, :, ::-1]).then_inc(at_oT, 1)
                else:
                    nc.scalar.copy(mixT[:, c, :], ps[:, 6, 0:T]).then_inc(at_oT, 1)

            def route(l):
                act_e.wait_ge(rt_d[l], 1)
                nc.scalar.activation(t4a, t4a, ACT.Exp).then_inc(rt_e[l], 1)
                act_e.wait_ge(rt_d[l], 2)
                nc.scalar.activation(sc[:, 6, :], sc[:, 5, :], ACT.Exp).then_inc(rt_e[l], 1)

            def quad(rn, c, pair, n0):
                act_e.wait_ge(rn.sig.selT_mm, c + 1)
                nc.scalar.copy(selwT.rearrange("p a t -> p (a t)"), ps[:, 2, 0:T]).then_inc(rn.sig.selwT_ready, 1)
                act_e.wait_ge(rn.ring_used, rn.used(pair, n0 + 4))
                nc.scalar.activation(sg, ps[:, 4, :], ACT.Sigmoid).then_inc(rn.sig.sig_done, 1)
                act_e.wait_ge(rn.sig.actT_mm, c + 1)
                nc.scalar.copy(actT.rearrange("p j s -> p (j s)"), ps[:, 3, :]).then_inc(rn.sig.actT_ready, 1)
                act_e.wait_ge(rn.ring_used, rn.used(pair, n0 + 12))
                for half in range(2):
                    nc.scalar.copy(yb[:, half * 512:half * 512 + 512], ps[:, 6 + half, :]).then_inc(rn.sig.yb_ready, 1)

            def experts(l):
                with act_e.Fori(0, PAIRS - 1 if l == 0 else PAIRS) as pair:
                    for s in range(2):
                        quad(main[l], pair * 2 + (l * NQ + s), pair, s * FILLS)
                if l == 0:
                    quad(main[0], NQ - 2, PAIRS - 1, 0)
                    copy_kv(1)
                    quad(main[0], NQ - 1, PAIRS - 1, FILLS + 1)
                act_e.wait_ge(rt_n[l], 1)
                lo, hi = rounds(act_e, l)
                with act_e.If(hi > lo):
                    with act_e.Fori(lo, hi) as r:
                        with act_e.Fori(0, PAIRS) as pair:
                            for s in range(2):
                                quad(extra, r * NQ + pair * 2 + s, r * PAIRS + pair, s * FILLS)

            act_e.wait_ge(s_scrap, 1)
            table(ACT.Sqrt)
            act_e.wait_ge(s_mem, 16)
            norm(0)
            act_e.wait_ge(s_x, 16)
            norm(1)
            copy_kv(0)
            act_e.wait_ge(mq_mm, 1)
            nc.scalar.copy(mqT0.rearrange("p m t -> p (m t)"), ps[:, 2, :]).then_inc(mq_cp[0], 1)
            for m in range(MPAIR):
                exps(0, m, prob0, True)
                if m == 0:
                    act_e.wait_ge(v_mm[0], 1)
                else:
                    act_e.wait_ge(ring_used, 3)
                nc.scalar.copy(v0[:, m, :].rearrange("p (b n) -> p b n", b=2), ps[:, 0:2, 0:384]).then_inc(v_cp[0], 1)
                copy_pT(0, m, pT0)
                if m == 0:
                    copy_o(0, 0, 6)
            for p in range(NPAIR):
                n = MPAIR + p
                if p % 2 == 0:
                    act_e.wait_ge(qk_mm, p // 2 + 1)
                else:
                    act_e.wait_ge(ring_used, 3 + (p + 1) // 2)
                nc.scalar.copy(by_row(qk[:, p % 2, 0, :]), by_row(ps[:, p % 2, 0:T])[:, :, ::-1]).then_inc(qk_cp, 1)
                nc.scalar.copy(qk[:, p % 2, 1, :], ps[:, p % 2, T:2 * T]).then_inc(qk_cp, 1)
                if p >= 1:
                    copy_pT(0, n - 1, pT0)
                copy_o(0, n - 1, p - 1 if p >= 1 else 7)
                exps(0, n, prob0, False)
            copy_pT(0, N1 - 1, pT0)
            copy_o(0, N1 - 1, NPAIR - 1)
            table(ACT.Sqrt)
            norm(2)
            route(0)
            experts(0)

            table(ACT.Sqrt)
            act_e.wait_ge(moe_done[0], 1)
            norm(3)
            act_e.wait_ge(r_mm, 1)
            nc.scalar.copy(rT, ps[0:32, 4, 0:T]).then_inc(r_cp, 1)
            act_e.wait_ge(ring_used, B1 + 1)
            nc.scalar.copy(mqT1.rearrange("p m t -> p (m t)"), ps[:, 5, :]).then_inc(mq_cp[1], 1)
            act_e.wait_ge(l_na, 1)
            nc.scalar.activation(ki, ki, ACT.Exp).then_inc(l_ex, 1)
            act_e.wait_ge(l_ex, 1)
            nc.scalar.activation(ki, ki, ACT.Ln, bias=1.0).then_inc(l_ln, 1)

            def copy_qk(j):
                if j < 2:
                    act_e.wait_ge(gq_mm, j + 1)
                else:
                    act_e.wait_ge(ring_used, B1 + 3)
                for dst, src in ((slice(0, DK), slice(0, DK)), (slice(32 * j, 32 * j + 32), slice(DK, P))):
                    h = j if dst.start == 0 and dst.stop == DK else HG - 1
                    nc.scalar.mul(qT[dst, h, :], ps[src, 4 + j, 0:T], DK ** -0.5).then_inc(gq_cp, 1)
                    nc.scalar.copy(kT[dst, h, :], ps[src, 4 + j, T:2 * T]).then_inc(gq_cp, 1)

            copy_qk(0)
            copy_qk(1)
            act_e.wait_ge(d_b, 2)
            nc.scalar.activation(qs, bcum, ACT.Exp, scale=1 / 16).then_inc(e_done, 1)
            act_e.wait_ge(d_mid, 2)
            nc.scalar.activation(ki, qi, ACT.Exp, scale=-1 / 16).then_inc(e_done, 1)
            act_e.wait_ge(e_done, 2)
            nc.scalar.activation(qi, qi, ACT.Exp, scale=1 / 16).then_inc(e_done, 1)
            act_e.wait_ge(d_last, 2)
            nc.scalar.activation(ks, ks, ACT.Exp, scale=1 / 16).then_inc(e_done, 1)
            copy_qk(2)
            for i in range(2 * TT):
                act_e.wait_ge(v_mm[1], i + 1)
                nc.scalar.copy(v1[:, i // 2, (i % 2) * 384:(i % 2) * 384 + 384], ps[:, i % 2, 0:384]).then_inc(v_cp[1], 1)
                if i == 1:
                    exps(1, N1, prob1, True)
            copy_pT(1, N1, pT1)
            copy_o(1, N1, 6)
            for i in range(4):
                act_e.wait_ge(kst_mm, i + 1)
                nc.scalar.copy(ksT[:, i // 2, i % 2].rearrange("p h c -> p (h c)"),
                               ps[:, KSTB[i], 0:HG * DK]).then_inc(kst_cp, 1)

            def copy_gate(i):
                act_e.wait_ge(g_mm, i + 1)
                nc.scalar.copy(g1[:, i // 2, (i % 2) * 384:(i % 2) * 384 + 384], ps[:, i % 2, 0:384]).then_inc(g_cp, 1)

            exps(1, N1 + 1, prob1, True)
            copy_gate(0)
            copy_pT(1, N1 + 1, pT1)
            copy_o(1, N1 + 1, 7)
            copy_gate(1)
            act_e.wait_ge(g_cp, 2)
            nc.scalar.activation(sig1[:, 0, :], g1[:, 0, :], ACT.Sigmoid).then_inc(g_ex, 1)
            copy_gate(2)
            copy_gate(3)
            act_e.wait_ge(g_cp, 4)
            nc.scalar.activation(sig1[:, 1, :], g1[:, 1, :], ACT.Sigmoid).then_inc(g_ex, 1)
            table(ACT.Sqrt)
            for a in range(TT):
                if a == 0:
                    act_e.wait_ge(o_mm, 1)
                else:
                    act_e.wait_ge(ring_used, B1 + 8)
                for h in range(HG):
                    i = HG * a + h
                    nc.scalar.activation(sqj[:, i * DV:(i + 1) * DV], ps[:, OB[a] + h // 2, (h % 2) * DV:(h % 2 + 1) * DV],
                                         ACT.Square, accum_out=st[:, 64 + i:65 + i]).then_inc(o_sq, 1)
                act_e.wait_ge(o_var, a + 1)
                nc.scalar.activation(st[:, 80 + HG * a:84 + HG * a], st[:, 72 + HG * a:76 + HG * a], ACT.Sqrt).then_inc(o_sd, 1)
            for a in range(TT):
                act_e.wait_ge(m_tr, a + 1)
                for b, n in ((0, 4), (1, 2)):
                    nc.scalar.copy(mixT[:, 4 * b:4 * b + n, a * P:(a + 1) * P],
                                   ps[:, (6, 0)[a] + b, 0:n * P].rearrange("p (c t) -> p c t", t=P)).then_inc(m_cp, 1)
            norm(4)
            route(1)
            act_e.dma_start(fnorm, final_norm.rearrange("(o d) -> o d", o=1).to_broadcast([P, D])).then_inc(s_fn, 16)
            experts(1)
            table(ACT.Sqrt)
            act_e.wait_ge(moe_done[1], 1)
            for a in range(TT):
                nc.scalar.activation(xs[:, a, :], xres[:, a, :], ACT.Square,
                                     accum_out=st[:, 10 + a:11 + a]).then_inc(n_sq, 1)
            for a in range(TT):
                act_e.wait_ge(n_var, 6 + a)
                nc.scalar.activation(st[:, 34 + a:35 + a], st[:, 22 + a:23 + a], ACT.Sqrt).then_inc(n_sd, 1)
            for a in range(TT):
                act_e.wait_ge(fin_ready, a + 1)
                act_e.dma_start(out[0, a * P:(a + 1) * P, :], fin[:, a, :]).then_inc(s_out, 16)
            act_e.wait_ge(s_out, 32)

        @block.vector
        def _(dve):
            V = nc.vector
            cnt = [0]

            def link(ins):
                cnt[0] += 1
                ins.then_inc(dchain, 1)
                dve.wait_ge(dchain, cnt[0])

            def norm_scale(i):
                dve.wait_ge(n_sq, TT * (i + 1))
                V.tensor_scalar(st[:, 12 + 2 * i:14 + 2 * i], st[:, 2 * i:2 * i + 2], 1.0 / D, EPS, ALU.mult, ALU.add).then_inc(n_var, 1)
                dve.wait_ge(n_sd, i + 1)
                link(V.reciprocal(st[:, 48 + 2 * i:50 + 2 * i], st[:, 24 + 2 * i:26 + 2 * i]))
                return st[:, 48 + 2 * i:50 + 2 * i]

            def columns(i, a, hdst):
                dve.wait_ge(n_tr, TT * i + a + 1)
                b = NBANK[i][a]
                V.tensor_tensor(hdst[:, :, a * P:(a + 1) * P],
                                ps[:, b:b + 2, :].rearrange("p b (k t) -> p (b k) t", t=P),
                                gcol[:, i, :].unsqueeze(2).to_broadcast([P, KC, P]), ALU.mult).then_inc(n_hT, 1)

            def scale_tokens(i, dst):
                r = norm_scale(i)
                for a in range(TT):
                    V.tensor_scalar(dst[:, a, :], norm_src(i)[:, a, :], r[:, a:a + 1], None, ALU.mult).then_inc(n_xs, 1)

            def softmax_max(l, n, prob, raw):
                dve.wait_ge(at_sc, n + 1)
                if raw:
                    link(V.tensor_reduce(st[:, 36:40].rearrange("p (h a) -> p h a", h=2),
                                         ps[:, 2:4, :].rearrange("p h (a k) -> p h a k", a=TT), AX_X, ALU.max))
                    V.tensor_scalar(st[:, 40:44], st[:, 36:40], -DH ** -0.5, None, ALU.mult).then_inc(at_mx, 1)
                    return
                for h in range(2):
                    for a in range(TT):
                        bias = rpbt[:, 2 * (n - MPAIR) + h, 2 - 2 * a:6 - 2 * a, :].rearrange("p r c -> p (r c)")
                        link(V.scalar_tensor_tensor(prob[:, h, a, :], ps[:, 2 + h, a * T:(a + 1) * T], DH ** -0.5, bias,
                                                    ALU.mult, ALU.add))
                link(V.tensor_reduce(st[:, 36:40].rearrange("p (h a) -> p h a", h=2), prob, AX_X, ALU.max))
                V.tensor_scalar(st[:, 40:44], st[:, 36:40], -1.0, None, ALU.mult).then_inc(at_mx, 1)

            def softmax_div(l, n, prob):
                dve.wait_ge(at_ex, 4 * (n + 1))
                link(V.reciprocal(st[:, 60:64], st[:, 44:48]))
                V.tensor_tensor(prob.rearrange("p h a k -> p (h a) k"), prob.rearrange("p h a k -> p (h a) k"),
                                st[:, 60:64].unsqueeze(2).to_broadcast([P, 4, T]), ALU.mult).then_inc(at_p, 1)

            def add_mixed(l):
                i = 2 * l + 2
                for a in range(TT):
                    if a == 0 and l == 0:
                        dve.wait_ge(ring_used, PRE0 - 2)
                    elif a == 0:
                        dve.wait_ge(wo_mm, 1)
                    else:
                        dve.wait_ge(ring_used, (PRE0, PRE1)[l])
                    V.tensor_tensor(xres[:, a, :], xres[:, a, :],
                                    ps[:, WOB[l][a]:WOB[l][a] + 2, :].rearrange("p b n -> p (b n)"),
                                    ALU.add).then_inc(res[l], 1)
                    if a == 0:
                        dve.wait_ge(s_small, SMALL)
                        columns(i, 0, hT)
                columns(i, 1, hT)

            def one_hot(dst, vals, top, n, tmp):
                im = iotam[:, 0:n].unsqueeze(1).to_broadcast([P, TT, n])
                for a in range(TT):
                    ins = V.scalar_tensor_tensor(tmp[:, a, :], vals[:, a, :], top[:, a:a + 1], iotam[:, 0:n],
                                                 ALU.is_equal, ALU.mult)
                    if a == TT - 1:
                        link(ins)
                link(V.tensor_reduce(sc[:, 15, :], tmp, AX_X, ALU.min))
                link(V.tensor_tensor(dst, im, sc[:, 15, :].unsqueeze(2).to_broadcast([P, TT, n]), ALU.is_equal))

            def route(l):
                i = 2 * l + 2
                rms = norm_scale(i)
                dve.wait_ge(rt_mm[l], 1)
                for a in range(TT):
                    link(V.scalar_tensor_tensor(lg[:, a, :], ps[:, RTB[l], a * 64:a * 64 + NG + NE], rms[:, a:a + 1],
                                                rbias[:, l, :], ALU.mult, ALU.add))
                lgg, lge = lg[:, :, 0:NG], lg[:, :, NG:NG + NE]
                link(V.tensor_reduce(sc[:, 0, :], lgg, AX_X, ALU.max))
                V.tensor_tensor(t4a, lgg, sc[:, 0, :].unsqueeze(2).to_broadcast([P, TT, NG]), ALU.subtract).then_inc(rt_d[l], 1)
                one_hot(goh, lgg, sc[:, 0, :], NG, gpen)
                link(V.tensor_scalar(gpen, goh, BIG, -BIG, ALU.mult, ALU.add))
                link(V.tensor_tensor(me.rearrange("p a (g e) -> p a g e", g=NG), lge.rearrange("p a (g e) -> p a g e", g=NG),
                                     gpen.unsqueeze(3).to_broadcast([P, TT, NG, EG]), ALU.add))
                link(V.tensor_reduce(sc[:, 3, :], me, AX_X, ALU.max))
                one_hot(oh1, me, sc[:, 3, :], NE, t32a)
                link(V.scalar_tensor_tensor(t32b, oh1, -2 * BIG, me, ALU.mult, ALU.add))
                link(V.tensor_reduce(sc[:, 4, :], t32b, AX_X, ALU.max))
                V.tensor_tensor(sc[:, 5, :], sc[:, 4, :], sc[:, 3, :], ALU.subtract).then_inc(rt_d[l], 1)
                one_hot(oh2, t32b, sc[:, 4, :], NE, t32a)
                V.tensor_tensor(msk, oh1, oh2, ALU.add).then_inc(rt_m[l], 1)
                for a in range(TT):
                    V.tensor_scalar(xs[:, a, :], xres[:, a, :], rms[:, a:a + 1], None, ALU.mult)
                link(V.memset(ppos, 1000.0))
                link(V.tensor_scalar(t32a, msk, -1000.0, 1000.0, ALU.mult, ALU.add))
                dve.wait_ge(rt_p[l], 1)
                link(V.tensor_tensor(ppos[:, :, 0:NE], t32a,
                                     ps[:, RTB[l] + 1, 0:2 * NE].rearrange("p (a e) -> p a e", a=TT), ALU.add))

            def gates(l):
                dve.wait_ge(rt_e[l], 2)
                link(V.tensor_reduce(sc[:, 1, :], t4a, AX_X, ALU.add))
                link(V.tensor_scalar(sc[:, 7, :], sc[:, 6, :], 1.0, None, ALU.add))
                link(V.tensor_tensor(sc[:, 8, :], sc[:, 7, :], sc[:, 1, :], ALU.mult))
                link(V.reciprocal(sc[:, 9, :], sc[:, 8, :]))
                link(V.tensor_tensor(sc[:, 10, :], sc[:, 9, :], sc[:, 6, :], ALU.mult))
                link(V.memset(wtok, 0.0))
                link(V.tensor_tensor(t32a, oh1, sc[:, 9, :].unsqueeze(2).to_broadcast([P, TT, NE]), ALU.mult))
                link(V.tensor_tensor(t32b, oh2, sc[:, 10, :].unsqueeze(2).to_broadcast([P, TT, NE]), ALU.mult))
                link(V.tensor_tensor(wtok[:, :, 0:NE], t32a, t32b, ALU.add))

            def further_rounds(l):
                link(V.tensor_tensor(cmp8, ntmp[:, 0:1].to_broadcast([P, 8]), cst[:, C_THR:C_THR + 8], ALU.is_gt))
                link(V.tensor_reduce(ntmp[:, 1:2], cmp8, AX_X, ALU.add))
                if l == 0:
                    link(V.tensor_copy(roundf[:], ntmp[:, 1:2]))
                    V.tensor_copy(nround[:, 0:1], ntmp[:, 1:2]).then_inc(rt_n[l], 1)
                else:
                    V.tensor_tensor(nround[:, 1:2], roundf[:], ntmp[:, 1:2], ALU.add).then_inc(rt_n[l], 1)

            def select(rn, g):
                V.tensor_tensor(sel, iota.unsqueeze(1).unsqueeze(1).to_broadcast([P, TT, E4, CAP]),
                                ppos[:, :, bass.ds(g * E4, E4)].unsqueeze(3).to_broadcast([P, TT, E4, CAP]),
                                ALU.is_equal).then_inc(rn.sig.sel_ready, 1)

            def select_w(rn, g, count):
                dve.wait_ge(rn.sig.sel_ready, count)
                V.tensor_tensor(selw, sel, wtok[:, :, bass.ds(g * E4, E4)].unsqueeze(3).to_broadcast([P, TT, E4, CAP]),
                                ALU.mult).then_inc(rn.sig.sel_ready, 1)

            def quad(rn, l, c, pair, n0, g, sel_count):
                dve.wait_ge(rn.sig.gathered, c + 1)
                for b in range(2):
                    V.tensor_tensor(xsel[:, 4 * b:4 * b + 4, :], ps[:, b, :].rearrange("p (k t) -> p k t", t=P),
                                    gcol[:, 2 + 2 * l, 4 * b:4 * b + 4].unsqueeze(2).to_broadcast([P, 4, P]),
                                    ALU.mult).then_inc(rn.sig.xsel_ready, 1)
                dve.wait_ge(rn.sig.sel_ready, sel_count)
                select(rn, g + 1)
                dve.wait_ge(rn.sig.selT_mm, c + 1)
                select_w(rn, g + 1, sel_count + 1)
                dve.wait_ge(rn.sig.sig_done, c + 1)
                V.tensor_tensor(sg, sg, ps[:, 4, :], ALU.mult).then_inc(rn.sig.silu, 1)
                dve.wait_ge(rn.sig.silu, c + 1)
                dve.wait_ge(rn.ring_used, rn.used(pair, n0 + 8))
                V.tensor_tensor(act, sg, ps[:, 5, :], ALU.mult).then_inc(rn.sig.act_ready, 1)
                for a in range(TT):
                    dve.wait_ge(rn.sig.scattered, c * 2 + a + 1)
                    V.tensor_tensor(xres[:, a, :], xres[:, a, :], ps[:, 4 + 2 * a:6 + 2 * a, :].rearrange("p b n -> p (b n)"),
                                    ALU.add).then_inc(rn.sig.added, 1)
                dve.wait_ge(rn.sig.added, c * 2 + 2)

            def experts(l):
                select(main[l], 0)
                dve.wait_ge(rt_p[l], 2)
                link(V.tensor_reduce(ntmp[:, 0:1], ps[:, RTB[l] + 2, 0:NE], AX_X, ALU.max))
                gates(l)
                select_w(main[l], 0, l * SELS + 1)
                further_rounds(l)
                with dve.Fori(0, PAIRS - 1 if l == 0 else PAIRS) as pair:
                    for s in range(2):
                        quad(main[l], l, pair * 2 + (l * NQ + s), pair, s * FILLS, pair * 2 + s,
                             pair * 4 + (l * SELS + 2 + 2 * s))
                if l == 0:
                    quad(main[0], 0, NQ - 2, PAIRS - 1, 0, NQ - 2, 2 * NQ - 2)
                    quad(main[0], 0, NQ - 1, PAIRS - 1, FILLS + 1, NQ - 1, 2 * NQ)
                dve.wait_ge(rt_n[l], 1)
                lo, hi = rounds(dve, l)
                with dve.If(hi > lo):
                    with dve.Fori(lo, hi) as r:
                        V.tensor_scalar(ppos, ppos, -float(CAP), None, ALU.add).then_inc(next_round, 1)
                        dve.wait_ge(next_round, r + 1)
                        select(extra, 0)
                        select_w(extra, 0, r * SELS + 1)
                        with dve.Fori(0, PAIRS) as pair:
                            for s in range(2):
                                quad(extra, l, r * NQ + pair * 2 + s, r * PAIRS + pair, s * FILLS, pair * 2 + s,
                                     r * SELS + pair * 4 + (2 + 2 * s))
                V.tensor_copy(ntmp[:, 0:1], xres[:, 0, 0:1]).then_inc(moe_done[l], 1)

            V.memset(scrap[:], 1.0).then_inc(s_scrap, 1)
            dve.wait_ge(s_mem, 16)
            dve.wait_ge(s_cst, 16)
            scale_tokens(0, mixT_as_tokens)
            dve.wait_ge(s_x, 16)
            scale_tokens(1, xs)
            dve.wait_ge(s_gain, 16 * 2)
            for i, hdst in ((0, memT), (1, hT)):
                for a in range(TT):
                    columns(i, a, hdst)
            for n in range(MPAIR):
                softmax_max(0, n, prob0, True)
                softmax_div(0, n, prob0)
            dve.wait_ge(s_mask, 1)
            for n in range(MPAIR, N1):
                softmax_max(0, n, prob0, False)
                softmax_div(0, n, prob0)
            add_mixed(0)
            route(0)
            experts(0)

            dve.wait_ge(moe_done[0], 1)
            scale_tokens(3, xs)
            for a in range(TT):
                columns(3, a, hT)
            dve.wait_ge(z_mm, 1)
            for d in range(2):
                V.tensor_tensor(qs[:, d].rearrange("p (h t) -> p h t", t=T),
                                ps[0:DK, 2 * d:2 * d + 2, :].rearrange("p b (h t) -> p (b h) t", t=T),
                                gbias[:, d, :].unsqueeze(2).to_broadcast([DK, HG, T]), ALU.add).then_inc(z_sb, 1)
            dve.wait_ge(z_sb, 2)
            V.scalar_tensor_tensor(ki, qs, -1.0, qs, ALU.mult, ALU.min).then_inc(l_na, 1)
            dve.wait_ge(l_ln, 1)
            link(V.scalar_tensor_tensor(qi, qs, 0.0, ki, ALU.min, ALU.subtract))
            dve.wait_ge(resets, 3)
            V.tensor_tensor_scan(bcum[:, 0], ks[:, 0], qi[:, 0], 0.0, ALU.mult, ALU.add).then_inc(d_b, 1)
            V.tensor_tensor_scan(bcum[:, 1][:, ::-1], ks[:, 1][:, ::-1], qi[:, 1][:, ::-1], 0.0, ALU.mult, ALU.add).then_inc(d_b, 1)
            dve.wait_ge(d_b, 2)

            def chunked(t, d):
                return t[:, d].rearrange("p (n c) -> p n c", c=CH)

            MID, LAST = (CH // 2 - 1, CH // 2), (CH - 1, 0)
            for d in range(2):
                b = chunked(bcum, d)
                V.tensor_tensor(chunked(qi, d), b, b[:, :, MID[d]:MID[d] + 1].to_broadcast([DK, HG * NCH, CH]),
                                ALU.subtract).then_inc(d_mid, 1)
            for d in range(2):
                b = chunked(bcum, d)
                V.tensor_tensor(chunked(ks, d), b[:, :, LAST[d]:LAST[d] + 1].to_broadcast([DK, HG * NCH, CH]), b,
                                ALU.subtract).then_inc(d_last, 1)
            dve.wait_ge(gq_cp, 4 * 3)
            for i, (e, by, s) in enumerate(((qs, qT, None), (ki, kT, k_in), (qi, qT, q_in), (ks, kT, k_st))):
                dve.wait_ge(e_done, i + 1)
                if i == 0:
                    for d in range(2):
                        link(V.tensor_copy(st_dec[:, d, :].unsqueeze(2), chunked(qs, d)[:, :, LAST[d]:LAST[d] + 1]))
                    s = q_st
                for d in range(2):
                    V.tensor_tensor(e[:, d], e[:, d], by.rearrange("p h t -> p (h t)"), ALU.mult).then_inc(s, 1)
            for m in range(MPAIR):
                softmax_max(1, N1 + m, prob1, True)
                softmax_div(1, N1 + m, prob1)
            dve.wait_ge(at_o, N1 + 2)
            for d in range(2):
                dve.wait_ge(a_mm, d + 1)
                link(V.tensor_tensor(amask[:, d].rearrange("p h a c -> p (h a) c"),
                                     ps[:, 2 + d, :].rearrange("p (h c) -> p h c", c=CH),
                                     cst[:, (C_MF, C_MB)[d]:(C_MF, C_MB)[d] + CH].unsqueeze(1).to_broadcast([P, HG * TT, CH]),
                                     ALU.mult))
            V.tensor_tensor(asum, amask[:, 0], amask[:, 1], ALU.add).then_inc(a_cp, 1)

            def new_state(i):
                step, d = i // 2, i % 2
                n = step if d == 0 else NCH - 1 - step
                dve.wait_ge(u_mm, i + 1)
                u = ps[0:DK, 4 + 2 * d:6 + 2 * d, 0:2 * DV].rearrange("p b (h v) -> p b h v", h=2)
                if step == 0:
                    V.tensor_copy(state[:, d, step].rearrange("p (b h) v -> p b h v", h=2), u).then_inc(u_st, 1)
                    return
                dve.wait_ge(u_st, i - 1)
                for h in range(HG):
                    ins = V.scalar_tensor_tensor(state[:, d, step, h, :], state[:, d, step - 1, h, :],
                                                 st_dec[:, d, h * NCH + n:h * NCH + n + 1], u[:, h // 2, h % 2, :],
                                                 ALU.mult, ALU.add)
                ins.then_inc(u_st, 1)

            def gate(a):
                dve.wait_ge(g_ex, a + 1)
                link(V.tensor_tensor(g1[:, a, :], g1[:, a, :], sig1[:, a, :], ALU.mult))
                link(V.tensor_tensor(g1[:, a, :].rearrange("p (h v) -> p h v", v=DV),
                                     g1[:, a, :].rearrange("p (h v) -> p h v", v=DV),
                                     gnorm[:].unsqueeze(1).to_broadcast([P, HG, DV]), ALU.mult))

            for i in range(4):
                new_state(i)
            gate(0)
            new_state(4)
            new_state(5)
            gate(1)
            for a in range(TT):
                dve.wait_ge(o_sq, HG * (a + 1))
                V.tensor_scalar(st[:, 72 + HG * a:76 + HG * a], st[:, 64 + HG * a:68 + HG * a], 1.0 / DV, EPS,
                                ALU.mult, ALU.add).then_inc(o_var, 1)
                dve.wait_ge(o_sd, a + 1)
                link(V.reciprocal(st[:, 88 + HG * a:92 + HG * a], st[:, 80 + HG * a:84 + HG * a]))
                o = ps[:, OB[a]:OB[a] + 2, 0:2 * DV].rearrange("p b (h v) -> p b h v", h=2)
                r = st[:, 88 + HG * a:88 + HG * a + HG].rearrange("p (b h) -> p b h", h=2)
                link(V.tensor_tensor(sig1[:, a].rearrange("p (b h v) -> p b h v", b=2, h=2), o,
                                     r.unsqueeze(3).to_broadcast([P, 2, 2, DV]), ALU.mult))
                V.tensor_tensor(g1[:, a, :], g1[:, a, :], sig1[:, a, :], ALU.mult).then_inc(o_mix, 1)
            add_mixed(1)
            route(1)
            experts(1)
            dve.wait_ge(moe_done[1], 1)
            dve.wait_ge(s_fn, 16)
            for a in range(TT):
                dve.wait_ge(n_sq, TT * 5 + a + 1)
                V.tensor_scalar(st[:, 22 + a:23 + a], st[:, 10 + a:11 + a], 1.0 / D, EPS, ALU.mult, ALU.add).then_inc(n_var, 1)
            for a in range(TT):
                dve.wait_ge(n_sd, 6 + a)
                link(V.reciprocal(st[:, 58 + a:59 + a], st[:, 34 + a:35 + a]))
                V.scalar_tensor_tensor(fin[:, a, :], xres[:, a, :], st[:, 58 + a:59 + a], fnorm, ALU.mult, ALU.mult).then_inc(fin_ready, 1)


def kernel(**inputs):
    import numpy as np
    import concourse.bacc as bacc
    from concourse.bass_utils import run_bass_kernel_spmd as run

    nc = bacc.Bacc("TRN2", target_bir_lowering=False, num_devices=1)
    arrays, args = {}, []
    data = dict(inputs)
    data["consts"] = make_consts()
    for name in NAMES:
        a = np.ascontiguousarray(data[name])
        arrays[f"in_{name}"] = a
        args.append(nc.dram_tensor(f"in_{name}", a.shape, mybir.dt.from_np(a.dtype), kind="ExternalInput").ap())
    o = nc.dram_tensor("out_0", (1, T, D), F32, kind="ExternalOutput").ap()
    build(nc, *args, o)
    r = run(nc, [arrays], core_ids=[0])
    return r.results[0]["out_0"]


NAMES = ["x", "mem", "mem_norm", "final_norm", "norm_mix", "norm_ffn", "w_mem_kv", "w_out", "na_w_in", "na_rpb",
         "gla_w_in", "gla_gate_up", "gla_gate_bias", "gla_out_norm", "moe_w_group", "moe_b_group", "moe_w_router",
         "moe_b_router", "moe_w1", "moe_w3", "moe_w2", "consts"]
```
